# Optimizing a Trainium2 kernel written in Bass

```python
import jax, jax.numpy as jnp
from jax import lax
import numpy as np

D_MODEL = 1024
BATCH = 1
SEQ = 256
DEPTH = 2

N_MIXERS = 2
N_CONV = (DEPTH + 1) // 2
N_NSA = DEPTH // 2

CONV_WIDTH = 31

HEAD_DIM = 64
N_HEADS = D_MODEL // HEAD_DIM
N_KV = 4
GROUP = N_HEADS // N_KV
CMP_BLOCK = 32
CMP_STRIDE = 16
CMP_HIDDEN = 256
SLC_BLOCK = 64
N_SEL = 16
WINDOW = 512
Q_BLOCK = 32
ROPE_THETA = 10000.0
NSA_IN = N_HEADS * HEAD_DIM + 6 * N_KV * HEAD_DIM + 3 * N_HEADS

N_GROUPS = 4
EXPERTS_PER_GROUP = 8
N_EXPERTS = N_GROUPS * EXPERTS_PER_GROUP
EXPERT_TOPK = 2
D_EXPERT = 512
EXPERT_BLOCK = 256

PLE_DIM = 256

EPS = 1e-6
NEG = -1e30

kernel_name = "hybrid_conv_nsa_hmoe_ple"

def rms_norm(x, g):
    xf = x.astype(jnp.float32)
    y = xf * lax.rsqrt(jnp.mean(xf * xf, axis=-1, keepdims=True) + EPS)
    return (y * g.astype(jnp.float32)).astype(x.dtype)

def layer_norm(x, g, b):
    xf = x.astype(jnp.float32)
    mu = jnp.mean(xf, axis=-1, keepdims=True)
    var = jnp.mean(jnp.square(xf - mu), axis=-1, keepdims=True)
    y = (xf - mu) * lax.rsqrt(var + EPS)
    return (y * g.astype(jnp.float32) + b.astype(jnp.float32)).astype(x.dtype)

def rope(x, pos):
    half = x.shape[-1] // 2
    inv = 1.0 / (ROPE_THETA ** (jnp.arange(half, dtype=jnp.float32) / half))
    ang = pos.astype(jnp.float32)[..., None] * inv
    cos = jnp.cos(ang)[:, :, None, :]
    sin = jnp.sin(ang)[:, :, None, :]
    xf = x.astype(jnp.float32)
    x1, x2 = xf[..., :half], xf[..., half:]
    return jnp.concatenate([x1 * cos - x2 * sin, x2 * cos + x1 * sin], axis=-1).astype(x.dtype)

def masked_softmax(s, mask):
    p = jax.nn.softmax(jnp.where(mask, s, NEG), axis=-1)
    return p * mask

def conv_module(xn, w_pw1, b_pw1, w_dw, b_dw, ln_g, ln_b, w_pw2, b_pw2):
    u = xn @ w_pw1 + b_pw1
    a, g = jnp.split(u, 2, axis=-1)
    u = a * jax.nn.sigmoid(g)
    u = lax.conv_general_dilated(
        u, w_dw[:, None, :].astype(u.dtype), window_strides=(1,),
        padding=[(CONV_WIDTH - 1, 0)], dimension_numbers=("NWC", "WIO", "NWC"),
        feature_group_count=u.shape[-1]) + b_dw
    u = jax.nn.silu(layer_norm(u, ln_g, ln_b))
    return u @ w_pw2 + b_pw2

def compress(x, pe, w1, w2):
    B, T, G, dh = x.shape
    xr = x.reshape(B, T // CMP_STRIDE, CMP_STRIDE, G, dh)
    blocks = jnp.concatenate([xr[:, :-1], xr[:, 1:]], axis=2)
    blocks = blocks + pe[None, None, :, None, :]
    blocks = jnp.transpose(blocks, (0, 1, 3, 2, 4)).reshape(B, -1, G, CMP_BLOCK * dh)
    return jax.nn.gelu(blocks @ w1) @ w2

def nsa_attention(xn, positions, w_in, q_norm, k_norm, cmp_pe, cmp_w1, cmp_w2, w_out):
    B, T, _ = xn.shape
    H, G, R, dh = N_HEADS, N_KV, GROUP, HEAD_DIM
    HD, KD = H * dh, G * dh
    NC = T // CMP_STRIDE - 1
    NS = T // SLC_BLOCK
    NQ = T // Q_BLOCK
    n_sel = min(N_SEL, NS)
    a = SLC_BLOCK // CMP_STRIDE
    b = CMP_BLOCK // CMP_STRIDE
    scale = HEAD_DIM ** -0.5

    proj = xn @ w_in
    q = proj[..., :HD].reshape(B, T, H, dh)
    kv = proj[..., HD:HD + 6 * KD].reshape(B, T, 6, G, dh)
    gate = jax.nn.sigmoid(proj[..., HD + 6 * KD:].astype(jnp.float32)).reshape(B, T, G, R, 3)

    q = rope(rms_norm(q, q_norm), positions)
    k_s = rope(rms_norm(kv[:, :, 2], k_norm[1]), positions)
    k_w = rope(rms_norm(kv[:, :, 4], k_norm[2]), positions)
    kc = compress(kv[:, :, 0], cmp_pe[0], cmp_w1[0], cmp_w2[0])
    kc = rope(rms_norm(kc, k_norm[0]), positions[:, CMP_BLOCK - 1::CMP_STRIDE])
    vc = compress(kv[:, :, 1], cmp_pe[1], cmp_w1[1], cmp_w2[1])

    to_g = lambda t: jnp.moveaxis(t, 2, 1)
    kc, vc = to_g(kc), to_g(vc)
    ks_blk = to_g(k_s).reshape(B, G, NS, SLC_BLOCK, dh)
    vs_blk = to_g(kv[:, :, 3]).reshape(B, G, NS, SLC_BLOCK, dh)
    pad_w = ((0, 0), (0, 0), (WINDOW, 0), (0, 0))
    kw_pad = jnp.pad(to_g(k_w), pad_w)
    vw_pad = jnp.pad(to_g(kv[:, :, 5]), pad_w)

    q_chunks = jnp.moveaxis(jnp.transpose(q.reshape(B, T, G, R, dh), (0, 2, 3, 1, 4))
                            .reshape(B, G, R, NQ, Q_BLOCK, dh), 3, 0)
    g_chunks = jnp.moveaxis(jnp.transpose(gate, (0, 2, 3, 1, 4))
                            .reshape(B, G, R, NQ, Q_BLOCK, 3), 3, 0)

    cmp_end = CMP_STRIDE * jnp.arange(NC) + CMP_BLOCK - 1
    blk = jnp.arange(NS)
    bi = jnp.arange(B)[:, None, None, None]
    gi = jnp.arange(G)[None, :, None, None]

    def block_fn(args):
        qc, gc, c = args
        t0 = c * Q_BLOCK
        tq = t0 + jnp.arange(Q_BLOCK)
        s = jnp.einsum('bgrqd,bgkd->bgrqk', qc, kc, preferred_element_type=jnp.float32) * scale
        p_c = masked_softmax(s, cmp_end[None, :] <= tq[:, None])
        o_c = jnp.einsum('bgrqk,bgkd->bgrqd', p_c.astype(vc.dtype), vc)
        imp = p_c.sum(axis=2)
        imp = jnp.pad(imp, ((0, 0), (0, 0), (0, 0), (0, a * NS + a + b - NC)))
        p_slc = sum(imp[..., m + n: m + n + a * NS: a] for m in range(a) for n in range(b))
        cur = tq // SLC_BLOCK
        forced = (blk[None, :] == 0) | (blk[None, :] == cur[:, None]) | (blk[None, :] == cur[:, None] - 1)
        valid = blk[None, :] * SLC_BLOCK <= tq[:, None]
        score = jnp.where(forced, jnp.inf, jnp.where(valid, p_slc, -jnp.inf))
        _, idx = lax.top_k(score, n_sel)
        k_sel = ks_blk[bi, gi, idx].reshape(B, G, Q_BLOCK, n_sel * SLC_BLOCK, dh)
        v_sel = vs_blk[bi, gi, idx].reshape(B, G, Q_BLOCK, n_sel * SLC_BLOCK, dh)
        kpos = (idx[..., None] * SLC_BLOCK + jnp.arange(SLC_BLOCK)).reshape(B, G, Q_BLOCK, -1)
        mask_s = (kpos <= tq[None, None, :, None])[:, :, None]
        s = jnp.einsum('bgrqd,bgqkd->bgrqk', qc, k_sel, preferred_element_type=jnp.float32) * scale
        p_s = masked_softmax(s, mask_s)
        o_s = jnp.einsum('bgrqk,bgqkd->bgrqd', p_s.astype(v_sel.dtype), v_sel)
        kw = lax.dynamic_slice_in_dim(kw_pad, t0, WINDOW + Q_BLOCK, axis=2)
        vw = lax.dynamic_slice_in_dim(vw_pad, t0, WINDOW + Q_BLOCK, axis=2)
        kpos_w = t0 - WINDOW + jnp.arange(WINDOW + Q_BLOCK)
        mask_w = ((kpos_w[None, :] <= tq[:, None]) & (kpos_w[None, :] > tq[:, None] - WINDOW)
                  & (kpos_w[None, :] >= 0))
        s = jnp.einsum('bgrqd,bgkd->bgrqk', qc, kw, preferred_element_type=jnp.float32) * scale
        p_w = masked_softmax(s, mask_w)
        o_w = jnp.einsum('bgrqk,bgkd->bgrqd', p_w.astype(vw.dtype), vw)
        o = gc[..., 0:1] * o_c + gc[..., 1:2] * o_s + gc[..., 2:3] * o_w
        return o.astype(qc.dtype)

    out = lax.map(block_fn, (q_chunks, g_chunks, jnp.arange(NQ)))
    out = jnp.transpose(out, (1, 0, 4, 2, 3, 5)).reshape(B, T, HD)
    return out @ w_out

def hier_moe(xn, w_rg, b_rg, w_re, b_re, w_gate, w_up, w_down):
    B, T, D = xn.shape
    N = B * T
    xf = xn.reshape(N, D)
    lg = (xf @ w_rg + b_rg).astype(jnp.float32)
    pg = jax.nn.softmax(lg, axis=-1)
    pg_sel, grp = lax.top_k(pg, 1)
    le = (xf @ w_re + b_re).astype(jnp.float32).reshape(N, N_GROUPS, EXPERTS_PER_GROUP)
    le_g = jnp.take_along_axis(le, grp[:, :, None], axis=1)[:, 0]
    top_v, top_i = lax.top_k(le_g, EXPERT_TOPK)
    wts = jax.nn.softmax(top_v, axis=-1) * pg_sel
    eid = grp * EXPERTS_PER_GROUP + top_i
    A = N * EXPERT_TOPK
    e_flat = eid.reshape(A)
    tok = jnp.repeat(jnp.arange(N), EXPERT_TOPK)
    w_flat = wts.reshape(A)
    order = jnp.argsort(e_flat)
    e_s = e_flat[order]
    counts = jnp.zeros((N_EXPERTS,), jnp.int32).at[e_flat].add(1)
    pc = (counts + EXPERT_BLOCK - 1) // EXPERT_BLOCK * EXPERT_BLOCK
    ends = jnp.cumsum(pc)
    starts = jnp.cumsum(counts) - counts
    dest = (ends - pc)[e_s] + jnp.arange(A) - starts[e_s]
    n_blocks = -(-A // EXPERT_BLOCK) + N_EXPERTS
    P = n_blocks * EXPERT_BLOCK
    slot_tok = jnp.zeros((P,), jnp.int32).at[dest].set(tok[order])
    slot_w = jnp.zeros((P,), jnp.float32).at[dest].set(w_flat[order])
    blk_e = jnp.minimum(jnp.searchsorted(ends, jnp.arange(n_blocks) * EXPERT_BLOCK, side='right'),
                        N_EXPERTS - 1)
    xb = xf[slot_tok].reshape(n_blocks, EXPERT_BLOCK, D)

    def expert_block(args):
        xblk, e = args
        h = jax.nn.silu(xblk @ w_gate[e]) * (xblk @ w_up[e])
        return h @ w_down[e]

    yb = lax.map(expert_block, (xb, blk_e)).reshape(P, D)
    out = jnp.zeros((N, D), yb.dtype).at[slot_tok].add(yb * slot_w[:, None].astype(yb.dtype))
    return out.reshape(B, T, D)

def setup_inputs(seed: int = 0) -> dict:
    key = jax.random.key(seed)
    ks = iter(jax.random.split(key, 40))
    D, F = D_MODEL, D_EXPERT

    def nrm(shape, fan_in):
        return jax.random.normal(next(ks), shape, jnp.float32) * (fan_in ** -0.5)

    def gain(shape):
        return 1.0 + 0.02 * jax.random.normal(next(ks), shape, jnp.float32)

    def small(shape, s=0.02):
        return s * jax.random.normal(next(ks), shape, jnp.float32)

    x = jax.random.normal(next(ks), (BATCH, SEQ, D), jnp.float32)
    p = jax.random.normal(next(ks), (DEPTH, BATCH, SEQ, PLE_DIM), jnp.float32)
    offset = jax.random.randint(next(ks), (BATCH, 1), 0, 1024, dtype=jnp.int32)
    positions = (offset + jnp.arange(SEQ, dtype=jnp.int32)[None, :]).astype(jnp.int32)
    return {
        "x": x, "p": p, "positions": positions,
        "g_mix": gain((DEPTH, D)), "g_ffn": gain((DEPTH, D)), "g_ple": gain((DEPTH, D)),
        "conv_w_pw1": nrm((N_CONV, D, 2 * D), D), "conv_b_pw1": small((N_CONV, 2 * D)),
        "conv_w_dw": nrm((N_CONV, CONV_WIDTH, D), CONV_WIDTH), "conv_b_dw": small((N_CONV, D)),
        "conv_ln_g": gain((N_CONV, D)), "conv_ln_b": small((N_CONV, D)),
        "conv_w_pw2": nrm((N_CONV, D, D), D), "conv_b_pw2": small((N_CONV, D)),
        "nsa_w_in": nrm((N_NSA, D, NSA_IN), D),
        "nsa_q_norm": gain((N_NSA, HEAD_DIM)), "nsa_k_norm": gain((N_NSA, 3, HEAD_DIM)),
        "nsa_cmp_pe": small((N_NSA, 2, CMP_BLOCK, HEAD_DIM), 0.1),
        "nsa_cmp_w1": nrm((N_NSA, 2, CMP_BLOCK * HEAD_DIM, CMP_HIDDEN), CMP_BLOCK * HEAD_DIM),
        "nsa_cmp_w2": nrm((N_NSA, 2, CMP_HIDDEN, HEAD_DIM), CMP_HIDDEN),
        "nsa_w_out": nrm((N_NSA, N_HEADS * HEAD_DIM, D), N_HEADS * HEAD_DIM),
        "moe_w_rg": nrm((DEPTH, D, N_GROUPS), D), "moe_b_rg": small((DEPTH, N_GROUPS), 0.01),
        "moe_w_re": nrm((DEPTH, D, N_EXPERTS), D), "moe_b_re": small((DEPTH, N_EXPERTS), 0.01),
        "moe_w_gate": nrm((DEPTH, N_EXPERTS, D, F), D), "moe_w_up": nrm((DEPTH, N_EXPERTS, D, F), D),
        "moe_w_down": nrm((DEPTH, N_EXPERTS, F, D), F),
        "ple_w_proj": nrm((DEPTH, PLE_DIM, D), PLE_DIM), "ple_w_gate": nrm((DEPTH, D, D), D),
    }

def reference(x, p, positions, g_mix, g_ffn, g_ple, conv_w_pw1, conv_b_pw1, conv_w_dw, conv_b_dw,
              conv_ln_g, conv_ln_b, conv_w_pw2, conv_b_pw2, nsa_w_in, nsa_q_norm, nsa_k_norm,
              nsa_cmp_pe, nsa_cmp_w1, nsa_cmp_w2, nsa_w_out, moe_w_rg, moe_b_rg, moe_w_re, moe_b_re,
              moe_w_gate, moe_w_up, moe_w_down, ple_w_proj, ple_w_gate):
    h = x
    for i in range(DEPTH):
        xn = rms_norm(h, g_mix[i])
        j = i // N_MIXERS
        if i % N_MIXERS == 0:
            h = h + conv_module(xn, conv_w_pw1[j], conv_b_pw1[j], conv_w_dw[j], conv_b_dw[j],
                                conv_ln_g[j], conv_ln_b[j], conv_w_pw2[j], conv_b_pw2[j])
        else:
            h = h + nsa_attention(xn, positions, nsa_w_in[j], nsa_q_norm[j], nsa_k_norm[j],
                                  nsa_cmp_pe[j], nsa_cmp_w1[j], nsa_cmp_w2[j], nsa_w_out[j])
        h = h + hier_moe(rms_norm(h, g_ffn[i]), moe_w_rg[i], moe_b_rg[i], moe_w_re[i], moe_b_re[i],
                         moe_w_gate[i], moe_w_up[i], moe_w_down[i])
        gate = jax.nn.sigmoid(rms_norm(h, g_ple[i]) @ ple_w_gate[i])
        h = h + gate * (p[i] @ ple_w_proj[i])
    return h


_drawn_inputs = setup_inputs


def setup_inputs(seed=0):
    import zlib

    import numpy as np

    out = dict(_drawn_inputs(seed))
    spreads = {}
    factors = {'g_ple': 8.0, 'nsa_q_norm': 8.0, 'nsa_k_norm': 8.0, 'moe_b_rg': 2.769, 'moe_b_re': 4.107}
    for name, (base, spread) in spreads.items():
        noise = np.random.default_rng([zlib.crc32(name.encode()), seed]).standard_normal(out[name].shape)
        drawn = base * np.exp(spread * noise) if base else spread * noise
        out[name] = __import__('jax').numpy.asarray(drawn.astype(out[name].dtype))
    for name, factor in factors.items():
        out[name] = (out[name] * factor).astype(out[name].dtype)
    return out
```

```python
from contextlib import ExitStack

import numpy as np

import concourse.bass as bass
from concourse import mybir

ALU = mybir.AluOpType
ACT = mybir.ActivationFunctionType
F32 = mybir.dt.float32
I32 = mybir.dt.int32
AX = mybir.AxisListType

P = 128
DEPTH = 2
D = 1024
T = 256
NT = T // P
KD = D // P
TAPS = 31
HEADS, DH, NKV = 16, 64, 4
CMP_STRIDE, CMP_BLOCK, CMP_HID = 16, 32, 256
NC_ = T // CMP_STRIDE - 1
NG, NE, NEG_E = 4, 32, 8
F = 512
SLOTS = 32
Q4 = D // 4
EPS = 1e-6
NEG = -1e30
BIGI = 1000.0
MAGIC = 12582912.0
TWO_PI = (6.28125, 1.9350051879882812e-3, 3.0199159819567e-7)
PI_LO = 3.1415925
N_VEC, N_MISC, N_ATT = 14, 8 + 6, 9
SCALE = DH ** -0.5
ROPE_THETA = 10000.0

ACC = 0
BGU, BGX, BHT, BY = 4, 5, 6, 7

H_DVE = [0, 4, 6, 10, 14, 16, 20]
H_ACT = [0, 0, 2, 2, 2, 4, 4]
ROW_MIX, ROW_FFN, ROW_PLE, ROW_BPW1, ROW_BDW, ROW_LNG, ROW_LNB, NROWS = 0, 16, 32, 48, 64, 72, 80, 88


def build(nc, x, p, positions, g_mix, g_ffn, g_ple, conv_w_pw1, conv_b_pw1, conv_w_dw, conv_b_dw,
          conv_ln_g, conv_ln_b, conv_w_pw2, conv_b_pw2, nsa_w_in, nsa_q_norm, nsa_k_norm,
          nsa_cmp_pe, nsa_cmp_w1, nsa_cmp_w2, nsa_w_out, moe_w_rg, moe_b_rg, moe_w_re, moe_b_re,
          moe_w_gate, moe_w_up, moe_w_down, ple_w_proj, ple_w_gate, inv_freq, out):
    with ExitStack() as ctx:
        def sb(name, shape, dt=F32):
            return ctx.enter_context(nc.sbuf_tensor(name, shape, dt))

        def sem(name):
            return ctx.enter_context(nc.semaphore(name))

        PS = ctx.enter_context(nc.psum_tensor("PS", [P, 8, 512], F32))

        ring = sb("ring", [P, 2, 12288])
        wb = sb("wb", [P, 3, 4096])
        h = sb("h", [P, NT, D])
        hn = sb("hn", [P, NT, D])
        xnT = sb("xnT", [P, KD, T])
        ppw = sb("ppw", [P, 4096])
        ident = sb("ident", [P, P])
        ones = sb("ones", [P, P])
        upper = sb("upper", [P, P])
        cmask = sb("cmask", [P, 2, P])
        vecT = sb("vecT", [P, NROWS])
        g8 = sb("g8", [P, 2, 8])
        wr = sb("wr", [P, DEPTH, KD, NG + NE])
        rowb = sb("rowb", [1, DEPTH * (NG + NE)])
        rstd = sb("rstd", [P, 2, NT])
        iot = sb("iot", [P, 32])
        ioti = sb("ioti", [P, 32], I32)
        nhalf = sb("nhalf", [P, 1])
        colp = sb("colp", [P, 1])
        xtot = sb("xtot", [P, 1])
        tab = sb("tab", [P, 2, NE], I32)
        A = sb("arena", [P, 4480])

        off = [0]

        def carve(n):
            a = off[0]
            off[0] += n
            assert off[0] <= 4480, off[0]
            return A[:, a:a + n]

        srow = carve(512).rearrange("p (a t) -> p a t", a=2)
        wrow = carve(512).rearrange("p (a t) -> p a t", a=2)
        eqr = carve(512).rearrange("p (a t) -> p a t", a=2)
        wT = [carve(256) for _ in range(2)]
        eq4 = carve(128).rearrange("p (t a s) -> p t a s", t=2, a=2)
        sel = [carve(64).rearrange("p (t s) -> p t s", t=2) for _ in range(2)]
        cur32 = carve(32)
        curc = carve(1)
        xcur32 = carve(32)
        xcurc = carve(1)
        xg = carve(256)
        xgT = carve(256).rearrange("p (k s) -> p k s", k=8)
        xfree = [off[0], 0]
        xsel = carve(64).rearrange("p (t s) -> p t s", t=2)
        xwT = carve(256)
        xxgT = carve(256).rearrange("p (k s) -> p k s", k=8)
        xfree[1] = off[0]
        gs = carve(256)
        hh = carve(256)
        hT = carve(128).rearrange("p (c s) -> p c s", c=2)
        ysb = carve(256)
        S4 = carve(4).rearrange("p (t a) -> p t a", t=2)
        W4 = carve(4).rearrange("p (t a) -> p t a", t=2)
        scn = carve(64).rearrange("p (n e) -> p n e", n=2)
        rt_mem, rt_off = A[:, xfree[0]:xfree[1]], [0]

        def rt(n):
            rt_off[0] += n
            assert rt_off[0] <= xfree[1] - xfree[0]
            return rt_mem[:, rt_off[0] - n:rt_off[0]]

        R = rt(72).rearrange("p (t e) -> p t e", t=2)
        dg = rt(8).rearrange("p (t e) -> p t e", t=2)
        eg = rt(8).rearrange("p (t e) -> p t e", t=2)
        cg = rt(8).rearrange("p (t e) -> p t e", t=2)
        og = rt(8).rearrange("p (t e) -> p t e", t=2)
        lm = rt(64).rearrange("p (t e) -> p t e", t=2)
        dd = rt(64).rearrange("p (t e) -> p t e", t=2)
        O1 = rt(64).rearrange("p (t e) -> p t e", t=2)
        O2 = rt(64).rearrange("p (t e) -> p t e", t=2)
        Cc = rt(64).rearrange("p (t e) -> p t e", t=2)
        cnt = rt(32)
        ext = rt(32)
        sm = rt(32).rearrange("p (n t) -> p n t", t=2)

        off[0] = 0
        sq = ppw[:, 0:1536]
        wgate3 = ppw[:, 1536:1920].rearrange("p (k c) -> p k c", k=KD)
        rot_tmp = ppw[:, 2048:3072]
        tcos = ppw[:, 3072:3840].rearrange("p (t f m e) -> p t f m e", t=2, f=2, m=3)
        gn = ppw[:, 3840:4096].rearrange("p (m e) -> p m e", m=4)
        invb = carve(DH // 2)
        trig = carve(128).rearrange("p (t f e) -> p t f e", t=2, f=2)
        trk = carve(128).rearrange("p (t f e) -> p t f e", t=2, f=2)
        trg = carve(128).rearrange("p (t f e) -> p t f e", t=2, f=2)
        posf = carve(4)
        gt = carve(96).rearrange("p (t c) -> p t c", t=2)
        ssn = carve(48)
        mx = carve(2 * 8).rearrange("p (b n) -> p b n", b=2)
        nmx = carve(2 * 8).rearrange("p (b n) -> p b n", b=2)
        sme = carve(2 * 8).rearrange("p (b n) -> p b n", b=2)
        fac = carve(2 * 8).rearrange("p (b n) -> p b n", b=2)
        cst = carve(32 * 3).rearrange("p (n m) -> p n m", n=3)
        mka = carve(2 * NC_).rearrange("p (t n) -> p t n", t=2)
        mk1 = carve(2 * NC_).rearrange("p (t n) -> p t n", t=2)
        pei = carve(256).rearrange("p (s c) -> p s c", s=2)
        peT = carve(32).rearrange("p (s j) -> p s j", s=2)
        kcT = carve(60)
        h1v = [sq[:, 768:1024], sq[:, 1024:1280]]
        vcr = carve(256).rearrange("p (g e) -> p g e", g=4)
        w2c = carve(256).rearrange("p (s c e) -> p s c e", s=2, c=2)
        h1T = carve(2 * 128).rearrange("p (c n) -> p c n", c=2)
        kcx = carve(64 * 4).rearrange("p (n e) -> p n e", n=4)
        tcc = carve(128 + 64 * 3)
        mcol = carve(8)
        off[0] = 0
        sgm = [carve(256) for _ in range(2)]
        mu = carve(256)
        var = carve(256)
        wdw = carve(8 * TAPS).rearrange("p (c w) -> p c w", c=8)
        accb = [carve(256) for _ in range(2)]
        prow = carve(384)
        bpw2 = carve(1024)[0:1, :]
        wdw_rows = ppw[0:TAPS, 3072:4096]

        posi = sb("posi", [P, 4], I32)
        pp = ppw[:, 0:2048].rearrange("p (t d) -> p t d", t=NT)
        wproj = ppw[:, 2048:4096].rearrange("p (c d) -> p c d", c=2)
        pin = ppw[:, 0:512].rearrange("p (t d) -> p t d", t=NT)
        pT2 = eqr

        def w_gu(s):
            return ring[:, s, 0:8192].rearrange("p (g k f) -> p g k f", g=2, k=8)

        def w_dn(s):
            return ring[:, s, 8192:12288].rearrange("p (f c d) -> p f c d", f=2, c=2)

        def dense(buf):
            return buf.rearrange("p (k n) -> p k n", k=KD)

        WB = [wb[:, i, :] for i in range(3)]
        R0 = [ring[:, 0, 4096 * i:4096 * (i + 1)] for i in range(3)]
        R1 = [ring[:, 1, 4096 * i:4096 * (i + 1)] for i in range(3)]
        PW1 = [WB[0], WB[1], WB[2], R1[0]]
        PW2 = [R1[1], R1[2]]
        cv0 = ppw[:, 0:KD * (T + TAPS - 1)].rearrange("p (k q) -> p k q", k=KD)
        cT = hn[:, :, :].rearrange("p t (k q) -> p (t k) q", q=T)

        S = ring[:, 1, :]
        raw = S[:, 0:3072].rearrange("p (t n e) -> p t n e", t=2, n=24)
        rotq = S[:, 3072:5120].rearrange("p (t n e) -> p t n e", t=2, n=16)
        rotk = S[:, 5120:7168].rearrange("p (t m u e) -> p t m u e", t=2, m=8, u=2)
        vv = S[:, 7168:8192].rearrange("p (t s e) -> p t s e", t=2, s=2)
        xp = S[:, 8192:9216].rearrange("p (s g u e) -> p s g u e", s=2, g=4, u=2)
        xpT = S[:, 9216:10240].rearrange("p (s g m) -> p s g m", s=2, g=4)
        Bc = S[:, 10240:12160].rearrange("p (s j g n) -> p s j g n", s=2, j=16, g=4)
        OT = S[:, 0:2048].rearrange("p (k q) -> p k q", k=8)
        Pc = S[:, 2048:3072].rearrange("p (t n e) -> p t n e", t=2, n=16)
        pT = S[:, 3072:6144].rearrange("p (b n) -> p b n", b=2)
        Pb = S[:, 8192:11264].rearrange("p (b i n) -> p b i n", b=2, i=2)
        PcT = S[:, 11264:12288].rearrange("p (c q) -> p c q", c=4)
        qT = hn[:, :, :].rearrange("p t (k q) -> p (t k) q", q=T)
        kT = xnT[:, :, :].rearrange("p (s g) q -> p s g q", s=2)

        x_in, vec_in, misc_in, p_in = sem("x_in"), sem("vec_in"), sem("misc_in"), sem("p_in")
        pw1_in = [sem(f"pw1_in{i}") for i in range(4)]
        pw2_in = [sem(f"pw2_in{i}") for i in range(2)]
        ple_in = [sem(f"ple_in{i}") for i in range(2)]
        proj_in = sem("proj_in")
        att_in, mask_ok, c_bld = sem("att_in"), sem("mask_ok"), sem("c_bld")
        x_bld = sem("x_bld")
        pe_step, pool_step = sem("pe_step"), sem("pool_step")
        in_in = [sem(f"in_in{i}") for i in range(5)]
        cw_in = [sem(f"cw_in{i}") for i in range(2)]
        wo_in = [sem(f"wo_in{i}") for i in range(2)]
        gu_in = [sem(f"gu_in{i}") for i in range(2)]
        dn_in = [sem(f"dn_in{i}") for i in range(2)]
        out_st = sem("out_st")
        c_pool, c_dve, c_act = sem("c_pool"), sem("c_dve"), sem("c_act")
        const_ok = sem("const_ok")
        vtr, vec_ok = sem("vtr"), sem("vec_ok")
        h_dve, h_act = sem("h_dve"), sem("h_act")
        ssq_ok, var_ok, rs_ok, hn_dve, hn_act, tr_ok = sem("ssq_ok"), sem("var_ok"), sem("rs_ok"), sem("hn_dve"), sem("hn_act"), sem("tr_ok")
        xt_dve, xt_act = sem("xt_dve"), sem("xt_act")
        pw1_mm, sig_ok, glu_ok, conv_ok, lnmm, ln_mu, ln_c, ln_sq, ln_r, silu_ok, pw2_mm = [
            sem(s) for s in ("pw1_mm", "sig_ok", "glu_ok", "conv_ok", "lnmm", "ln_mu", "ln_c", "ln_sq",
                             "ln_r", "silu_ok", "pw2_mm")]
        ptr, pT_ok, pp_mm, pp_ok = sem("ptr"), sem("pT_ok"), sem("pp_mm"), sem("pp_ok")
        rt_mm, rt_d, rt_e, rt_c, rt_pf, rt_s, rt_row, row_dve, row_act, tab_ok, acc_init = [
            sem(s) for s in ("rt_mm", "rt_d", "rt_e", "rt_c", "rt_pf", "rt_s", "rt_row", "row_dve",
                             "row_act", "tab_ok", "acc_init")]
        sel_ok, wT_ok, wT_free = sem("sel_ok"), sem("wT_ok"), sem("wT_free")
        ga_mm, xg_ok, xt_mm, xgT_ok = sem("ga_mm"), sem("xg_ok"), sem("xt_mm"), sem("xgT_ok")
        gu_mm, sil_ok, h_ok, ht_mm, hT_ok, y_mm, y_ok = [
            sem(s) for s in ("gu_mm", "sil_ok", "h_ok", "ht_mm", "hT_ok", "y_mm", "y_ok")]
        slot_free = sem("slot_free")
        XN = ("x_sel", "x_ga", "x_xg", "x_xt", "x_xgT", "x_gu", "x_sil", "x_h", "x_ht", "x_hT", "x_y", "x_ysb", "x_done", "x_wT")
        X = {n: sem(n) for n in XN}
        pl_mm, pl_sig, pl_mul = sem("pl_mm"), sem("pl_sig"), sem("pl_mul")
        wb_free = sem("wb_free")
        xp_mm, xp_ok, xpt_mm, xpt_ok, B_ok = sem("xp_mm"), sem("xp_ok"), sem("xpt_mm"), sem("xpt_ok"), sem("B_ok")
        kv_mm, kv_dve, kv_act, gate_mm, gate_ok, q_mm = (sem("kv_mm"), sem("kv_dve"), sem("kv_act"), sem("gate_mm"),
                                                         sem("gate_ok"), sem("q_mm"))
        trig_ok, sin_ok = sem("trig_ok"), sem("sin_ok")
        sq_ok, sq_used, rot_ok = sem("sq_ok"), sem("sq_used"), sem("rot_ok")
        c1_mm, c1_x, c1_s, c1_g, c1_t, c1_T, kc_mm, kc_x, kct_mm, kcT_ok, vcr_ok = [
            sem(s) for s in ("c1_mm", "c1_x", "c1_s", "c1_g", "c1_t", "c1_T", "kc_mm", "kc_x", "kct_mm",
                             "kcT_ok", "vcr_ok")]
        qt_mm, qt_dve, qt_act = sem("qt_mm"), sem("qt_dve"), sem("qt_act")
        sc_mm, sc_d, sc_e, sc_p, sct_mm, pct_ok = (sem("sc_mm"), sem("sc_d"), sem("sc_e"), sem("sc_p"),
                                                   sem("sct_mm"), sem("pct_ok"))
        s_mm, s_max, s_exp, s_fac, s_scl, t_mm, pt_dve, pt_act, o_mm, o_ok, wo_mm = [
            sem(s) for s in ("s_mm", "s_max", "s_exp", "s_fac", "s_scl", "t_mm", "pt_dve", "pt_act", "o_mm",
                             "o_ok", "wo_mm")]

        block = ctx.enter_context(nc.Block())

        @block.sync
        def _(sp):
            def cols(w, n):
                return w.rearrange("(k p) n -> p k n", p=P)[:, :, 512 * n:512 * (n + 1)]

            def expert(L, e, s):
                for g, w in enumerate((moe_w_gate, moe_w_up)):
                    sp.dma_start(ring[:, s, 4096 * g:4096 * (g + 1)].rearrange("p (j r) -> p j r", j=4),
                                 w[L, e].rearrange("(j p c) f -> p j (c f)", j=4, c=2)).then_inc(gu_in[s], 16)
                sp.dma_start(ring[:, s, 8192:12288].rearrange("p (f r) -> p f r", f=2),
                             moe_w_down[L, e].rearrange("(f p c) d -> p f (c d)", f=2, c=2)).then_inc(dn_in[s], 16)

            def experts(L):
                with sp.Fori(1, NE // 2) as it:
                    for s in range(2):
                        sp.wait_ge(slot_free, it * 2 + (s - 1 + NE * L))
                        expert(L, it * 2 + s, s)

            def embeddings(L):
                sp.dma_start(pin, p[L, 0].rearrange("(t q) d -> q t d", q=P)).then_inc(p_in, 16)
                sp.dma_start(wproj, ple_w_proj[L].rearrange("(c p) d -> p c d", p=P)).then_inc(proj_in, 16)

            for t in range(NT):
                sp.dma_start(h[:, t, :], x[0, t * P:(t + 1) * P, :]).then_inc(x_in, 16)
            sp.dma_start(dense(PW1[0]), cols(conv_w_pw1[0], 0)).then_inc(pw1_in[0], 16)
            sp.dma_start(dense(PW1[1]), cols(conv_w_pw1[0], 2)).then_inc(pw1_in[1], 16)
            sp.dma_start(dense(PW1[2]), cols(conv_w_pw1[0], 1)).then_inc(pw1_in[2], 16)
            sp.dma_start(dense(PW1[3]), cols(conv_w_pw1[0], 3)).then_inc(pw1_in[3], 16)
            for n in range(2):
                sp.dma_start(dense(PW2[n]), cols(conv_w_pw2[0], n)).then_inc(pw2_in[n], 16)
            expert(0, 0, 0)
            sp.wait_ge(pw1_mm, 4)
            for n in range(2):
                sp.dma_start(dense(WB[n]), cols(ple_w_gate[0], n)).then_inc(ple_in[n], 16)
            sp.wait_ge(pw1_mm, 8)
            sp.dma_start(dense(WB[2]), cols(nsa_w_in[0], 2)).then_inc(in_in[2], 16)
            sp.wait_ge(pw2_mm, 4)
            embeddings(0)
            expert(0, 1, 1)
            experts(0)
            sp.wait_ge(slot_free, NE - 1)
            for n, b in ((3, 0), (4, 1), (0, 2)):
                sp.dma_start(dense(R0[b]), cols(nsa_w_in[0], n)).then_inc(in_in[n], 16)
            sp.wait_ge(pl_mm, 2)
            sp.dma_start(dense(WB[0]), cols(nsa_w_in[0], 1)).then_inc(in_in[1], 16)
            sp.wait_ge(pl_mm, 4)
            sp.dma_start(WB[1].rearrange("p (j n) -> p j n", j=16),
                         nsa_cmp_w1[0, 0].rearrange("(j p) n -> p j n", p=P)).then_inc(cw_in[0], 16)
            sp.wait_ge(h_dve, H_DVE[3])
            sp.dma_start(wgate3, nsa_w_in[0].rearrange("(k p) n -> p k n", p=P)[:, :, 2560:2608]).then_inc(att_in, 16)
            sp.dma_start(pei[0:16, :, :], nsa_cmp_pe[0].rearrange("s (j u) e -> j s (u e)", u=2)).then_inc(att_in, 16)
            for m, v in enumerate((nsa_q_norm[0:1, :], nsa_k_norm[0, 1:2, :], nsa_k_norm[0, 2:3, :], nsa_k_norm[0, 0:1, :])):
                sp.dma_start(gn[:, m, :], v.broadcast_to([P, DH])).then_inc(att_in, 16)
            sp.dma_start(invb, inv_freq.broadcast_to([P, DH // 2])).then_inc(att_in, 16)
            for s in range(2):
                sp.dma_start(w2c[:, s, :, :], nsa_cmp_w2[0, s].rearrange("(c p) n -> p c n", p=P)).then_inc(att_in, 16)
            sp.wait_ge(xp_mm, 2)
            sp.dma_start(WB[2].rearrange("p (j n) -> p j n", j=16),
                         nsa_cmp_w1[0, 1].rearrange("(j p) n -> p j n", p=P)).then_inc(cw_in[1], 16)
            sp.wait_ge(q_mm, 4)
            sp.dma_start(dense(WB[0]), cols(nsa_w_out[0], 0)).then_inc(wo_in[0], 16)
            sp.wait_ge(c1_mm, 1)
            sp.dma_start(dense(WB[1]), cols(nsa_w_out[0], 1)).then_inc(wo_in[1], 16)
            expert(1, 0, 0)
            sp.wait_ge(c1_mm, 2)
            sp.dma_start(dense(WB[2]), cols(ple_w_gate[1], 0)).then_inc(ple_in[0], 16)
            sp.wait_ge(wo_mm, 4)
            embeddings(1)
            expert(1, 1, 1)
            sp.dma_start(dense(WB[0]), cols(ple_w_gate[1], 1)).then_inc(ple_in[1], 16)
            experts(1)
            sp.wait_ge(h_dve, H_DVE[6])
            for t in range(NT):
                sp.dma_start(out[0, t * P:(t + 1) * P, :], h[:, t, :]).then_inc(out_st, 16)
            sp.wait_ge(out_st, 16 * NT)

        PLE_W = [[WB[0], WB[1]], [WB[2], WB[0]]]

        @block.tensor
        def _(pe):
            def norm_T(a):
                pe.wait_ge(hn_dve, a + 1)
                pe.wait_ge(hn_act, a + 1)
                for kp in range(4):
                    for kk in range(2):
                        for t in range(NT):
                            k = 2 * kp + kk
                            i = pe.transpose(PS[:, 4 + kp, (kk * 2 + t) * P:(kk * 2 + t + 1) * P],
                                             hn[:, t, k * P:(k + 1) * P], ident[:, :])
                    i.then_inc(tr_ok, 1)

            def xnT_ready(a, k):
                kp = k // 2
                pe.wait_ge(xt_act if kp % 2 else xt_dve, 4 * a + 2 * (kp // 2) + k % 2 + 1)

            def tokens_out(w, bank, t, done, a=None, lhs=xnT, start=True):
                for k in range(KD):
                    if a is not None:
                        xnT_ready(a, k)
                    i = pe.matmul(PS[:, bank, :], lhs[:, k, t * P:(t + 1) * P], w[:, k, :],
                                  start=start and k == 0, stop=(k == KD - 1))
                i.then_inc(done, 1)

            pe.wait_ge(const_ok, 1)
            pe.wait_ge(vec_in, 16 * N_VEC)
            pe.transpose(PS[:, 0, 0:NROWS], prow[0:NROWS, 0:P], ident[0:NROWS, 0:NROWS]).then_inc(vtr, 1)
            for c in range(2):
                i = pe.transpose(PS[:, 1, c * 8:c * 8 + 8], prow[0:8, P + c:P + 256:2], ident[0:8, 0:8])
            i.then_inc(vtr, 1)
            for c in range(KD):
                i = pe.transpose(PS[:, 2, c * TAPS:(c + 1) * TAPS], wdw_rows[:, c * P:(c + 1) * P],
                                 ident[0:TAPS, 0:TAPS])
            i.then_inc(vtr, 1)

            norm_T(0)
            for c in range(KD):
                b = c // 4
                pe.wait_ge(pw1_in[2 * b], 16)
                pe.wait_ge(pw1_in[2 * b + 1], 16)
                if c >= 4:
                    pe.wait_ge(glu_ok, c - 3)
                else:
                    pe.wait_ge(vec_ok, 3)
                for g in range(2):
                    w = dense(PW1[2 * b + g])
                    for k in range(KD):
                        xnT_ready(0, k)
                        i = pe.matmul(PS[:, c % 4, g * T:(g + 1) * T], w[:, k, (c % 4) * P:(c % 4 + 1) * P],
                                      xnT[:, k, :], start=(k == 0), stop=(k == KD - 1))
                i.then_inc(pw1_mm, 1)
            pe.wait_ge(glu_ok, KD)
            for c in range(KD):
                pe.wait_ge(conv_ok, c + 1)
                i = pe.matmul(PS[:, 4, 0:T], ones[:, :], cT[:, c, :], start=(c == 0), stop=(c == KD - 1))
            i.then_inc(lnmm, 1)
            for c in range(KD):
                pe.wait_ge(ln_sq, c + 1)
                i = pe.matmul(PS[:, 5, 0:T], ones[:, :], xnT[:, c, :], start=(c == 0), stop=(c == KD - 1))
            i.then_inc(lnmm, 1)
            for n in range(2):
                pe.wait_ge(pw2_in[n], 16)
                for t in range(NT):
                    bk = 2 * n + t
                    pe.matmul(PS[:, bk, :], ones[0:1, :], bpw2[:, 512 * n:512 * (n + 1)], start=True, stop=False)
                    for k in range(KD):
                        pe.wait_ge(silu_ok, k + 1)
                        i = pe.matmul(PS[:, bk, :], cT[:, k, t * P:(t + 1) * P], dense(PW2[n])[:, k, :],
                                      start=False, stop=(k == KD - 1))
                    i.then_inc(pw2_mm, 1)

            def gather(lhs):
                for t in range(NT):
                    for j in range(4):
                        i = pe.matmul(PS[32 * j:32 * j + 32, BGX, 0:Q4], lhs[:, t, :], hn[:, t, Q4 * j:Q4 * (j + 1)],
                                      start=(t == 0), stop=(t == NT - 1))
                return i

            def xg_T():
                for c in range(2):
                    i = pe.transpose(PS[:, BGX, Q4 + P * c:Q4 + P * (c + 1)], xg[:, c::2], ident[:, :])
                return i

            def gate_up(s, xT):
                for k in range(8):
                    for j in range(4):
                        i = pe.matmul(PS[32 * j:32 * j + 32, BGU, 0:256], xT[:, k, :],
                                      w_gu(s)[:, j // 2, k, 256 * (j % 2):256 * (j % 2 + 1)],
                                      start=(k == 0), stop=(k == 7))
                return i

            def h_T():
                pe.sem_inc(pe_step, 1)
                for c in range(2):
                    i = pe.transpose(PS[:, BHT, 64 * c:64 * (c + 1)], hh[64:128, c::2], ident[64:128, 64:128])
                return i

            def down(s):
                for q in range(4):
                    f, c = q // 2, q % 2
                    for j in range(4):
                        i = pe.matmul(PS[32 * j:32 * j + 32, BY, 0:Q4], hT[:, c, 32 * f:32 * f + 32],
                                      w_dn(s)[:, f, c, Q4 * j:Q4 * (j + 1)], start=(q == 0), stop=(q == 3))
                return i

            def scatter(w):
                for t in range(NT):
                    for j in range(4):
                        i = pe.matmul(PS[:, ACC + j, 256 * t:256 * (t + 1)], w[32 * j:32 * j + 32, t * P:(t + 1) * P],
                                      ysb[32 * j:32 * j + 32, :], start=False, stop=False, skip_group_check=True)
                return i

            def moe(L):
                a = 3 * L + 1
                norm_T(a)
                pe.wait_ge(misc_in, 16 * N_MISC)
                xnT_ready(a, 0)
                xnT_ready(a, 1)
                for t in range(NT):
                    o = PS[:, BGU, 64 * t:64 * t + 36]
                    pe.matmul(o, ones[0:1, :], rowb[0:1, 36 * L:36 * (L + 1)], start=True, stop=False)
                    for k in range(KD):
                        xnT_ready(a, k)
                        i = pe.matmul(o, xnT[:, k, t * P:(t + 1) * P], wr[:, L, k, :], start=False, stop=(k == KD - 1))
                i.then_inc(rt_mm, 1)
                pe.wait_ge(p_in, 16 * (L + 1))
                pe.wait_ge(xt_dve, 4 * a + 4)
                pe.wait_ge(xt_act, 4 * a + 4)
                for c in range(2):
                    for t in range(NT):
                        i = pe.transpose(PS[:, 5, (2 * c + t) * P:(2 * c + t + 1) * P], pin[:, t, c * P:(c + 1) * P], ident[:, :])
                i.then_inc(ptr, 1)
                pe.wait_ge(pT_ok, L + 1)
                pe.wait_ge(proj_in, 16 * (L + 1))
                for n in range(2):
                    for t in range(NT):
                        for c in range(2):
                            i = pe.matmul(PS[:, 2 * n + t, :], pT2[:, c, t * P:(t + 1) * P],
                                          wproj[:, c, 512 * n:512 * (n + 1)], start=(c == 0), stop=(c == 1))
                        i.then_inc(pp_mm, 1)
                pe.wait_ge(rt_c, L + 1)
                pe.matmul(PS[:, 6, 0:32], upper[:, :], Cc[:, 0, :], start=True, stop=True)
                pe.matmul(PS[:, 6, 32:64], upper[:, :], Cc[:, 1, :], start=True, stop=False)
                pe.matmul(PS[:, 6, 32:64], ones[:, :], Cc[:, 0, :], start=False, stop=True)
                pe.matmul(PS[:, 6, 64:96], ones[:, :], Cc[:, 0, :], start=True, stop=False)
                pe.matmul(PS[:, 6, 64:96], ones[:, :], Cc[:, 1, :], start=False, stop=True).then_inc(rt_pf, 1)
                pe.wait_ge(pp_ok, 4 * (L + 1))
                for t in range(NT):
                    for j in range(4):
                        i = pe.matmul(PS[:, ACC + j, 256 * t:256 * (t + 1)], ident[:, :], h[:, t, Q4 * j:Q4 * (j + 1)],
                                      start=(t == 0), stop=False, skip_group_check=True)
                i.then_inc(acc_init, 1)
                pe.wait_ge(rt_s, L + 1)
                for v, bk in ((S4, 5), (W4, 7)):
                    for t in range(NT):
                        for s in range(2):
                            i = pe.matmul(PS[:, bk, (2 * s + t) * P:(2 * s + t + 1) * P],
                                          v[:, t, s:s + 1].broadcast_to([P, P]), ident[:, :], start=True, stop=True)
                i.then_inc(rt_row, 1)
                pe.wait_ge(row_dve, L + 1)
                pe.wait_ge(row_act, L + 1)
                pe.wait_ge(tab_ok, L + 1)
                g0 = (NE + 1) * L
                pe.wait_ge(sel_ok, g0 + 1)
                gather(sel[0]).then_inc(ga_mm, 1)
                pe.wait_ge(xg_ok, g0 + 1)
                xg_T().then_inc(xt_mm, 1)
                with pe.Fori(0, NE // 2) as it:
                    for s in range(2):
                        n = it * 2 + (s + NE * L + 1)
                        gi = it * 2 + (s + g0 + 2)
                        ld = it * 16 + 16 * (NE // 2 * L + 1)
                        pe.wait_ge(gu_in[s], ld * 2)
                        pe.wait_ge(xgT_ok, gi - 1)
                        gate_up(s, xgT).then_inc(gu_mm, 1)
                        pe.wait_ge(sel_ok, gi)
                        gather(sel[1 - s]).then_inc(ga_mm, 1)
                        pe.wait_ge(h_ok, n)
                        h_T().then_inc(ht_mm, 1)
                        pe.wait_ge(dn_in[s], ld)
                        pe.wait_ge(hT_ok, n)
                        down(s).then_inc(y_mm, 1)
                        pe.wait_ge(xg_ok, gi)
                        xg_T().then_inc(xt_mm, 1)
                        pe.wait_ge(wT_ok, gi - 1)
                        pe.wait_ge(y_ok, n)
                        scatter(wT[s]).then_inc(wT_free, 1)
                        e = it * 2 + s
                        more = pe.value_load(tab[0:1, 0, bass.ds(e, 1)], min_val=0, max_val=7)
                        before = pe.value_load(tab[0:1, 1, bass.ds(e, 1)], min_val=0, max_val=64)
                        with pe.If(more > 0):
                            with pe.Fori(0, more) as r:
                                c = before + r + 1
                                pe.wait_ge(X["x_sel"], c)
                                pe.wait_ge(xgT_ok, gi)
                                gather(xsel).then_inc(X["x_ga"], 1)
                                pe.wait_ge(X["x_xg"], c)
                                xg_T().then_inc(X["x_xt"], 1)
                                pe.wait_ge(X["x_xgT"], c)
                                gate_up(s, xxgT).then_inc(X["x_gu"], 1)
                                pe.wait_ge(X["x_h"], c)
                                h_T().then_inc(X["x_ht"], 1)
                                pe.wait_ge(X["x_hT"], c)
                                down(s).then_inc(X["x_y"], 1)
                                pe.wait_ge(X["x_wT"], c)
                                pe.wait_ge(X["x_ysb"], c)
                                scatter(xwT).then_inc(X["x_done"], 1)
                        pe.drain().then_inc(slot_free, 1)
                norm_T(a + 1)
                for n in range(2):
                    pe.wait_ge(ple_in[n], 16 * (L + 1))
                    for t in range(NT):
                        tokens_out(dense(PLE_W[L][n]), 2 * n + t, t, pl_mm, a + 1)

            pe.sem_inc(wT_free, 1)
            pe.sem_inc(X["x_done"], 1)
            moe(0)

            norm_T(3)
            pe.wait_ge(in_in[2], 16)
            pe.wait_ge(pl_mul, 4)
            for u in range(2):
                for k in range(KD):
                    xnT_ready(3, k)
                    i = pe.matmul(PS[:, u, :], xnT[:, k, u::2], dense(WB[2])[:, k, :], start=(k == 0), stop=(k == KD - 1))
                i.then_inc(xp_mm, 1)
            for s in range(2):
                pe.wait_ge(in_in[3 + s], 16)
                for t in range(NT):
                    bk = 2 + t if s == 0 else 4 + t
                    tokens_out(dense(R0[s]), bk, t, kv_mm, 3)
            pe.wait_ge(att_in, 16 * N_ATT)
            for t in range(NT):
                for k in range(KD):
                    i = pe.matmul(PS[:, 6, 64 * t:64 * t + 48], xnT[:, k, t * P:(t + 1) * P], wgate3[:, k, :],
                                  start=(k == 0), stop=(k == KD - 1))
            i.then_inc(gate_mm, 1)
            pe.wait_ge(xp_ok, 2)
            for s in range(2):
                for g in range(NKV):
                    i = pe.transpose(PS[:, s, g * P:(g + 1) * P], xp[:, s, g, :, :].rearrange("p u e -> p (u e)"), ident[:, :])
                i.then_inc(xpt_mm, 1)
            for s in range(2):
                i = pe.transpose(PS[:, 7, 16 * s:16 * s + 16], pei[0:16, s, :], ident[0:16, 0:16])
            i.then_inc(xpt_mm, 1)
            for n in range(2):
                pe.wait_ge(in_in[n], 16)
                if n == 0:
                    pe.wait_ge(kv_dve, 2)
                    pe.wait_ge(kv_act, 2)
                else:
                    pe.wait_ge(kv_dve, 4)
                    pe.wait_ge(kv_act, 4)
                for t in range(NT):
                    tokens_out(dense(R0[2] if n == 0 else WB[0]), 2 + 2 * n + t, t, q_mm)
            for s in range(2):
                pe.wait_ge(cw_in[s], 16)
                pe.wait_ge(B_ok, s + 1)
                w1 = (WB[1] if s == 0 else WB[2]).rearrange("p (j n) -> p j n", j=16)
                for j in range(16):
                    i = pe.matmul(PS[0:60, s, 0:256], Bc[:, s, j, :, :].rearrange("p g n -> p (g n)"), w1[:, j, :], start=(j == 0), stop=(j == 15))
                i.then_inc(c1_mm, 1)
            for s in range(2):
                pe.wait_ge(c1_g, s + 1)
                if s == 1:
                    pe.wait_ge(kc_x, 1)
                for c in range(2):
                    i = pe.transpose(PS[:, 0, 256 + 64 * c:256 + 64 * c + 60], h1v[s][0:60, c * P:(c + 1) * P], ident[0:60, 0:60])
                i.then_inc(c1_t, 1)
                pe.wait_ge(c1_T, s + 1)
                if s == 0:
                    for c in range(2):
                        i = pe.matmul(PS[0:60, 0, 0:64], h1T[:, c, 0:60], w2c[:, 0, c, :], start=(c == 0), stop=(c == 1))
                else:
                    for c in range(2):
                        for g in range(4):
                            for q in range(4):
                                i = pe.matmul(PS[32 * q:32 * q + NC_, 1, 256 + 64 * g:256 + 64 * g + 64], h1T[:, c, NC_ * g:NC_ * (g + 1)],
                                              w2c[:, 1, c, :], start=(c == 0 and g == 0), stop=(c == 1), skip_group_check=True)
                i.then_inc(kc_mm, 1)
            pe.wait_ge(rot_ok, 6)
            for b in range(4):
                for kk in range(2):
                    for t in range(NT):
                        hp = 2 * b + kk
                        i = pe.transpose(PS[:, 2 + b, (2 * kk + t) * P:(2 * kk + t + 1) * P],
                                         rotq[:, t, 2 * hp:2 * hp + 2, :], ident[:, :])
                i.then_inc(qt_mm, 1)
            for b in range(4):
                if b < 2:
                    bk = 6 + b
                else:
                    bk = b
                    pe.wait_ge(qt_dve if b % 2 == 0 else qt_act, 1)
                for kk in range(2):
                    for t in range(NT):
                        m = 4 * (b // 2) + 2 * (b % 2) + kk
                        i = pe.transpose(PS[:, bk, (2 * kk + t) * P:(2 * kk + t + 1) * P], rotk[:, t, m, :, :], ident[:, :])
                i.then_inc(qt_mm, 1)
            pe.wait_ge(kc_x, 2)
            pe.transpose(PS[:, 0, 384:444], kcx[0:60, 2:4, :], ident[0:60, 0:60]).then_inc(kct_mm, 1)
            pe.wait_ge(kcT_ok, 1)
            pe.wait_ge(vcr_ok, 1)
            pe.wait_ge(qt_dve, 4)
            pe.wait_ge(qt_act, 4)
            for hp in range(8):
                for t in range(NT):
                    for i_ in range(2):
                        r = slice(64 * i_, 64 * i_ + 64)
                        o = 128 * t + 16 * hp
                        i = pe.matmul(PS[:, i_, o:o + NC_], qT[r, hp, t * P:(t + 1) * P], kcT[r, NC_ * (hp // 2):NC_ * (hp // 2 + 1)],
                                      start=True, stop=True)
            i.then_inc(sc_mm, 1)

            def scores(hp):
                g = hp // 2
                if hp > 0:
                    pe.wait_ge(s_max, 9 * hp - 1)
                else:
                    pe.wait_ge(sc_d, 1)
                for t in range(NT):
                    for i_ in range(2):
                        r = slice(64 * i_, 64 * i_ + 64)
                        i = pe.matmul(PS[:, 2 * t + i_, 0:256 * (t + 1)], qT[r, hp, t * P:(t + 1) * P],
                                      kT[r, :, g, 0:P * (t + 1)], start=True, stop=True)
                i.then_inc(s_mm, 1)

            def probs_T(hp):
                pe.wait_ge(s_scl, 8 * (hp + 1))
                if hp > 0:
                    pe.wait_ge(pt_dve, 2 * hp)
                    pe.wait_ge(pt_act, hp)
                for n in range(12):
                    i_, s, q = n // 6, (n // 3) % 2, n % 3
                    src = Pb[:, hp % 2, i_, 128 * s:128 * s + 128] if q == 0 else \
                        Pb[:, hp % 2, i_, 256 + 256 * s + 128 * (q - 1):256 + 256 * s + 128 * q]
                    i = pe.transpose(PS[:, 4 + n // 4, (n % 4) * P:(n % 4 + 1) * P], src, ident[:, :])
                    if n % 4 == 3:
                        i.then_inc(t_mm, 1)

            def pv(hp):
                g = hp // 2
                pe.wait_ge(pt_dve, 2 * hp + 2)
                pe.wait_ge(pt_act, hp + 1)
                if hp > 0:
                    pe.wait_ge(o_ok, hp)
                for s in range(2):
                    for kb in range(2):
                        for i_ in range(2):
                            o = i_ * 768 + s * 384
                            rhs = pT[:, hp % 2, o:o + 256] if kb == 0 else pT[:, hp % 2, o + 256:o + 384]
                            pe.matmul(PS[64 * i_:64 * i_ + 64, 7, 128 * kb:256], vv[:, kb, s, 64 * g:64 * g + 64], rhs,
                                      start=(s == 0 and kb == 0), stop=False, skip_group_check=True)
                for i_ in range(2):
                    hd = 2 * hp + i_
                    r = slice(32 * (hd % 4), 32 * (hd % 4) + NC_)
                    i = pe.matmul(PS[64 * i_:64 * i_ + 64, 7, 0:256], vcr[r, g, :], PcT[r, hd // 4, :],
                                  start=False, stop=True, skip_group_check=True)
                i.then_inc(o_mm, 1)

            scores(0)
            pe.wait_ge(sc_p, 1)
            for t in range(NT):
                for c in range(4):
                    i = pe.transpose(PS[:, 4 + c // 2, (2 * (c % 2) + t) * P:(2 * (c % 2) + t + 1) * P], Pc[:, t, 4 * c:4 * c + 4, :], ident[:, :])
            i.then_inc(sct_mm, 1)
            pe.wait_ge(pct_ok, 2)
            for hp in range(8):
                if hp < 7:
                    scores(hp + 1)
                probs_T(hp)
                pv(hp)
            pe.wait_ge(o_ok, 8)
            for n in range(2):
                pe.wait_ge(wo_in[n], 16)
                for t in range(NT):
                    tokens_out(dense(WB[n]), 2 * n + t, t, wo_mm, lhs=OT)
            moe(1)

        @block.gpsimd
        def _(pool):
            g = nc.gpsimd
            own = [0]

            def link(i):
                own[0] += 1
                i.then_inc(c_pool, 1)
                pool.wait_ge(c_pool, own[0])

            link(g.memset(ident[:, :], 0.0))
            link(g.affine_select(out=ident[:, :], in_=ident[:, :], compare_op=ALU.not_equal, fill=1.0, base=0,
                                 pattern=[[-1, P]], channel_multiplier=1))
            link(g.memset(ones[:, :], 1.0))
            link(g.memset(nhalf[:, :], -0.5))
            link(g.affine_select(out=upper[:, :], in_=ones[:, :], compare_op=ALU.is_gt, fill=0.0, base=0,
                                 pattern=[[1, P]], channel_multiplier=-1))
            link(g.memset(cmask[:, :, :], 0.0))
            link(g.affine_select(out=cmask[:, 1, :], in_=cmask[:, 1, :], compare_op=ALU.is_ge, fill=NEG, base=0,
                                 pattern=[[-1, P]], channel_multiplier=1))
            link(g.iota(ioti[:, :], pattern=[[1, 32]], base=0, channel_multiplier=0))
            link(g.tensor_copy(iot[:, :], ioti[:, :]))
            for q in range(4):
                link(g.iota(ioti[32 * q:32 * q + 32, 0:1], pattern=[[0, 1]], base=0, channel_multiplier=1))
            g.tensor_copy(colp[:, :], ioti[:, 0:1]).then_inc(const_ok, 1)

            def rsqrt(n, x):
                pool.wait_ge(var_ok, n)
                g.tensor_tensor(x, x, nhalf[0:x.shape[0], 0:1].broadcast_to(list(x.shape)), ALU.pow).then_inc(rs_ok, 1)

            def build_block(c32, cc, to_sel, to_wT, count, base, s_ok, w_ok):
                for t in range(NT):
                    for k in range(2):
                        i = g.tensor_scalar(eq4[:, t, k, :], c32, S4[:, t, k:k + 1], None, ALU.is_equal)
                i.then_inc(count, 1)
                g.tensor_scalar(eqr, srow, cc, None, ALU.is_equal).then_inc(count, 1)
                pool.wait_ge(count, base + 1)
                g.tensor_tensor(to_sel, eq4[:, :, 0, :], eq4[:, :, 1, :], ALU.add).then_inc(s_ok, 1)
                pool.wait_ge(count, base + 2)
                g.tensor_tensor(eqr, eqr, wrow, ALU.mult).then_inc(count, 1)
                pool.wait_ge(count, base + 3)
                g.tensor_tensor(to_wT, eqr[:, 0, :], eqr[:, 1, :], ALU.add).then_inc(w_ok, 1)

            def moe(L):
                g0 = (NE + 1) * L
                pool.wait_ge(row_dve, L + 1)
                pool.wait_ge(row_act, L + 1)
                pool.wait_ge(tab_ok, L + 1)
                g.tensor_copy(cur32, iot[:, :]).then_inc(c_bld, 1)
                g.tensor_copy(curc, colp[:, :]).then_inc(c_bld, 1)
                pool.wait_ge(c_bld, 5 * g0 + 2)
                build_block(cur32, curc, sel[0], wT[0], c_bld, 5 * g0 + 2, sel_ok, wT_ok)
                with pool.Fori(0, NE // 2) as it:
                    for s in range(2):
                        gi = it * 2 + (s + g0 + 1)
                        pool.wait_ge(wT_free, it * 2 + (s + NE * L + 1))
                        pool.sem_inc(pool_step, 1)
                        g.tensor_scalar(cur32, cur32, 256.0, None, ALU.add).then_inc(c_bld, 1)
                        g.tensor_scalar(curc, curc, 256.0, None, ALU.add).then_inc(c_bld, 1)
                        pool.wait_ge(c_bld, gi * 5 + 2)
                        pool.sem_inc(pool_step, 1)
                        build_block(cur32, curc, sel[1 - s], wT[1 - s], c_bld, gi * 5 + 2, sel_ok, wT_ok)
                        e = it * 2 + s
                        more = pool.value_load(tab[0:1, 0, bass.ds(e, 1)], min_val=0, max_val=7)
                        before = pool.value_load(tab[0:1, 1, bass.ds(e, 1)], min_val=0, max_val=64)
                        with pool.If(more > 0):
                            g.tensor_scalar(xcur32, cur32, -256.0, None, ALU.add)
                            g.tensor_scalar(xcurc, curc, -256.0, None, ALU.add)
                            pool.drain()
                            with pool.Fori(0, more) as r:
                                c = before + r
                                pool.wait_ge(X["x_done"], c + 1)
                                pool.sem_inc(pool_step, 1)
                                g.tensor_scalar(xcur32, xcur32, float(SLOTS), None, ALU.add).then_inc(x_bld, 1)
                                g.tensor_scalar(xcurc, xcurc, float(SLOTS), None, ALU.add).then_inc(x_bld, 1)
                                pool.wait_ge(x_bld, c * 5 + 2)
                                pool.sem_inc(pool_step, 1)
                                build_block(xcur32, xcurc, xsel, xwT, x_bld, c * 5 + 2, X["x_sel"], X["x_wT"])

            rsqrt(1, rstd[:, 1, :])
            rsqrt(2, var)
            rsqrt(3, rstd[:, 1, :])
            moe(0)
            rsqrt(4, rstd[:, 1, :])
            rsqrt(5, rstd[:, 1, :])
            pool.wait_ge(h_dve, H_DVE[3])
            link(g.memset(mka, 0.0))
            link(g.memset(mk1, 1.0))
            for t in range(NT):
                for m, f in ((mka, NEG), (mk1, 0.0)):
                    link(g.affine_select(out=m[:, t, :], in_=m[:, t, :], compare_op=ALU.is_ge, fill=f,
                                         base=t * P - (CMP_BLOCK - 1), pattern=[[-CMP_STRIDE, NC_]], channel_multiplier=1))
            g.memset(mcol[:, 2:3], 0.0).then_inc(mask_ok, 1)
            for t in range(NT):
                rsqrt(6 + t, ssn[:, 24:48])
            rsqrt(8, mcol[0:60, 1:2])
            for hp in range(8):
                pool.wait_ge(s_fac, hp + 1)
                for i_ in range(2):
                    for t in range(NT):
                        for s in range(2):
                            n = 4 * i_ + 2 * t + s
                            v = Pb[:, hp % 2, i_, 256 * t + 128 * (t + 1) * s:256 * t + 128 * (t + 1) * (s + 1)]
                            g.tensor_scalar(v, v, fac[:, hp % 2, n:n + 1], None, ALU.mult).then_inc(s_scl, 1)
            rsqrt(9, rstd[:, 1, :])
            moe(1)
            rsqrt(10, rstd[:, 1, :])

        @block.scalar
        def _(act):
            own = [0]

            def link(i):
                own[0] += 1
                i.then_inc(c_act, 1)
                act.wait_ge(c_act, own[0])

            def norm(a, row):
                junk = xnT[:, :, :].rearrange("p k q -> p (k q)")
                if a == 0:
                    act.wait_ge(x_in, 16 * NT)
                else:
                    act.wait_ge(h_dve, H_DVE[a])
                    if H_ACT[a]:
                        act.wait_ge(h_act, H_ACT[a])
                for t in range(NT):
                    nc.scalar.activation(junk[:, t * D:(t + 1) * D], h[:, t, :], ACT.Square,
                                         accum_out=rstd[:, 0, t:t + 1]).then_inc(ssq_ok, 1)
                act.wait_ge(rs_ok, (1, 3, 4, 5, 9, 10)[a])
                nc.scalar.activation(hn[:, 1, :], h[:, 1, :], ACT.Copy, scale=rstd[:, 1, 1:2]).then_inc(hn_act, 1)
                if a == 0:
                    act.wait_ge(vec_ok, 3)
                for kp in (1, 3):
                    act.wait_ge(tr_ok, 4 * a + kp + 1)
                    for k in (2 * kp, 2 * kp + 1):
                        nc.scalar.activation(xnT[:, k, :], PS[:, 4 + kp, 256 * (k % 2):256 * (k % 2 + 1)], ACT.Copy,
                                             scale=vecT[:, row + k:row + k + 1]).then_inc(xt_act, 1)

            def fill(dst, src):
                act.dma_start(dst, src).then_inc(vec_in, 16)

            def fill2(dst, src):
                act.dma_start(dst, src, allow_slow_non_contiguous=True).then_inc(misc_in, 16)

            for r, v in ((ROW_MIX, g_mix[0]), (ROW_MIX + 8, g_mix[1]), (ROW_FFN, g_ffn[0]), (ROW_FFN + 8, g_ffn[1]),
                         (ROW_PLE, g_ple[0]), (ROW_PLE + 8, g_ple[1]), (ROW_BDW, conv_b_dw[0]),
                         (ROW_LNG, conv_ln_g[0]), (ROW_LNB, conv_ln_b[0])):
                fill(prow[r:r + 8, 0:P], v.rearrange("(r c) -> r c", c=P))
            fill(prow[ROW_BPW1:ROW_BPW1 + 16, 0:P], conv_b_pw1[0].rearrange("(r c) -> r c", c=P))
            for L in range(DEPTH):
                fill(prow[4 * L:4 * L + 4, P:P + 256], g_ffn[L].rearrange("(r c) -> r c", c=256))
            fill(wdw_rows, conv_w_dw[0])
            fill(bpw2, conv_b_pw2)
            for L in range(DEPTH):
                fill2(wr[:, L, :, 0:NG], moe_w_rg[L].rearrange("(k p) n -> p k n", p=P))
                fill2(wr[:, L, :, NG:], moe_w_re[L].rearrange("(k p) n -> p k n", p=P))
                fill2(rowb[0:1, 36 * L:36 * L + NG], moe_b_rg[L:L + 1, :])
                fill2(rowb[0:1, 36 * L + NG:36 * (L + 1)], moe_b_re[L:L + 1, :])
            for t in range(NT):
                fill2(posi[:, t:t + 1], positions[0:1, t * P:(t + 1) * P].rearrange("o q -> q o"))
            for g in range(NKV):
                fill2(posi[NC_ * g:NC_ * (g + 1), 2:3],
                      positions[0:1, CMP_BLOCK - 1:T:CMP_STRIDE].rearrange("o q -> q o"))

            norm(0, ROW_MIX)
            for c in range(KD):
                act.wait_ge(pw1_mm, c + 1)
                if c >= 2:
                    act.wait_ge(glu_ok, c - 1)
                nc.scalar.activation(sgm[c % 2], PS[:, c % 4, T:2 * T], ACT.Sigmoid,
                                     bias=vecT[:, ROW_BPW1 + 8 + c:ROW_BPW1 + 9 + c]).then_inc(sig_ok, 1)
            for c in range(KD):
                act.wait_ge(ln_c, c + 1)
                nc.scalar.activation(xnT[:, c, :], cT[:, c, :], ACT.Square).then_inc(ln_sq, 1)
            for c in range(KD):
                act.wait_ge(ln_r, c + 1)
                nc.scalar.activation(cT[:, c, :], cT[:, c, :], ACT.Silu, scale=vecT[:, ROW_LNG + c:ROW_LNG + c + 1],
                                     bias=vecT[:, ROW_LNB + c:ROW_LNB + c + 1]).then_inc(silu_ok, 1)

            def moe(L):
                a = 3 * L + 1
                norm(a, ROW_FFN + 8 * L)
                act.wait_ge(ptr, L + 1)
                nc.scalar.copy(pT2, PS[:, 5, :].rearrange("p (c q) -> p c q", c=2)).then_inc(pT_ok, 1)
                act.wait_ge(rt_d, 2 * L + 1)
                nc.scalar.activation(eg, dg, ACT.Exp).then_inc(rt_e, 1)
                for n in range(2):
                    for t in range(NT):
                        act.wait_ge(pp_mm, 4 * L + 2 * n + t + 1)
                        nc.scalar.copy(pp[:, t, 512 * n:512 * (n + 1)], PS[:, 2 * n + t, :]).then_inc(pp_ok, 1)
                act.wait_ge(rt_d, 2 * L + 2)
                nc.scalar.activation(sm[:, 4, :], sm[:, 3, :], ACT.Exp).then_inc(rt_e, 1)
                act.wait_ge(rt_row, L + 1)
                nc.scalar.copy(wrow, PS[:, 7, :].rearrange("p (a q) -> p a q", a=2)).then_inc(row_act, 1)
                act.wait_ge(tab_ok, L + 1)
                g0 = (NE + 1) * L
                act.wait_ge(ga_mm, g0 + 1)
                nc.scalar.copy(xg, PS[:, BGX, 0:Q4]).then_inc(xg_ok, 1)
                with act.Fori(0, NE // 2) as it:
                    for s in range(2):
                        n = it * 2 + (s + NE * L + 1)
                        gi = it * 2 + (s + g0 + 2)
                        act.wait_ge(gu_mm, n)
                        nc.scalar.activation(gs[64:128, :], PS[0:64, BGU, 0:256], ACT.Silu).then_inc(sil_ok, 1)
                        act.wait_ge(ga_mm, gi)
                        nc.scalar.copy(xg, PS[:, BGX, 0:Q4]).then_inc(xg_ok, 1)
                        act.wait_ge(y_mm, n)
                        nc.scalar.copy(ysb, PS[:, BY, 0:Q4]).then_inc(y_ok, 1)
                        e = it * 2 + s
                        more = act.value_load(tab[0:1, 0, bass.ds(e, 1)], min_val=0, max_val=7)
                        before = act.value_load(tab[0:1, 1, bass.ds(e, 1)], min_val=0, max_val=64)
                        with act.If(more > 0):
                            with act.Fori(0, more) as r:
                                c = before + r + 1
                                act.wait_ge(X["x_ga"], c)
                                nc.scalar.copy(xg, PS[:, BGX, 0:Q4]).then_inc(X["x_xg"], 1)
                                act.wait_ge(X["x_gu"], c)
                                nc.scalar.activation(gs[64:128, :], PS[0:64, BGU, 0:256], ACT.Silu).then_inc(X["x_sil"], 1)
                                act.wait_ge(X["x_y"], c)
                                nc.scalar.copy(ysb, PS[:, BY, 0:Q4]).then_inc(X["x_ysb"], 1)
                act.wait_ge(slot_free, NE * (L + 1))
                for j in (1, 3):
                    nc.scalar.copy(h[:, :, Q4 * j:Q4 * (j + 1)],
                                   PS[:, ACC + j, :].rearrange("p (t q) -> p t q", t=2)).then_inc(h_act, 1)
                norm(a + 1, ROW_PLE + 8 * L)
                for n in range(2):
                    for t in range(NT):
                        b = 2 * n + t
                        act.wait_ge(pl_mm, 4 * L + b + 1)
                        nc.scalar.activation(hn[:, t, 512 * n:512 * (n + 1)], PS[:, b, :], ACT.Sigmoid).then_inc(pl_sig, 1)

            moe(0)
            norm(3, ROW_MIX + 8)
            act.wait_ge(trig_ok, 1)
            nc.scalar.activation(trig, trig, ACT.Sin).then_inc(sin_ok, 1)
            act.wait_ge(trig_ok, 2)
            nc.scalar.activation(tcc[0:60, 0:64], tcc[0:60, 0:64], ACT.Sin).then_inc(sin_ok, 1)
            for u in range(2):
                act.wait_ge(xp_mm, u + 1)
                nc.scalar.copy(xp[:, :, :, u, :], PS[:, u, :].rearrange("p (s g e) -> p s g e", s=2, g=4)).then_inc(xp_ok, 1)
            for s in range(2):
                for t in range(NT):
                    act.wait_ge(kv_dve, 2 * s + t + 1)
                    nc.scalar.copy(vv[:, t, s, :], PS[:, 2 + 2 * s + t, 256:512]).then_inc(kv_act, 1)
            act.wait_ge(gate_mm, 1)
            nc.scalar.activation(gt, PS[:, 6, 0:128].rearrange("p (t c) -> p t c", t=2)[:, :, 0:48], ACT.Sigmoid).then_inc(gate_ok, 1)
            for n in range(2):
                for t in range(NT):
                    act.wait_ge(q_mm, 2 * n + t + 1)
                    nc.scalar.copy(raw[:, t, 8 * n:8 * n + 8, :],
                                   PS[:, 2 + 2 * n + t, :].rearrange("p (m e) -> p m e", m=8)).then_inc(c_act, 1)
                    own[0] += 1
            for t in range(NT):
                act.wait_ge(c_act, own[0])
                act.wait_ge(kv_dve, 4)
                if t == 1:
                    act.wait_ge(sq_used, 1)
                nc.scalar.activation(sq.rearrange("p (m e) -> p m e", m=24), raw[:, t, :, :], ACT.Square).then_inc(sq_ok, 1)
            for s in range(2):
                act.wait_ge(c1_x, s + 1)
                nc.scalar.activation(sq[0:60, 512:768], sq[0:60, 256:512], ACT.Sigmoid, scale=2.0 * float(np.sqrt(2.0 / np.pi))).then_inc(c1_s, 1)
                act.wait_ge(c1_t, s + 1)
                nc.scalar.copy(h1T[:, :, 0:60], PS[:, 0, 256:384].rearrange("p (c n) -> p c n", c=2)[:, :, 0:60]).then_inc(c1_T, 1)
            act.wait_ge(kc_mm, 2)
            act.wait_ge(const_ok, 1)
            for q in range(4):
                i = nc.scalar.copy(vcr[32 * q:32 * q + NC_, :, :], PS[32 * q:32 * q + NC_, 1, 256:512].rearrange("p (g e) -> p g e", g=4))
            i.then_inc(vcr_ok, 1)
            for b in (1, 3):
                act.wait_ge(qt_mm, b + 1)
                nc.scalar.copy(qT[:, 2 * b:2 * b + 2, :], PS[:, 2 + b, :].rearrange("p (k q) -> p k q", k=2)).then_inc(qt_act, 1)
            for b in (1, 3):
                act.wait_ge(qt_mm, 4 + b + 1)
                nc.scalar.copy(kT[:, b // 2, 2 * (b % 2):2 * (b % 2) + 2, :],
                               PS[:, 7 if b == 1 else 3, :].rearrange("p (k q) -> p k q", k=2)).then_inc(qt_act, 1)
            act.wait_ge(sc_d, 2)
            nc.scalar.activation(Pc[:, :, :, 0:NC_], Pc[:, :, :, 0:NC_], ACT.Exp, scale=SCALE).then_inc(sc_e, 1)

            def exps(hp):
                act.wait_ge(s_max, 8 * (hp + 1) + (hp + 1))
                if hp >= 2:
                    act.wait_ge(s_fac, hp - 1)
                for i_ in range(2):
                    for t in range(NT):
                        for s in range(2):
                            n = 4 * i_ + 2 * t + s
                            v = Pb[:, hp % 2, i_, 256 * t + 128 * (t + 1) * s:256 * t + 128 * (t + 1) * (s + 1)]
                            nc.scalar.activation(v, v, ACT.Exp, scale=SCALE, bias=nmx[:, hp % 2, n:n + 1],
                                                 accum_out=sme[:, hp % 2, n:n + 1]).then_inc(s_exp, 1)

            exps(0)
            for c in range(1):
                act.wait_ge(sct_mm, 1)
                nc.scalar.copy(PcT[:, 0:2, :], PS[:, 4, :].rearrange("p (k q) -> p k q", k=2)).then_inc(pct_ok, 1)
            for hp in range(8):
                if hp < 7:
                    exps(hp + 1)
                act.wait_ge(t_mm, 3 * hp + 3)
                if hp >= 2:
                    act.wait_ge(o_mm, hp - 1)
                nc.scalar.copy(pT[:, hp % 2, 1024:1536], PS[:, 6, :]).then_inc(pt_act, 1)
                act.wait_ge(o_mm, hp + 1)
                nc.scalar.copy(OT[:, hp, :], PS[:, 7, 0:256]).then_inc(o_ok, 1)
            moe(1)

        @block.vector
        def _(dve):
            v = nc.vector
            own = [0]

            def link(i):
                own[0] += 1
                i.then_inc(c_dve, 1)
                dve.wait_ge(c_dve, own[0])

            def bc(ap, dims):
                return ap.broadcast_to(dims)

            def norm(a, row):
                dve.wait_ge(ssq_ok, 2 * a + 2)
                v.tensor_scalar(rstd[:, 1, :], rstd[:, 0, :], 1.0 / D, EPS, ALU.mult, ALU.add).then_inc(var_ok, 1)
                dve.wait_ge(rs_ok, (1, 3, 4, 5, 9, 10)[a])
                v.tensor_scalar(hn[:, 0, :], h[:, 0, :], rstd[:, 1, 0:1], None, ALU.mult).then_inc(hn_dve, 1)
                if a == 0:
                    first_columns()
                for kp in (0, 2):
                    dve.wait_ge(tr_ok, 4 * a + kp + 1)
                    for k in (2 * kp, 2 * kp + 1):
                        v.tensor_scalar(xnT[:, k, :], PS[:, 4 + kp, 256 * (k % 2):256 * (k % 2 + 1)],
                                        vecT[:, row + k:row + k + 1], None, ALU.mult).then_inc(xt_dve, 1)

            def first_columns():
                dve.wait_ge(vtr, 1)
                v.tensor_copy(vecT[:, :], PS[:, 0, 0:NROWS]).then_inc(vec_ok, 1)
                dve.wait_ge(vtr, 2)
                v.tensor_copy(g8[:, :, :], PS[:, 1, 0:16].rearrange("p (c n) -> p c n", c=2)).then_inc(vec_ok, 1)
                dve.wait_ge(vtr, 3)
                v.tensor_copy(wdw, PS[:, 2, 0:8 * TAPS].rearrange("p (c w) -> p c w", c=8)).then_inc(vec_ok, 1)
                dve.wait_ge(vec_ok, 3)
                link(v.memset(cv0[:, :, 0:TAPS - 1], 0.0))

            dve.wait_ge(x_in, 16 * NT)
            norm(0, ROW_MIX)
            for c in range(KD):
                dve.wait_ge(sig_ok, c + 1)
                v.scalar_tensor_tensor(out=cv0[:, c, TAPS - 1:], in0=PS[:, c % 4, 0:T],
                                       scalar=vecT[:, ROW_BPW1 + c:ROW_BPW1 + c + 1], in1=sgm[c % 2],
                                       op0=ALU.add, op1=ALU.mult).then_inc(glu_ok, 1)
                dve.wait_ge(glu_ok, c + 1)
                if c == 0:
                    dve.wait_ge(tr_ok, 4)
                for w in range(TAPS):
                    o = cT[:, c, :] if w % 2 == 0 else accb[0]
                    u = cv0[:, c, w:w + T]
                    if w == 0:
                        i = v.tensor_scalar(o, u, wdw[:, c, w:w + 1], vecT[:, ROW_BDW + c:ROW_BDW + c + 1], ALU.mult, ALU.add)
                    elif w == 1:
                        i = v.tensor_scalar(o, u, wdw[:, c, w:w + 1], None, ALU.mult)
                    else:
                        i = v.scalar_tensor_tensor(out=o, in0=u, scalar=wdw[:, c, w:w + 1], in1=o, op0=ALU.mult, op1=ALU.add)
                    i.then_inc(c_dve, 1)
                    own[0] += 1
                    if w >= 1:
                        dve.wait_ge(c_dve, own[0] - 1)
                dve.wait_ge(c_dve, own[0])
                v.tensor_tensor(cT[:, c, :], cT[:, c, :], accb[0], ALU.add).then_inc(conv_ok, 1)
                dve.wait_ge(conv_ok, c + 1)
            dve.wait_ge(lnmm, 1)
            link(v.tensor_scalar(mu, PS[:, 4, 0:T], 1.0 / D, None, ALU.mult))
            for c in range(KD):
                v.tensor_tensor(cT[:, c, :], cT[:, c, :], mu, ALU.subtract).then_inc(ln_c, 1)
            dve.wait_ge(lnmm, 2)
            v.tensor_scalar(var, PS[:, 5, 0:T], 1.0 / D, EPS, ALU.mult, ALU.add).then_inc(var_ok, 1)
            dve.wait_ge(rs_ok, 2)
            dve.wait_ge(ln_c, KD)
            for c in range(KD):
                v.tensor_tensor(cT[:, c, :], cT[:, c, :], var, ALU.mult).then_inc(ln_r, 1)
            for n in range(2):
                for t in range(NT):
                    dve.wait_ge(pw2_mm, 2 * n + t + 1)
                    hs = h[:, t, 512 * n:512 * (n + 1)]
                    v.tensor_tensor(hs, PS[:, 2 * n + t, :], hs, ALU.add).then_inc(h_dve, 1)

            def first_of(vals, mx_, onehot, idx, n, d):
                link(v.tensor_reduce(mx_, vals, AX.X, ALU.max))
                link(v.tensor_tensor(d, vals, bc(mx_.unsqueeze(2), [P, 2, n]), ALU.subtract))
                link(v.tensor_scalar(onehot, d, 0.0, -BIGI, ALU.is_equal, ALU.mult))
                link(v.tensor_tensor(onehot, onehot, bc(iot[:, 0:n].unsqueeze(1), [P, 2, n]), ALU.add))
                link(v.tensor_reduce(idx, onehot, AX.X, ALU.min))
                link(v.tensor_tensor(onehot, onehot, bc(idx.unsqueeze(2), [P, 2, n]), ALU.is_equal))

            def xgT_copy(dst, L):
                gain = g8[:, :, 4 * L:4 * L + 4].rearrange("p c j -> p j c").unsqueeze(3)
                return v.tensor_tensor(dst.rearrange("p (j c) s -> p j c s", c=2),
                                       PS[:, BGX, Q4:Q4 + 256].rearrange("p (c j s) -> p j c s", c=2, j=4),
                                       bc(gain, [P, 4, 2, SLOTS]), ALU.mult)

            def hmul():
                return v.tensor_tensor(hh[64:128, :], PS[64:128, BGU, 0:256], gs[64:128, :], ALU.mult)

            def hT_copy():
                return v.tensor_copy(hT, PS[:, BHT, 0:128].rearrange("p (c s) -> p c s", c=2))

            def moe(L):
                a = 3 * L + 1
                norm(a, ROW_FFN + 8 * L)
                dve.wait_ge(rt_mm, L + 1)
                link(v.tensor_copy(R, PS[:, BGU, 0:128].rearrange("p (t e) -> p t e", t=2)[:, :, 0:36]))
                lg, le = R[:, :, 0:NG], R[:, :, NG:]
                link(v.tensor_reduce(sm[:, 0, :], lg, AX.X, ALU.max))
                v.tensor_tensor(dg, lg, bc(sm[:, 0, :].unsqueeze(2), [P, 2, NG]), ALU.subtract).then_inc(rt_d, 1)
                dve.wait_ge(rt_d, 2 * L + 1)
                link(v.tensor_scalar(og, dg, 0.0, -BIGI, ALU.is_equal, ALU.mult))
                link(v.tensor_tensor(og, og, bc(iot[:, 0:NG].unsqueeze(1), [P, 2, NG]), ALU.add))
                link(v.tensor_reduce(sm[:, 1, :], og, AX.X, ALU.min))
                link(v.tensor_tensor(og, og, bc(sm[:, 1, :].unsqueeze(2), [P, 2, NG]), ALU.is_equal))
                link(v.tensor_scalar(cg, og, -1.0, -NEG, ALU.add, ALU.mult))
                for t in range(NT):
                    grp = [P, NG, NEG_E]
                    link(v.tensor_tensor(lm[:, t, :].rearrange("p (g e) -> p g e", g=NG), le[:, t, :].rearrange("p (g e) -> p g e", g=NG),
                                         bc(og[:, t, :].unsqueeze(2), grp), ALU.mult))
                    link(v.tensor_tensor(lm[:, t, :].rearrange("p (g e) -> p g e", g=NG), lm[:, t, :].rearrange("p (g e) -> p g e", g=NG),
                                         bc(cg[:, t, :].unsqueeze(2), grp), ALU.add))
                first_of(lm, sm[:, 2, :], O1, sm[:, 5, :], NE, dd)
                link(v.scalar_tensor_tensor(out=lm, in0=O1, scalar=NEG, in1=lm, op0=ALU.mult, op1=ALU.add))
                first_of(lm, sm[:, 6, :], O2, sm[:, 7, :], NE, dd)
                v.tensor_tensor(Cc, O1, O2, ALU.add).then_inc(rt_c, 1)
                v.tensor_tensor(sm[:, 3, :], sm[:, 6, :], sm[:, 2, :], ALU.subtract).then_inc(rt_d, 1)
                dve.wait_ge(rt_e, 2 * L + 2)
                link(v.tensor_reduce(sm[:, 8, :], eg, AX.X, ALU.add))
                link(v.tensor_scalar(sm[:, 9, :], sm[:, 4, :], 1.0, None, ALU.add))
                link(v.tensor_tensor(sm[:, 8, :], sm[:, 8, :], sm[:, 9, :], ALU.mult))
                link(v.reciprocal(W4[:, :, 0], sm[:, 8, :]))
                link(v.tensor_tensor(W4[:, :, 1], W4[:, :, 0], sm[:, 4, :], ALU.mult))
                dve.wait_ge(rt_pf, L + 1)
                dve.wait_ge(rt_c, L + 1)
                pf = PS[:, 6, 0:64].rearrange("p (t e) -> p t e", t=2)
                for s, (O, ix) in enumerate(((O1, 5), (O2, 7))):
                    link(v.tensor_tensor(dd, pf, O, ALU.mult))
                    link(v.tensor_reduce(sm[:, 10, :], dd, AX.X, ALU.add))
                    link(v.tensor_scalar(sm[:, 11, :], sm[:, ix, :], BIGI, 256.0, ALU.add, ALU.mult))
                    link(v.tensor_tensor(S4[:, :, s], sm[:, 11, :], sm[:, 10, :], ALU.add))
                v.tensor_copy(cnt, PS[:, 6, 64:96]).then_inc(rt_s, 1)
                dve.wait_ge(rt_s, L + 1)
                link(v.tensor_scalar(ext, cnt, float(SLOTS), None, ALU.is_gt))
                for m in range(2, T // SLOTS):
                    link(v.scalar_tensor_tensor(out=ext, in0=cnt, scalar=float(SLOTS * m), in1=ext, op0=ALU.is_gt, op1=ALU.add))
                link(v.tensor_copy(scn[:, 0, :], ext))
                b = 0
                for sh in (1, 2, 4, 8, 16):
                    link(v.tensor_copy(scn[:, 1 - b, 0:sh], scn[:, b, 0:sh]))
                    link(v.tensor_tensor(scn[:, 1 - b, sh:], scn[:, b, sh:], scn[:, b, 0:NE - sh], ALU.add))
                    b = 1 - b
                if L == 0:
                    link(v.tensor_copy(xtot[:, :], scn[:, b, NE - 1:NE]))
                else:
                    link(v.tensor_scalar(scn[:, b, :], scn[:, b, :], xtot[:, 0:1], None, ALU.add))
                link(v.tensor_tensor(scn[:, b, :], scn[:, b, :], ext, ALU.subtract))
                link(v.tensor_copy(tab[:, 0, :], ext))
                v.tensor_copy(tab[:, 1, :], scn[:, b, :]).then_inc(tab_ok, 1)
                dve.wait_ge(rt_row, L + 1)
                v.tensor_copy(srow, PS[:, 5, :].rearrange("p (a q) -> p a q", a=2)).then_inc(row_dve, 1)
                dve.wait_ge(tab_ok, L + 1)
                g0 = (NE + 1) * L
                dve.wait_ge(xt_mm, g0 + 1)
                xgT_copy(xgT, L).then_inc(xgT_ok, 1)
                with dve.Fori(0, NE // 2) as it:
                    for s in range(2):
                        n = it * 2 + (s + NE * L + 1)
                        gi = it * 2 + (s + g0 + 2)
                        dve.wait_ge(sil_ok, n)
                        hmul().then_inc(h_ok, 1)
                        dve.wait_ge(ht_mm, n)
                        hT_copy().then_inc(hT_ok, 1)
                        dve.wait_ge(xt_mm, gi)
                        xgT_copy(xgT, L).then_inc(xgT_ok, 1)
                        e = it * 2 + s
                        more = dve.value_load(tab[0:1, 0, bass.ds(e, 1)], min_val=0, max_val=7)
                        before = dve.value_load(tab[0:1, 1, bass.ds(e, 1)], min_val=0, max_val=64)
                        with dve.If(more > 0):
                            with dve.Fori(0, more) as r:
                                c = before + r + 1
                                dve.wait_ge(X["x_xt"], c)
                                xgT_copy(xxgT, L).then_inc(X["x_xgT"], 1)
                                dve.wait_ge(X["x_sil"], c)
                                hmul().then_inc(X["x_h"], 1)
                                dve.wait_ge(X["x_ht"], c)
                                hT_copy().then_inc(X["x_hT"], 1)
                dve.wait_ge(slot_free, NE * (L + 1))
                for j in (0, 2):
                    v.tensor_copy(h[:, :, Q4 * j:Q4 * (j + 1)],
                                  PS[:, ACC + j, :].rearrange("p (t q) -> p t q", t=2)).then_inc(h_dve, 1)
                norm(a + 1, ROW_PLE + 8 * L)
                for n in range(2):
                    for t in range(NT):
                        b = 2 * n + t
                        dve.wait_ge(pl_sig, 4 * L + b + 1)
                        if b == 0:
                            dve.wait_ge(pp_ok, 4 * (L + 1))
                        gsl = hn[:, t, 512 * n:512 * (n + 1)]
                        hs = h[:, t, 512 * n:512 * (n + 1)]
                        v.tensor_tensor(gsl, gsl, pp[:, t, 512 * n:512 * (n + 1)], ALU.mult).then_inc(pl_mul, 1)
                        dve.wait_ge(pl_mul, 4 * L + b + 1)
                        v.tensor_tensor(hs, hs, gsl, ALU.add).then_inc(h_dve, 1)

            moe(0)

            def angles(dst, tmp, tmp2, pos, rows):
                for f, (quarter, shift) in enumerate(((0.25, float(np.pi / 2)), (0.0, 0.0))):
                    link(v.tensor_scalar(tmp[:, f], invb[0:rows, :], pos, None, ALU.mult))
                    link(v.tensor_scalar(tmp2[:, f], tmp[:, f], float(1 / (2 * np.pi)), quarter, ALU.mult, ALU.add))
                    link(v.tensor_scalar(tmp2[:, f], tmp2[:, f], MAGIC, None, ALU.add))
                    link(v.tensor_scalar(tmp2[:, f], tmp2[:, f], MAGIC, None, ALU.subtract))
                    for part in TWO_PI:
                        link(v.scalar_tensor_tensor(out=tmp[:, f], in0=tmp2[:, f], scalar=-part, in1=tmp[:, f], op0=ALU.mult, op1=ALU.add))
                    link(v.tensor_scalar(tmp[:, f], tmp[:, f], shift, PI_LO, ALU.add, ALU.min))
                    link(v.tensor_scalar(dst[:, f], tmp[:, f], -PI_LO, None, ALU.max))

            def gain_tables(dst, tr, gains, rows):
                link(v.tensor_tensor(dst[:, 0, 0:32], tr[:, 0], gains[:, 0:32], ALU.mult))
                link(v.tensor_tensor(dst[:, 0, 32:64], tr[:, 0], gains[:, 32:64], ALU.mult))
                link(v.scalar_tensor_tensor(out=dst[:, 1, 0:32], in0=tr[:, 1], scalar=-1.0, in1=gains[:, 32:64], op0=ALU.mult, op1=ALU.mult))
                link(v.tensor_tensor(dst[:, 1, 32:64], tr[:, 1], gains[:, 0:32], ALU.mult))

            dve.wait_ge(misc_in, 16 * N_MISC)
            dve.wait_ge(att_in, 16 * N_ATT)
            link(v.tensor_copy(posf[:, 0:2], posi[:, 0:2]))
            for t in range(NT):
                angles(trig[:, t], trk[:, t], trg[:, t], posf[:, t:t + 1], P)
            v.tensor_copy(posf[0:60, 2:3], posi[0:60, 2:3]).then_inc(trig_ok, 1)
            dve.wait_ge(trig_ok, 1)
            tc2 = tcc[0:60, 0:64].rearrange("p (f e) -> p f e", f=2)
            angles(tc2, trk[0:60, 0], trg[0:60, 0], posf[0:60, 2:3], 60)
            v.tensor_copy(posf[0:60, 3:4], posf[0:60, 2:3]).then_inc(trig_ok, 1)
            norm(3, ROW_MIX + 8)
            dve.wait_ge(sin_ok, 2)
            for t in range(NT):
                for m in range(3):
                    gain_tables(tcos[:, t, :, m, :], trig[:, t], gn[:, m, :], P)
            ktab = tcc[0:60, 64:192].rearrange("p (f e) -> p f e", f=2)
            gain_tables(ktab, tc2, gn[0:60, 3, :], 60)
            for s in range(2):
                for t in range(NT):
                    dve.wait_ge(kv_mm, 2 * s + t + 1)
                    v.tensor_copy(raw[:, t, 16 + 4 * s:20 + 4 * s, :],
                                  PS[:, 2 + 2 * s + t, 0:256].rearrange("p (m e) -> p m e", m=4)).then_inc(kv_dve, 1)
            dve.wait_ge(xpt_mm, 3)
            link(v.tensor_copy(peT, PS[:, 7, 0:32].rearrange("p (s j) -> p s j", s=2)))
            for s in range(2):
                v.tensor_copy(xpT[:, s, :, :], PS[:, s, :].rearrange("p (g m) -> p g m", g=4)).then_inc(xpt_ok, 1)
                dve.wait_ge(xpt_ok, s + 1)
                for b in range(2):
                    x3 = xpT[:, s, :, 8 * b:8 * b + 8 * NC_].rearrange("p g (n j) -> p j g n", j=8)
                    i = v.tensor_tensor(Bc[:, s, 8 * b:8 * b + 8, :, :], x3,
                                        bc(peT[:, s, 8 * b:8 * b + 8].unsqueeze(2).unsqueeze(3), [P, 8, NKV, NC_]), ALU.add)
                i.then_inc(B_ok, 1)

            for t in range(NT):
                dve.wait_ge(sq_ok, t + 1)
                v.tensor_reduce(ssn[:, 0:24], sq.rearrange("p (m e) -> p m e", m=24), AX.X, ALU.add).then_inc(sq_used, 1)
                dve.wait_ge(sq_used, t + 1)
                v.tensor_scalar(ssn[:, 24:48], ssn[:, 0:24], 1.0 / DH, EPS, ALU.mult, ALU.add).then_inc(var_ok, 1)
                dve.wait_ge(rs_ok, 6 + t)
                link(v.tensor_tensor(raw[:, t, :, :], raw[:, t, :, :], bc(ssn[:, 24:48].unsqueeze(2), [P, 24, 64]), ALU.mult))
                for m, (lo, n) in enumerate(((0, 16), (16, 4), (20, 4))):
                    x_ = raw[:, t, lo:lo + n, :]
                    tA = bc(tcos[:, t, 0, m, :].unsqueeze(1), [P, n, 64])
                    dst = rotq[:, t, :, :] if m == 0 else rotk[:, t, 4 * (m - 1):4 * m, 0, :]
                    tmp = rot_tmp[:, 0:64 * n].rearrange("p (m e) -> p m e", m=n)
                    link(v.tensor_tensor(dst, x_, tA, ALU.mult))
                    for f in range(2):
                        link(v.tensor_tensor(tmp[:, :, 32 * f:32 * f + 32], x_[:, :, 32 * (1 - f):32 * (1 - f) + 32],
                                             bc(tcos[:, t, 1, m, 32 * f:32 * f + 32].unsqueeze(1), [P, n, 32]), ALU.mult))
                    if m > 0:
                        link(v.tensor_tensor(rotk[:, t, 4 * (m - 1):4 * m, 1, :], dst, tmp, ALU.add))
                    v.tensor_tensor(dst, dst, tmp, ALU.add).then_inc(rot_ok, 1)
                    dve.wait_ge(rot_ok, 3 * t + m + 1)

            for s in range(2):
                dve.wait_ge(c1_mm, s + 1)
                xx, t1, sg = sq[0:60, 0:256], sq[0:60, 256:512], sq[0:60, 512:768]
                link(v.tensor_copy(xx, PS[0:60, s, 0:256]))
                link(v.tensor_tensor(t1, xx, xx, ALU.mult))
                link(v.tensor_scalar(t1, t1, 0.044715, 1.0, ALU.mult, ALU.add))
                v.tensor_tensor(t1, t1, xx, ALU.mult).then_inc(c1_x, 1)
                dve.wait_ge(c1_s, s + 1)
                v.tensor_tensor(h1v[s][0:60, :], xx, sg, ALU.mult).then_inc(c1_g, 1)
                if s == 0:
                    dve.wait_ge(kc_mm, 1)
                    link(v.tensor_copy(kcx[0:60, 0, :], PS[0:60, 0, 0:64]))
                    v.tensor_copy(kcx[0:60, 1, :], kcx[0:60, 0, :]).then_inc(kc_x, 1)
                    dve.wait_ge(kc_x, 1)
                    link(v.tensor_tensor(kcx[0:60, 1, :], kcx[0:60, 0, :], kcx[0:60, 0, :], ALU.mult))
                    link(v.tensor_reduce(mcol[0:60, 0:1], kcx[0:60, 1, :], AX.X, ALU.add))
                    v.tensor_scalar(mcol[0:60, 1:2], mcol[0:60, 0:1], 1.0 / DH, EPS, ALU.mult, ALU.add).then_inc(var_ok, 1)
                    dve.wait_ge(rs_ok, 8)
                    link(v.tensor_scalar(kcx[0:60, 0, :], kcx[0:60, 0, :], mcol[0:60, 1:2], None, ALU.mult))
                    link(v.tensor_tensor(kcx[0:60, 2, :], kcx[0:60, 0, :], ktab[:, 0, :], ALU.mult))
                    for f in range(2):
                        link(v.tensor_tensor(kcx[0:60, 1, 32 * f:32 * f + 32], kcx[0:60, 0, 32 * (1 - f):32 * (1 - f) + 32],
                                             ktab[:, 1, 32 * f:32 * f + 32], ALU.mult))
                    link(v.tensor_tensor(kcx[0:60, 3, :], kcx[0:60, 2, :], kcx[0:60, 1, :], ALU.add))
                    v.tensor_tensor(kcx[0:60, 2, :], kcx[0:60, 2, :], kcx[0:60, 1, :], ALU.add).then_inc(kc_x, 1)
                    dve.wait_ge(kc_x, 2)
            for b in (0, 2):
                dve.wait_ge(qt_mm, b + 1)
                v.tensor_copy(qT[:, 2 * b:2 * b + 2, :], PS[:, 2 + b, :].rearrange("p (k q) -> p k q", k=2)).then_inc(qt_dve, 1)
            for b in (0, 2):
                dve.wait_ge(qt_mm, 4 + b + 1)
                v.tensor_copy(kT[:, b // 2, 2 * (b % 2):2 * (b % 2) + 2, :],
                              PS[:, 6 if b == 0 else 2, :].rearrange("p (k q) -> p k q", k=2)).then_inc(qt_dve, 1)
            dve.wait_ge(kct_mm, 1)
            v.tensor_copy(kcT, PS[:, 0, 384:444]).then_inc(kcT_ok, 1)
            dve.wait_ge(sc_mm, 1)
            dve.wait_ge(mask_ok, 1)
            link(v.memset(Pc[:, :, :, NC_:], 0.0))
            for i_ in range(2):
                for t in range(NT):
                    i = v.tensor_tensor(Pc[:, t, i_::2, 0:NC_], PS[:, i_, 128 * t:128 * (t + 1)].rearrange("p (m n) -> p m n", m=8)[:, :, 0:NC_],
                                        bc(mka[:, t, :].unsqueeze(1), [P, 8, NC_]), ALU.add)
            i.then_inc(sc_d, 1)
            dve.wait_ge(sc_d, 1)
            pc3 = Pc.rearrange("p t n e -> p (t n) e")[:, :, 0:NC_]
            link(v.tensor_reduce(cst[:, 0, :], pc3, AX.X, ALU.max))
            v.tensor_tensor(pc3, pc3, bc(cst[:, 0, :].unsqueeze(2), [P, 32, NC_]), ALU.subtract).then_inc(sc_d, 1)

            def maxes(hp):
                dve.wait_ge(s_mm, hp + 1)
                if hp >= 2:
                    dve.wait_ge(t_mm, 3 * (hp - 1))
                for i_ in range(2):
                    for t in range(NT):
                        for s in range(2):
                            n = 4 * i_ + 2 * t + s
                            w = 128 * (t + 1)
                            mk = cmask[:, 1, :] if t == 0 else cmask[:, :, :].rearrange("p a b -> p (a b)")
                            v.tensor_tensor_reduce(Pb[:, hp % 2, i_, 256 * t + w * s:256 * t + w * (s + 1)],
                                                   PS[:, 2 * t + i_, w * s:w * (s + 1)], mk, 1.0, NEG, ALU.add, ALU.max,
                                                   mx[:, hp % 2, n:n + 1]).then_inc(s_max, 1)
                dve.wait_ge(s_max, 9 * hp + 8)
                v.tensor_scalar(nmx[:, hp % 2, :], mx[:, hp % 2, :], -SCALE, None, ALU.mult).then_inc(s_max, 1)

            def factors(hp):
                dve.wait_ge(s_exp, 8 * (hp + 1))
                if hp == 0:
                    dve.wait_ge(gate_ok, 1)
                link(v.reciprocal(sme[:, hp % 2, :], sme[:, hp % 2, :]))
                for i_ in range(2):
                    hd = 2 * hp + i_
                    i = v.tensor_tensor(fac[:, hp % 2, 4 * i_:4 * i_ + 4].rearrange("p (t s) -> p t s", t=2),
                                        sme[:, hp % 2, 4 * i_:4 * i_ + 4].rearrange("p (t s) -> p t s", t=2),
                                        gt[:, :, 3 * hd + 1:3 * hd + 3], ALU.mult)
                i.then_inc(s_fac, 1)

            maxes(0)
            dve.wait_ge(sc_e, 1)
            link(v.tensor_reduce(cst[:, 1, :], pc3, AX.X, ALU.add))
            link(v.reciprocal(cst[:, 2, :], cst[:, 1, :]))
            dve.wait_ge(gate_ok, 1)
            link(v.tensor_tensor(cst[:, 2, :].rearrange("p (t n) -> p t n", t=2), cst[:, 2, :].rearrange("p (t n) -> p t n", t=2),
                                 gt.rearrange("p t (n b) -> p t n b", b=3)[:, :, :, 0], ALU.mult))
            link(v.tensor_tensor(pc3, pc3, bc(cst[:, 2, :].unsqueeze(2), [P, 32, NC_]), ALU.mult))
            v.tensor_tensor(Pc[:, :, :, 0:NC_], Pc[:, :, :, 0:NC_], bc(mk1.unsqueeze(2), [P, 2, 16, NC_]), ALU.mult).then_inc(sc_p, 1)
            factors(0)
            dve.wait_ge(sct_mm, 1)
            v.tensor_copy(PcT[:, 2:4, :], PS[:, 5, :].rearrange("p (k q) -> p k q", k=2)).then_inc(pct_ok, 1)
            for hp in range(8):
                if hp < 7:
                    maxes(hp + 1)
                dve.wait_ge(t_mm, 3 * hp + 2)
                if hp >= 2:
                    dve.wait_ge(o_mm, hp - 1)
                for b in range(2):
                    v.tensor_copy(pT[:, hp % 2, 512 * b:512 * (b + 1)], PS[:, 4 + b, :]).then_inc(pt_dve, 1)
                if hp < 7:
                    factors(hp + 1)
            for n in range(2):
                for t in range(NT):
                    dve.wait_ge(wo_mm, 2 * n + t + 1)
                    hs = h[:, t, 512 * n:512 * (n + 1)]
                    v.tensor_tensor(hs, PS[:, 2 * n + t, :], hs, ALU.add).then_inc(h_dve, 1)
            moe(1)


_INS = ['x', 'p', 'positions', 'g_mix', 'g_ffn', 'g_ple', 'conv_w_pw1', 'conv_b_pw1', 'conv_w_dw', 'conv_b_dw',
        'conv_ln_g', 'conv_ln_b', 'conv_w_pw2', 'conv_b_pw2', 'nsa_w_in', 'nsa_q_norm', 'nsa_k_norm',
        'nsa_cmp_pe', 'nsa_cmp_w1', 'nsa_cmp_w2', 'nsa_w_out', 'moe_w_rg', 'moe_b_rg', 'moe_w_re', 'moe_b_re',
        'moe_w_gate', 'moe_w_up', 'moe_w_down', 'ple_w_proj', 'ple_w_gate']


def kernel(**inputs):
    import numpy as _np
    import concourse.bacc as _bacc
    from concourse import mybir as _mybir
    from concourse.bass_utils import run_bass_kernel_spmd as _run

    nc = _bacc.Bacc("TRN2", target_bir_lowering=False, num_devices=1)
    arrays, args = {}, []
    given = {name: _np.ascontiguousarray(inputs[name]) for name in _INS}
    half = DH // 2
    given["inv_freq"] = (1.0 / (ROPE_THETA ** (_np.arange(half, dtype=_np.float32) / half))).astype(_np.float32)[None, :]
    for name, a in given.items():
        arrays[f"in_{name}"] = a
        args.append(nc.dram_tensor(f"in_{name}", a.shape, _mybir.dt.from_np(a.dtype), kind="ExternalInput").ap())
    args.append(nc.dram_tensor("out_h", (1, T, D), F32, kind="ExternalOutput").ap())
    build(nc, *args)
    return _run(nc, [arrays], core_ids=[0]).results[0]["out_h"]
```

```python
from contextlib import ExitStack

import numpy as np

import concourse.bass as bass
from concourse import mybir

ALU = mybir.AluOpType
ACT = mybir.ActivationFunctionType
F32 = mybir.dt.float32
I32 = mybir.dt.int32
AX = mybir.AxisListType

P = 128
DEPTH = 2
D = 1024
T = 256
NT = T // P
KD = D // P
TAPS = 31
HEADS, DH, NKV = 16, 64, 4
CMP_STRIDE, CMP_BLOCK, CMP_HID = 16, 32, 256
NC_ = T // CMP_STRIDE - 1
NG, NE, NEG_E = 4, 32, 8
F = 512
SLOTS = 32
Q4 = D // 4
EPS = 1e-6
NEG = -1e30
BIGI = 1000.0
MAGIC = 12582912.0
TWO_PI = (6.28125, 1.9350051879882812e-3, 3.0199159819567e-7)
PI_LO = 3.1415925
PW1_PARTS = ((0, 1), (1, 2), (2, 4), (4, 8))
PE_TAPS, POOL_TAPS = 5, 6
N_VEC, N_MISC, N_ATT = 10, 8 + 6, 8
SCALE = DH ** -0.5
ROPE_THETA = 10000.0

ACC = 0
BGU, BGX, BHT, BY = 4, 5, 6, 7

H_DVE = [0, 4, 6, 10, 14, 16, 20]
H_ACT = [0, 0, 2, 2, 2, 4, 4]
ROW_MIX, ROW_FFN, ROW_PLE, ROW_BPW1, ROW_BDW, ROW_LNG, ROW_LNB, NROWS = 0, 16, 32, 48, 64, 72, 80, 88


def build(nc, x, p, positions, g_mix, g_ffn, g_ple, conv_w_pw1, conv_b_pw1, conv_w_dw, conv_b_dw,
          conv_ln_g, conv_ln_b, conv_w_pw2, conv_b_pw2, nsa_w_in, nsa_q_norm, nsa_k_norm,
          nsa_cmp_pe, nsa_cmp_w1, nsa_cmp_w2, nsa_w_out, moe_w_rg, moe_b_rg, moe_w_re, moe_b_re,
          moe_w_gate, moe_w_up, moe_w_down, ple_w_proj, ple_w_gate, inv_freq, out):
    with ExitStack() as ctx:
        def sb(name, shape, dt=F32):
            return ctx.enter_context(nc.sbuf_tensor(name, shape, dt))

        def sem(name):
            return ctx.enter_context(nc.semaphore(name))

        PS = ctx.enter_context(nc.psum_tensor("PS", [P, 8, 512], F32))

        ring = sb("ring", [P, 2, 12288])
        wb = sb("wb", [P, 3, 4096])
        h = sb("h", [P, NT, D])
        hn = sb("hn", [P, NT, D])
        xnT = sb("xnT", [P, KD, T])
        ppw = sb("ppw", [P, 4096])
        ident = sb("ident", [P, P])
        ones = sb("ones", [P, P])
        upper = sb("upper", [P, P])
        cmask = sb("cmask", [P, 2, P])
        vecT = sb("vecT", [P, NROWS])
        g8 = sb("g8", [P, 2, 8])
        wr = sb("wr", [P, DEPTH, KD, NG + NE])
        rowb = sb("rowb", [1, DEPTH * (NG + NE)])
        rstd = sb("rstd", [P, 2, NT])
        iot = sb("iot", [P, 32])
        ioti = sb("ioti", [P, 32], I32)
        nhalf = sb("nhalf", [P, 1])
        colp = sb("colp", [P, 1])
        xtot = sb("xtot", [P, 1])
        tab = sb("tab", [P, 2, NE], I32)
        A = sb("arena", [P, 4480])

        off = [0]

        def carve(n):
            a = off[0]
            off[0] += n
            assert off[0] <= 4480, off[0]
            return A[:, a:a + n]

        srow = carve(512).rearrange("p (a t) -> p a t", a=2)
        wrow = carve(512).rearrange("p (a t) -> p a t", a=2)
        eqr = carve(512).rearrange("p (a t) -> p a t", a=2)
        wT = [carve(256) for _ in range(2)]
        eq4 = carve(128).rearrange("p (t a s) -> p t a s", t=2, a=2)
        sel = [carve(64).rearrange("p (t s) -> p t s", t=2) for _ in range(2)]
        cur32 = carve(32)
        curc = carve(1)
        xcur32 = carve(32)
        xcurc = carve(1)
        xg = carve(256)
        xgT = carve(256).rearrange("p (k s) -> p k s", k=8)
        xfree = [off[0], 0]
        xsel = carve(64).rearrange("p (t s) -> p t s", t=2)
        xwT = carve(256)
        xxgT = carve(256).rearrange("p (k s) -> p k s", k=8)
        xfree[1] = off[0]
        gs = carve(256)
        hh = carve(256)
        hT = carve(128).rearrange("p (c s) -> p c s", c=2)
        ysb = carve(256)
        S4 = carve(4).rearrange("p (t a) -> p t a", t=2)
        W4 = carve(4).rearrange("p (t a) -> p t a", t=2)
        scn = carve(64).rearrange("p (n e) -> p n e", n=2)
        rt_mem, rt_off = A[:, xfree[0]:xfree[1]], [0]

        def rt(n):
            rt_off[0] += n
            assert rt_off[0] <= xfree[1] - xfree[0]
            return rt_mem[:, rt_off[0] - n:rt_off[0]]

        R = rt(72).rearrange("p (t e) -> p t e", t=2)
        dg = rt(8).rearrange("p (t e) -> p t e", t=2)
        eg = rt(8).rearrange("p (t e) -> p t e", t=2)
        cg = rt(8).rearrange("p (t e) -> p t e", t=2)
        og = rt(8).rearrange("p (t e) -> p t e", t=2)
        lm = rt(64).rearrange("p (t e) -> p t e", t=2)
        dd = rt(64).rearrange("p (t e) -> p t e", t=2)
        O1 = rt(64).rearrange("p (t e) -> p t e", t=2)
        O2 = rt(64).rearrange("p (t e) -> p t e", t=2)
        Cc = rt(64).rearrange("p (t e) -> p t e", t=2)
        cnt = rt(32)
        ext = rt(32)
        sm = rt(32).rearrange("p (n t) -> p n t", t=2)

        off[0] = 0
        sq = ppw[:, 0:1536]
        wgate3 = ppw[:, 1536:1920].rearrange("p (k c) -> p k c", k=KD)
        rot_tmp = ppw[:, 2048:3072]
        tcos = ppw[:, 3072:3840].rearrange("p (t f m e) -> p t f m e", t=2, f=2, m=3)
        gn = ppw[:, 3840:4096].rearrange("p (m e) -> p m e", m=4)
        invb = carve(DH // 2)
        trig = carve(128).rearrange("p (t f e) -> p t f e", t=2, f=2)
        trk = carve(128).rearrange("p (t f e) -> p t f e", t=2, f=2)
        trg = carve(128).rearrange("p (t f e) -> p t f e", t=2, f=2)
        posf = carve(4)
        gt = carve(96).rearrange("p (t c) -> p t c", t=2)
        ssn = carve(48)
        mx = carve(2 * 8).rearrange("p (b n) -> p b n", b=2)
        nmx = carve(2 * 8).rearrange("p (b n) -> p b n", b=2)
        sme = carve(2 * 8).rearrange("p (b n) -> p b n", b=2)
        fac = carve(2 * 8).rearrange("p (b n) -> p b n", b=2)
        cst = carve(32 * 3).rearrange("p (n m) -> p n m", n=3)
        mka = carve(2 * NC_).rearrange("p (t n) -> p t n", t=2)
        mk1 = carve(2 * NC_).rearrange("p (t n) -> p t n", t=2)
        pei = carve(256).rearrange("p (s c) -> p s c", s=2)
        peT = carve(32).rearrange("p (s j) -> p s j", s=2)
        kcT = carve(60)
        h1v = [sq[:, 768:1024], sq[:, 1024:1280]]
        vcr = carve(256).rearrange("p (g e) -> p g e", g=4)
        w2c = carve(256).rearrange("p (s c e) -> p s c e", s=2, c=2)
        h1T = carve(2 * 128).rearrange("p (c n) -> p c n", c=2)
        kcx = carve(64 * 4).rearrange("p (n e) -> p n e", n=4)
        tcc = carve(128 + 64 * 3)
        mcol = carve(8)
        off[0] = 0
        sgm = [carve(256) for _ in range(2)]
        mu = carve(256)
        var = carve(256)
        wdw = carve(8 * TAPS).rearrange("p (c w) -> p c w", c=8)
        accb = [carve(256) for _ in range(2)]
        prow = carve(384)
        dgb = carve(2 * PE_TAPS * P).rearrange("p (b i q) -> p b i q", b=2, i=PE_TAPS)
        pac = [ppw[:, 2304:2560], ppw[:, 2560:2816]]
        ptm = ppw[:, 2816:3072]
        bpw2 = carve(1024)[0:1, :]
        wdw_rows = ppw[0:TAPS, 3072:4096]

        posi = sb("posi", [P, 4], I32)
        pp = ppw[:, 0:2048].rearrange("p (t d) -> p t d", t=NT)
        wproj = ppw[:, 2048:4096].rearrange("p (c d) -> p c d", c=2)
        pin = ppw[:, 0:512].rearrange("p (t d) -> p t d", t=NT)
        pT2 = eqr

        def w_gu(s):
            return ring[:, s, 0:8192].rearrange("p (g k f) -> p g k f", g=2, k=8)

        def w_dn(s):
            return ring[:, s, 8192:12288].rearrange("p (f c d) -> p f c d", f=2, c=2)

        def dense(buf):
            return buf.rearrange("p (k n) -> p k n", k=KD)

        WB = [wb[:, i, :] for i in range(3)]
        R0 = [ring[:, 0, 4096 * i:4096 * (i + 1)] for i in range(3)]
        R1 = [ring[:, 1, 4096 * i:4096 * (i + 1)] for i in range(3)]
        PW1 = [WB[0], WB[1], WB[2], R1[0]]
        PW2 = [R1[1], R1[2]]
        cv0 = ppw[:, 0:KD * (T + TAPS - 1)].rearrange("p (k q) -> p k q", k=KD)
        cT = hn[:, :, :].rearrange("p t (k q) -> p (t k) q", q=T)

        S = ring[:, 1, :]
        raw = S[:, 0:3072].rearrange("p (t n e) -> p t n e", t=2, n=24)
        rotq = S[:, 3072:5120].rearrange("p (t n e) -> p t n e", t=2, n=16)
        rotk = S[:, 5120:7168].rearrange("p (t m u e) -> p t m u e", t=2, m=8, u=2)
        vv = S[:, 7168:8192].rearrange("p (t s e) -> p t s e", t=2, s=2)
        xp = S[:, 8192:9216].rearrange("p (s g u e) -> p s g u e", s=2, g=4, u=2)
        xpT = S[:, 9216:10240].rearrange("p (s g m) -> p s g m", s=2, g=4)
        Bc = S[:, 10240:12160].rearrange("p (s j g n) -> p s j g n", s=2, j=16, g=4)
        OT = S[:, 0:2048].rearrange("p (k q) -> p k q", k=8)
        Pc = S[:, 2048:3072].rearrange("p (t n e) -> p t n e", t=2, n=16)
        pT = S[:, 3072:6144].rearrange("p (b n) -> p b n", b=2)
        Pb = S[:, 8192:11264].rearrange("p (b i n) -> p b i n", b=2, i=2)
        PcT = S[:, 11264:12288].rearrange("p (c q) -> p c q", c=4)
        qT = hn[:, :, :].rearrange("p t (k q) -> p (t k) q", q=T)
        kT = xnT[:, :, :].rearrange("p (s g) q -> p s g q", s=2)

        x_in, vec_in, misc_in, p_in = sem("x_in"), sem("vec_in"), sem("misc_in"), sem("p_in")
        pw1_in = [sem(f"pw1_in{i}") for i in range(4)]
        w2_in = [sem(f"w2_in{i}") for i in range(2)]
        ple_in = [sem(f"ple_in{i}") for i in range(2)]
        proj_in = sem("proj_in")
        att_in, gate_in, mask_ok, c_bld = sem("att_in"), sem("gate_in"), sem("mask_ok"), sem("c_bld")
        tap_mm, dg_ok, ptap_ok, root_in, root_ok = sem("tap_mm"), sem("dg_ok"), sem("ptap_ok"), sem("root_in"), sem("root_ok")
        x_bld = sem("x_bld")
        pe_step, pool_step = sem("pe_step"), sem("pool_step")
        in_in = [sem(f"in_in{i}") for i in range(5)]
        gu_in = [sem(f"gu_in{i}") for i in range(2)]
        dn_in = [sem(f"dn_in{i}") for i in range(2)]
        out_st = sem("out_st")
        c_pool, c_dve, c_act = sem("c_pool"), sem("c_dve"), sem("c_act")
        const_ok = sem("const_ok")
        vtr, vec_ok = sem("vtr"), sem("vec_ok")
        h_dve, h_act = sem("h_dve"), sem("h_act")
        ssq_ok, var_ok, rs_ok, hn_dve, hn_act, tr_ok = sem("ssq_ok"), sem("var_ok"), sem("rs_ok"), sem("hn_dve"), sem("hn_act"), sem("tr_ok")
        xt_dve, xt_act = sem("xt_dve"), sem("xt_act")
        pw1_mm, sig_ok, glu_ok, conv_ok, lnmm, ln_c, ln_sq, ln_r, silu_ok, out_mm = [
            sem(s) for s in ("pw1_mm", "sig_ok", "glu_ok", "conv_ok", "lnmm", "ln_c", "ln_sq",
                             "ln_r", "silu_ok", "out_mm")]
        ptr, pT_ok, pp_mm, pp_ok = sem("ptr"), sem("pT_ok"), sem("pp_mm"), sem("pp_ok")
        rt_mm, rt_d, rt_e, rt_c, rt_pf, rt_s, rt_row, row_dve, row_act, tab_ok = [
            sem(s) for s in ("rt_mm", "rt_d", "rt_e", "rt_c", "rt_pf", "rt_s", "rt_row", "row_dve",
                             "row_act", "tab_ok")]
        sel_ok, wT_ok, wT_free = sem("sel_ok"), sem("wT_ok"), sem("wT_free")
        ga_mm, xg_ok, xt_mm, xgT_ok = sem("ga_mm"), sem("xg_ok"), sem("xt_mm"), sem("xgT_ok")
        gu_mm, sil_ok, h_ok, ht_mm, hT_ok, y_mm, y_ok = [
            sem(s) for s in ("gu_mm", "sil_ok", "h_ok", "ht_mm", "hT_ok", "y_mm", "y_ok")]
        slot_free = sem("slot_free")
        XN = ("x_sel", "x_ga", "x_xg", "x_xt", "x_xgT", "x_gu", "x_sil", "x_h", "x_ht", "x_hT", "x_y", "x_ysb", "x_done", "x_wT")
        X = {n: sem(n) for n in XN}
        pl_mm, pl_sig, pl_mul = sem("pl_mm"), sem("pl_sig"), sem("pl_mul")
        xp_mm, xp_ok, xpt_mm, xpt_ok, B_ok = sem("xp_mm"), sem("xp_ok"), sem("xpt_mm"), sem("xpt_ok"), sem("B_ok")
        kv_mm, kv_dve, kv_act, gate_mm, gate_ok, q_mm = (sem("kv_mm"), sem("kv_dve"), sem("kv_act"), sem("gate_mm"),
                                                         sem("gate_ok"), sem("q_mm"))
        trig_ok, sin_ok = sem("trig_ok"), sem("sin_ok")
        sq_ok, sq_used, rot_ok = sem("sq_ok"), sem("sq_used"), sem("rot_ok")
        s_sclv = sem("s_sclv")
        c1_mm, c1_x, c1_s, c1_g, c1_t, c1_T, kc_mm, kc_x, kct_mm, kcT_ok, vcr_ok = [
            sem(s) for s in ("c1_mm", "c1_x", "c1_s", "c1_g", "c1_t", "c1_T", "kc_mm", "kc_x", "kct_mm",
                             "kcT_ok", "vcr_ok")]
        qt_mm, qt_dve, qt_act = sem("qt_mm"), sem("qt_dve"), sem("qt_act")
        sc_mm, sc_d, sc_e, sc_p, sct_mm, pct_ok = (sem("sc_mm"), sem("sc_d"), sem("sc_e"), sem("sc_p"),
                                                   sem("sct_mm"), sem("pct_ok"))
        s_mm, s_max, s_exp, s_fac, s_scl, t_mm, pt_dve, pt_act, o_mm, o_ok = [
            sem(s) for s in ("s_mm", "s_max", "s_exp", "s_fac", "s_scl", "t_mm", "pt_dve", "pt_act", "o_mm",
                             "o_ok")]

        block = ctx.enter_context(nc.Block())

        @block.sync
        def _(sp):
            def cols(w, n):
                return w.rearrange("(k p) n -> p k n", p=P)[:, :, 512 * n:512 * (n + 1)]

            def expert(L, e, s):
                for g, w in enumerate((moe_w_gate, moe_w_up)):
                    sp.dma_start(ring[:, s, 4096 * g:4096 * (g + 1)].rearrange("p (j r) -> p j r", j=4),
                                 w[L, e].rearrange("(j p c) f -> p j (c f)", j=4, c=2)).then_inc(gu_in[s], 16)
                sp.dma_start(ring[:, s, 8192:12288].rearrange("p (f r) -> p f r", f=2),
                             moe_w_down[L, e].rearrange("(f p c) d -> p f (c d)", f=2, c=2)).then_inc(dn_in[s], 16)

            def experts(L):
                with sp.Fori(1, NE // 2) as it:
                    for s in range(2):
                        sp.wait_ge(slot_free, it * 2 + (s - 1 + NE * L))
                        expert(L, it * 2 + s, s)

            def embeddings(L):
                sp.dma_start(pin, p[L, 0].rearrange("(t q) d -> q t d", q=P)).then_inc(p_in, 16)
                sp.dma_start(wproj, ple_w_proj[L].rearrange("(c p) d -> p c d", p=P)).then_inc(proj_in, 16)

            for t in range(NT):
                sp.dma_start(h[:, t, :], x[0, t * P:(t + 1) * P, :]).then_inc(x_in, 16)
            for r, v in ((ROW_MIX, g_mix), (ROW_FFN, g_ffn), (ROW_PLE, g_ple), (ROW_BPW1, conv_b_pw1),
                         (ROW_BDW, conv_b_dw), (ROW_LNG, conv_ln_g), (ROW_LNB, conv_ln_b)):
                rows = v.shape[0] * v.shape[1] // P
                sp.dma_start(prow[r:r + rows, 0:P], v.rearrange("l (r c) -> (l r) c", c=P)).then_inc(vec_in, 16)
            sp.dma_start(prow[0:8, P:P + 256], g_ffn.rearrange("l (r c) -> (l r) c", c=256)).then_inc(vec_in, 16)
            sp.dma_start(wdw_rows, conv_w_dw[0]).then_inc(vec_in, 16)
            sp.dma_start(bpw2, conv_b_pw2).then_inc(vec_in, 16)
            for i, (c0, c1) in enumerate(PW1_PARTS):
                for g in range(2):
                    w = conv_w_pw1[0].rearrange("(k p) n -> p k n", p=P)[:, :, D * g + P * c0:D * g + P * c1]
                    o = P * (c0 % 4)
                    sp.dma_start(dense(PW1[2 * (c0 // 4) + g])[:, :, o:o + P * (c1 - c0)], w).then_inc(pw1_in[i], 16)
            for n in range(2):
                sp.dma_start(dense(PW2[n]), cols(conv_w_pw2[0], n)).then_inc(w2_in[n], 16)
            expert(0, 0, 0)
            sp.wait_ge(pw1_mm, 4)
            for n in range(2):
                sp.dma_start(dense(WB[n]), cols(ple_w_gate[0], n)).then_inc(ple_in[n], 16)
            sp.wait_ge(pw1_mm, 8)
            sp.dma_start(dense(WB[2]), cols(nsa_w_in[0], 2)).then_inc(in_in[2], 16)
            sp.wait_ge(out_mm, 4)
            embeddings(0)
            expert(0, 1, 1)
            experts(0)
            sp.wait_ge(slot_free, NE - 1)
            for n, b in ((3, 0), (4, 1), (0, 2)):
                sp.dma_start(dense(R0[b]), cols(nsa_w_in[0], n)).then_inc(in_in[n], 16)
            sp.wait_ge(slot_free, NE)
            sp.wait_ge(wT_ok, NE + 1)
            sp.dma_start(pei[0:16, :, :], nsa_cmp_pe[0].rearrange("s (j u) e -> j s (u e)", u=2)).then_inc(att_in, 16)
            for m, v in enumerate((nsa_q_norm[0:1, :], nsa_k_norm[0, 1:2, :], nsa_k_norm[0, 2:3, :], nsa_k_norm[0, 0:1, :])):
                sp.dma_start(gn[:, m, :], v.broadcast_to([P, DH])).then_inc(att_in, 16)
            sp.dma_start(invb, inv_freq.broadcast_to([P, DH // 2])).then_inc(att_in, 16)
            for s in range(2):
                sp.dma_start(w2c[:, s, :, :], nsa_cmp_w2[0, s].rearrange("(c p) n -> p c n", p=P)).then_inc(att_in, 16)
            sp.wait_ge(pl_mm, 2)
            sp.dma_start(dense(WB[0]), cols(nsa_w_in[0], 1)).then_inc(in_in[1], 16)
            sp.wait_ge(pl_mm, 4)
            sp.dma_start(WB[1].rearrange("p (j n) -> p j n", j=16),
                         nsa_cmp_w1[0, 0].rearrange("(j p) n -> p j n", p=P)).then_inc(w2_in[0], 16)
            sp.wait_ge(h_dve, H_DVE[3])
            sp.dma_start(wgate3, nsa_w_in[0].rearrange("(k p) n -> p k n", p=P)[:, :, 2560:2608]).then_inc(gate_in, 16)
            sp.wait_ge(xp_mm, 2)
            sp.dma_start(WB[2].rearrange("p (j n) -> p j n", j=16),
                         nsa_cmp_w1[0, 1].rearrange("(j p) n -> p j n", p=P)).then_inc(w2_in[1], 16)
            sp.wait_ge(q_mm, 4)
            sp.dma_start(dense(WB[0]), cols(nsa_w_out[0], 0)).then_inc(in_in[0], 16)
            sp.wait_ge(c1_mm, 1)
            sp.dma_start(dense(WB[1]), cols(nsa_w_out[0], 1)).then_inc(in_in[1], 16)
            expert(1, 0, 0)
            sp.wait_ge(c1_mm, 2)
            sp.dma_start(dense(WB[2]), cols(ple_w_gate[1], 0)).then_inc(ple_in[0], 16)
            sp.wait_ge(out_mm, 8)
            embeddings(1)
            expert(1, 1, 1)
            sp.dma_start(dense(WB[0]), cols(ple_w_gate[1], 1)).then_inc(ple_in[1], 16)
            experts(1)
            sp.wait_ge(h_dve, H_DVE[6])
            for t in range(NT):
                sp.dma_start(out[0, t * P:(t + 1) * P, :], h[:, t, :]).then_inc(out_st, 16)
            sp.wait_ge(out_st, 16 * NT)

        PLE_W = [[WB[0], WB[1]], [WB[2], WB[0]]]

        @block.tensor
        def _(pe):
            def norm_T(a):
                pe.wait_ge(hn_dve, a + 1)
                pe.wait_ge(hn_act, a + 1)
                for kp in range(4):
                    for kk in range(2):
                        for t in range(NT):
                            k = 2 * kp + kk
                            i = pe.transpose(PS[:, 4 + kp, (kk * 2 + t) * P:(kk * 2 + t + 1) * P],
                                             hn[:, t, k * P:(k + 1) * P], ident[:, :])
                    i.then_inc(tr_ok, 1)

            def xnT_ready(a, k):
                kp = k // 2
                pe.wait_ge(xt_act if kp % 2 else xt_dve, 4 * a + 2 * (kp // 2) + k % 2 + 1)

            def tokens_out(w, bank, t, done, a=None, lhs=xnT, start=True):
                for k in range(KD):
                    if a is not None:
                        xnT_ready(a, k)
                    i = pe.matmul(PS[:, bank, :], lhs[:, k, t * P:(t + 1) * P], w[:, k, :],
                                  start=start and k == 0, stop=(k == KD - 1))
                i.then_inc(done, 1)

            pe.wait_ge(const_ok, 1)
            pe.wait_ge(vec_in, 16 * N_VEC)
            pe.transpose(PS[:, 0, 0:NROWS], prow[0:NROWS, 0:P], ident[0:NROWS, 0:NROWS]).then_inc(vtr, 1)
            for c in range(2):
                i = pe.transpose(PS[:, 1, c * 8:c * 8 + 8], prow[0:8, P + c:P + 256:2], ident[0:8, 0:8])
            i.then_inc(vtr, 1)
            for c in range(KD):
                i = pe.transpose(PS[:, 2, c * TAPS:(c + 1) * TAPS], wdw_rows[:, c * P:(c + 1) * P],
                                 ident[0:TAPS, 0:TAPS])
            i.then_inc(vtr, 1)

            norm_T(0)
            def taps(c):
                pe.wait_ge(glu_ok, c + 1)
                pe.wait_ge(dg_ok, c + 1)
                if c >= 2:
                    pe.wait_ge(conv_ok, c - 1)
                for i_ in range(PE_TAPS):
                    w = TAPS - PE_TAPS + i_
                    i = pe.matmul(PS[:, 4 + c % 2, 0:T], dgb[:, c % 2, i_, :], cv0[:, c, w:w + T],
                                  start=(i_ == 0), stop=(i_ == PE_TAPS - 1))
                i.then_inc(tap_mm, 1)

            def channel_sum(c):
                pe.wait_ge(conv_ok, c + 1)
                i = pe.matmul(PS[:, 6, 0:T], ones[:, :], cT[:, c, :], start=(c == 0), stop=(c == KD - 1))
                if c == KD - 1:
                    i.then_inc(lnmm, 1)

            for c in range(KD):
                part = (0, 1, 2, 2, 3, 3, 3, 3)[c]
                pe.wait_ge(pw1_in[part], 32)
                if c >= 4:
                    pe.wait_ge(glu_ok, c - 3)
                else:
                    pe.wait_ge(vec_ok, 3)
                for g in range(2):
                    w = dense(PW1[2 * (c // 4) + g])
                    for k in range(KD):
                        xnT_ready(0, k)
                        i = pe.matmul(PS[:, c % 4, g * T:(g + 1) * T], w[:, k, (c % 4) * P:(c % 4 + 1) * P],
                                      xnT[:, k, :], start=(k == 0), stop=(k == KD - 1))
                i.then_inc(pw1_mm, 1)
                if c >= 1:
                    taps(c - 1)
                if c >= 3:
                    channel_sum(c - 3)
            taps(KD - 1)
            for n in range(2):
                for t in range(NT):
                    pe.matmul(PS[:, 2 * n + t, :], ones[0:1, :], bpw2[:, 512 * n:512 * (n + 1)], start=True, stop=False)
            for c in range(KD - 3, KD):
                channel_sum(c)
            for c in range(KD):
                pe.wait_ge(ln_sq, c + 1)
                i = pe.matmul(PS[:, 7, 0:T], ones[:, :], xnT[:, c, :], start=(c == 0), stop=(c == KD - 1))
            i.then_inc(lnmm, 1)
            for n in range(2):
                pe.wait_ge(w2_in[n], 16)
                for t in range(NT):
                    for k in range(KD):
                        pe.wait_ge(silu_ok, k + 1)
                        i = pe.matmul(PS[:, 2 * n + t, :], cT[:, k, t * P:(t + 1) * P], dense(PW2[n])[:, k, :],
                                      start=False, stop=(k == KD - 1))
                    i.then_inc(out_mm, 1)

            def gather(lhs):
                for t in range(NT):
                    for j in range(4):
                        i = pe.matmul(PS[32 * j:32 * j + 32, BGX, 0:Q4], lhs[:, t, :], hn[:, t, Q4 * j:Q4 * (j + 1)],
                                      start=(t == 0), stop=(t == NT - 1))
                return i

            def xg_T():
                for c in range(2):
                    i = pe.transpose(PS[:, BGX, Q4 + P * c:Q4 + P * (c + 1)], xg[:, c::2], ident[:, :])
                return i

            def gate_up(s, xT):
                for k in range(8):
                    for j in range(4):
                        i = pe.matmul(PS[32 * j:32 * j + 32, BGU, 0:256], xT[:, k, :],
                                      w_gu(s)[:, j // 2, k, 256 * (j % 2):256 * (j % 2 + 1)],
                                      start=(k == 0), stop=(k == 7))
                return i

            def h_T():
                pe.sem_inc(pe_step, 1)
                for c in range(2):
                    i = pe.transpose(PS[:, BHT, 64 * c:64 * (c + 1)], hh[64:128, c::2], ident[64:128, 64:128])
                return i

            def down(s):
                for q in range(4):
                    f, c = q // 2, q % 2
                    for j in range(4):
                        i = pe.matmul(PS[32 * j:32 * j + 32, BY, 0:Q4], hT[:, c, 32 * f:32 * f + 32],
                                      w_dn(s)[:, f, c, Q4 * j:Q4 * (j + 1)], start=(q == 0), stop=(q == 3))
                return i

            def scatter(w):
                for t in range(NT):
                    for j in range(4):
                        i = pe.matmul(PS[:, ACC + j, 256 * t:256 * (t + 1)], w[32 * j:32 * j + 32, t * P:(t + 1) * P],
                                      ysb[32 * j:32 * j + 32, :], start=False, stop=False, skip_group_check=True)
                return i

            def moe(L):
                a = 3 * L + 1
                norm_T(a)
                pe.wait_ge(misc_in, 16 * N_MISC)
                xnT_ready(a, 0)
                xnT_ready(a, 1)
                for t in range(NT):
                    o = PS[:, BGU, 64 * t:64 * t + 36]
                    pe.matmul(o, ones[0:1, :], rowb[0:1, 36 * L:36 * (L + 1)], start=True, stop=False)
                    for k in range(KD):
                        xnT_ready(a, k)
                        i = pe.matmul(o, xnT[:, k, t * P:(t + 1) * P], wr[:, L, k, :], start=False, stop=(k == KD - 1))
                i.then_inc(rt_mm, 1)
                pe.wait_ge(p_in, 16 * (L + 1))
                pe.wait_ge(xt_dve, 4 * a + 4)
                pe.wait_ge(xt_act, 4 * a + 4)
                for c in range(2):
                    for t in range(NT):
                        i = pe.transpose(PS[:, 5, (2 * c + t) * P:(2 * c + t + 1) * P], pin[:, t, c * P:(c + 1) * P], ident[:, :])
                i.then_inc(ptr, 1)
                pe.wait_ge(pT_ok, L + 1)
                pe.wait_ge(proj_in, 16 * (L + 1))
                def embedding_product(n, t):
                    for c in range(2):
                        i = pe.matmul(PS[:, 2 * n + t, :], pT2[:, c, t * P:(t + 1) * P],
                                      wproj[:, c, 512 * n:512 * (n + 1)], start=(c == 0), stop=(c == 1))
                    i.then_inc(pp_mm, 1)

                embedding_product(0, 0)
                embedding_product(0, 1)
                pe.wait_ge(rt_c, L + 1)
                pe.matmul(PS[:, 6, 0:32], upper[:, :], Cc[:, 0, :], start=True, stop=True)
                pe.matmul(PS[:, 6, 32:64], upper[:, :], Cc[:, 1, :], start=True, stop=False)
                pe.matmul(PS[:, 6, 32:64], ones[:, :], Cc[:, 0, :], start=False, stop=True)
                pe.matmul(PS[:, 6, 64:96], ones[:, :], Cc[:, 0, :], start=True, stop=False)
                pe.matmul(PS[:, 6, 64:96], ones[:, :], Cc[:, 1, :], start=False, stop=True).then_inc(rt_pf, 1)
                embedding_product(1, 0)
                embedding_product(1, 1)
                pe.wait_ge(rt_s, L + 1)
                for v, bk in ((S4, 5), (W4, 7)):
                    for t in range(NT):
                        for s in range(2):
                            i = pe.matmul(PS[:, bk, (2 * s + t) * P:(2 * s + t + 1) * P],
                                          v[:, t, s:s + 1].broadcast_to([P, P]), ident[:, :], start=True, stop=True)
                i.then_inc(rt_row, 1)
                pe.wait_ge(row_dve, L + 1)
                g0 = (NE + 1) * L
                pe.wait_ge(sel_ok, g0 + 1)
                gather(sel[0]).then_inc(ga_mm, 1)
                pe.wait_ge(pp_ok, 4 * (L + 1))
                for t in range(NT):
                    for j in range(4):
                        i = pe.matmul(PS[:, ACC + j, 256 * t:256 * (t + 1)], ident[:, :], h[:, t, Q4 * j:Q4 * (j + 1)],
                                      start=(t == 0), stop=False, skip_group_check=True)
                pe.wait_ge(xg_ok, g0 + 1)
                xg_T().then_inc(xt_mm, 1)
                pe.wait_ge(row_act, L + 1)
                pe.wait_ge(tab_ok, L + 1)
                with pe.Fori(0, NE // 2) as it:
                    for s in range(2):
                        n = it * 2 + (s + NE * L + 1)
                        gi = it * 2 + (s + g0 + 2)
                        ld = it * 16 + 16 * (NE // 2 * L + 1)
                        pe.wait_ge(gu_in[s], ld * 2)
                        pe.wait_ge(xgT_ok, gi - 1)
                        gate_up(s, xgT).then_inc(gu_mm, 1)
                        pe.wait_ge(sel_ok, gi)
                        gather(sel[1 - s]).then_inc(ga_mm, 1)
                        pe.wait_ge(h_ok, n)
                        h_T().then_inc(ht_mm, 1)
                        pe.wait_ge(dn_in[s], ld)
                        pe.wait_ge(hT_ok, n)
                        down(s).then_inc(y_mm, 1)
                        pe.wait_ge(xg_ok, gi)
                        xg_T().then_inc(xt_mm, 1)
                        pe.wait_ge(wT_ok, gi - 1)
                        pe.wait_ge(y_ok, n)
                        scatter(wT[s]).then_inc(wT_free, 1)
                        e = it * 2 + s
                        more = pe.value_load(tab[0:1, 0, bass.ds(e, 1)], min_val=0, max_val=7)
                        before = pe.value_load(tab[0:1, 1, bass.ds(e, 1)], min_val=0, max_val=64)
                        with pe.If(more > 0):
                            with pe.Fori(0, more) as r:
                                c = before + r + 1
                                pe.wait_ge(X["x_sel"], c)
                                pe.wait_ge(xgT_ok, gi)
                                gather(xsel).then_inc(X["x_ga"], 1)
                                pe.wait_ge(X["x_xg"], c)
                                xg_T().then_inc(X["x_xt"], 1)
                                pe.wait_ge(X["x_xgT"], c)
                                gate_up(s, xxgT).then_inc(X["x_gu"], 1)
                                pe.wait_ge(X["x_h"], c)
                                h_T().then_inc(X["x_ht"], 1)
                                pe.wait_ge(X["x_hT"], c)
                                down(s).then_inc(X["x_y"], 1)
                                pe.wait_ge(X["x_wT"], c)
                                pe.wait_ge(X["x_ysb"], c)
                                scatter(xwT).then_inc(X["x_done"], 1)
                        pe.drain().then_inc(slot_free, 1)
                norm_T(a + 1)
                for n in range(2):
                    pe.wait_ge(ple_in[n], 16 * (L + 1))
                    for t in range(NT):
                        tokens_out(dense(PLE_W[L][n]), 2 * n + t, t, pl_mm, a + 1)

            pe.sem_inc(wT_free, 1)
            pe.sem_inc(X["x_done"], 1)
            moe(0)

            norm_T(3)
            pe.wait_ge(in_in[2], 16)
            pe.wait_ge(pl_mul, 4)
            for u in range(2):
                for k in range(KD):
                    xnT_ready(3, k)
                    i = pe.matmul(PS[:, u, :], xnT[:, k, u::2], dense(WB[2])[:, k, :], start=(k == 0), stop=(k == KD - 1))
                i.then_inc(xp_mm, 1)
            for s in range(2):
                pe.wait_ge(in_in[3 + s], 16)
                for t in range(NT):
                    bk = 2 + t if s == 0 else 4 + t
                    tokens_out(dense(R0[s]), bk, t, kv_mm, 3)
            pe.wait_ge(gate_in, 16)
            for t in range(NT):
                for k in range(KD):
                    i = pe.matmul(PS[:, 6, 64 * t:64 * t + 48], xnT[:, k, t * P:(t + 1) * P], wgate3[:, k, :],
                                  start=(k == 0), stop=(k == KD - 1))
            i.then_inc(gate_mm, 1)
            pe.wait_ge(xp_ok, 2)
            for s in range(2):
                for g in range(NKV):
                    i = pe.transpose(PS[:, s, g * P:(g + 1) * P], xp[:, s, g, :, :].rearrange("p u e -> p (u e)"), ident[:, :])
                i.then_inc(xpt_mm, 1)
            for s in range(2):
                i = pe.transpose(PS[:, 7, 16 * s:16 * s + 16], pei[0:16, s, :], ident[0:16, 0:16])
            i.then_inc(xpt_mm, 1)
            pe.wait_ge(kv_dve, 4)
            pe.wait_ge(kv_act, 4)
            for t in range(NT):
                for n in range(2):
                    pe.wait_ge(in_in[n], 16)
                    tokens_out(dense(R0[2] if n == 0 else WB[0]), 2 + 2 * n + t, t, q_mm)
            for s in range(2):
                pe.wait_ge(w2_in[s], 32)
                pe.wait_ge(B_ok, s + 1)
                w1 = (WB[1] if s == 0 else WB[2]).rearrange("p (j n) -> p j n", j=16)
                for j in range(16):
                    i = pe.matmul(PS[0:60, s, 0:256], Bc[:, s, j, :, :].rearrange("p g n -> p (g n)"), w1[:, j, :], start=(j == 0), stop=(j == 15))
                i.then_inc(c1_mm, 1)
            for s in range(2):
                pe.wait_ge(c1_g, s + 1)
                if s == 1:
                    pe.wait_ge(kc_x, 1)
                for c in range(2):
                    i = pe.transpose(PS[:, 0, 256 + 64 * c:256 + 64 * c + 60], h1v[s][0:60, c * P:(c + 1) * P], ident[0:60, 0:60])
                i.then_inc(c1_t, 1)
                pe.wait_ge(c1_T, s + 1)
                if s == 0:
                    for c in range(2):
                        i = pe.matmul(PS[0:60, 0, 0:64], h1T[:, c, 0:60], w2c[:, 0, c, :], start=(c == 0), stop=(c == 1))
                else:
                    for c in range(2):
                        for g in range(4):
                            for q in range(4):
                                i = pe.matmul(PS[32 * q:32 * q + NC_, 1, 256 + 64 * g:256 + 64 * g + 64], h1T[:, c, NC_ * g:NC_ * (g + 1)],
                                              w2c[:, 1, c, :], start=(c == 0 and g == 0), stop=(c == 1), skip_group_check=True)
                i.then_inc(kc_mm, 1)
            for b in range(4):
                if b == 0:
                    pe.wait_ge(rot_ok, 1)
                    pe.wait_ge(gate_ok, 1)
                if b == 2:
                    pe.wait_ge(qt_dve, 1)
                    pe.wait_ge(qt_act, 1)
                for kk in range(2):
                    for t in range(NT):
                        m = 4 * (b // 2) + 2 * (b % 2) + kk
                        i = pe.transpose(PS[:, 6 + b % 2, (2 * kk + t) * P:(2 * kk + t + 1) * P], rotk[:, t, m, :, :], ident[:, :])
                i.then_inc(qt_mm, 1)
            pe.wait_ge(rot_ok, 3)
            for b in range(4):
                for kk in range(2):
                    for t in range(NT):
                        hp = 2 * b + kk
                        i = pe.transpose(PS[:, 2 + b, (2 * kk + t) * P:(2 * kk + t + 1) * P],
                                         rotq[:, t, 2 * hp:2 * hp + 2, :], ident[:, :])
                i.then_inc(qt_mm, 1)
            pe.wait_ge(kc_x, 2)
            pe.transpose(PS[:, 0, 384:444], kcx[0:60, 2:4, :], ident[0:60, 0:60]).then_inc(kct_mm, 1)
            pe.wait_ge(kcT_ok, 1)
            pe.wait_ge(vcr_ok, 1)
            pe.wait_ge(qt_dve, 4)
            pe.wait_ge(qt_act, 4)
            for hp in range(8):
                for t in range(NT):
                    for i_ in range(2):
                        r = slice(64 * i_, 64 * i_ + 64)
                        o = 128 * t + 16 * hp
                        i = pe.matmul(PS[:, i_, o:o + NC_], qT[r, hp, t * P:(t + 1) * P], kcT[r, NC_ * (hp // 2):NC_ * (hp // 2 + 1)],
                                      start=True, stop=True)
            i.then_inc(sc_mm, 1)

            def scores(hp):
                g = hp // 2
                if hp > 0:
                    pe.wait_ge(s_max, 9 * hp - 1)
                else:
                    pe.wait_ge(sc_d, 1)
                for t in range(NT):
                    for i_ in range(2):
                        r = slice(64 * i_, 64 * i_ + 64)
                        i = pe.matmul(PS[:, 2 * t + i_, 0:256 * (t + 1)], qT[r, hp, t * P:(t + 1) * P],
                                      kT[r, :, g, 0:P * (t + 1)], start=True, stop=True)
                i.then_inc(s_mm, 1)

            def probs_T(hp):
                pe.wait_ge(s_scl, 2 * (hp + 1))
                pe.wait_ge(s_sclv, hp + 1)
                if hp > 0:
                    pe.wait_ge(pt_dve, hp)
                    pe.wait_ge(pt_act, 2 * hp)
                for n in range(12):
                    i_, s, q = n // 6, (n // 3) % 2, n % 3
                    src = Pb[:, hp % 2, i_, 128 * s:128 * s + 128] if q == 0 else \
                        Pb[:, hp % 2, i_, 256 + 256 * s + 128 * (q - 1):256 + 256 * s + 128 * q]
                    i = pe.transpose(PS[:, 4 + n // 4, (n % 4) * P:(n % 4 + 1) * P], src, ident[:, :])
                    if n % 4 == 3:
                        i.then_inc(t_mm, 1)

            def pv(hp):
                g = hp // 2
                pe.wait_ge(pt_dve, hp + 1)
                pe.wait_ge(pt_act, 2 * hp + 2)
                if hp > 0:
                    pe.wait_ge(o_ok, hp)
                for s in range(2):
                    for kb in range(2):
                        for i_ in range(2):
                            o = i_ * 768 + s * 384
                            rhs = pT[:, hp % 2, o:o + 256] if kb == 0 else pT[:, hp % 2, o + 256:o + 384]
                            pe.matmul(PS[64 * i_:64 * i_ + 64, 7, 128 * kb:256], vv[:, kb, s, 64 * g:64 * g + 64], rhs,
                                      start=(s == 0 and kb == 0), stop=False, skip_group_check=True)
                for i_ in range(2):
                    hd = 2 * hp + i_
                    r = slice(32 * (hd % 4), 32 * (hd % 4) + NC_)
                    i = pe.matmul(PS[64 * i_:64 * i_ + 64, 7, 0:256], vcr[r, g, :], PcT[r, hd // 4, :],
                                  start=False, stop=True, skip_group_check=True)
                i.then_inc(o_mm, 1)

            scores(0)
            pe.wait_ge(sc_p, 1)
            for t in range(NT):
                for c in range(4):
                    i = pe.transpose(PS[:, 4 + c // 2, (2 * (c % 2) + t) * P:(2 * (c % 2) + t + 1) * P], Pc[:, t, 4 * c:4 * c + 4, :], ident[:, :])
            i.then_inc(sct_mm, 1)
            pe.wait_ge(pct_ok, 2)
            for hp in range(8):
                if hp < 7:
                    scores(hp + 1)
                probs_T(hp)
                pv(hp)
            pe.wait_ge(o_ok, 8)
            for n in range(2):
                pe.wait_ge(in_in[n], 32)
                for t in range(NT):
                    tokens_out(dense(WB[n]), 2 * n + t, t, out_mm, lhs=OT)
            moe(1)

        @block.gpsimd
        def _(pool):
            g = nc.gpsimd
            own = [0]

            def link(i):
                own[0] += 1
                i.then_inc(c_pool, 1)
                pool.wait_ge(c_pool, own[0])

            link(g.memset(ident[:, :], 0.0))
            link(g.affine_select(out=ident[:, :], in_=ident[:, :], compare_op=ALU.not_equal, fill=1.0, base=0,
                                 pattern=[[-1, P]], channel_multiplier=1))
            link(g.memset(ones[:, :], 1.0))
            link(g.memset(nhalf[:, :], -0.5))
            link(g.affine_select(out=upper[:, :], in_=ones[:, :], compare_op=ALU.is_gt, fill=0.0, base=0,
                                 pattern=[[1, P]], channel_multiplier=-1))
            link(g.memset(cmask[:, :, :], 0.0))
            link(g.affine_select(out=cmask[:, 1, :], in_=cmask[:, 1, :], compare_op=ALU.is_ge, fill=NEG, base=0,
                                 pattern=[[-1, P]], channel_multiplier=1))
            link(g.iota(ioti[:, :], pattern=[[1, 32]], base=0, channel_multiplier=0))
            link(g.tensor_copy(iot[:, :], ioti[:, :]))
            for q in range(4):
                link(g.iota(ioti[32 * q:32 * q + 32, 0:1], pattern=[[0, 1]], base=0, channel_multiplier=1))
            g.tensor_copy(colp[:, :], ioti[:, 0:1]).then_inc(const_ok, 1)

            def rsqrt(n, x):
                pool.wait_ge(var_ok, n)
                g.tensor_tensor(x, x, nhalf[0:x.shape[0], 0:1].broadcast_to(list(x.shape)), ALU.pow).then_inc(rs_ok, 1)

            def build_block(c32, cc, to_sel, to_wT, count, base, s_ok, w_ok, rows=None):
                for t in range(NT):
                    for k in range(2):
                        i = g.tensor_scalar(eq4[:, t, k, :], c32, S4[:, t, k:k + 1], None, ALU.is_equal)
                i.then_inc(count, 1)
                pool.wait_ge(count, base + 1)
                g.tensor_tensor(to_sel, eq4[:, :, 0, :], eq4[:, :, 1, :], ALU.add).then_inc(s_ok, 1)
                if rows is not None:
                    pool.wait_ge(row_dve, rows)
                    pool.wait_ge(row_act, rows)
                g.tensor_scalar(eqr, srow, cc, None, ALU.is_equal).then_inc(count, 1)
                pool.wait_ge(count, base + 2)
                g.tensor_tensor(eqr, eqr, wrow, ALU.mult).then_inc(count, 1)
                pool.wait_ge(count, base + 3)
                g.tensor_tensor(to_wT, eqr[:, 0, :], eqr[:, 1, :], ALU.add).then_inc(w_ok, 1)

            def moe(L):
                g0 = (NE + 1) * L
                pool.wait_ge(rt_s, L + 1)
                g.tensor_copy(cur32, iot[:, :]).then_inc(c_bld, 1)
                g.tensor_copy(curc, colp[:, :]).then_inc(c_bld, 1)
                pool.wait_ge(c_bld, 5 * g0 + 2)
                build_block(cur32, curc, sel[0], wT[0], c_bld, 5 * g0 + 2, sel_ok, wT_ok, L + 1)
                pool.wait_ge(tab_ok, L + 1)
                with pool.Fori(0, NE // 2) as it:
                    for s in range(2):
                        gi = it * 2 + (s + g0 + 1)
                        pool.wait_ge(wT_free, it * 2 + (s + NE * L + 1))
                        pool.sem_inc(pool_step, 1)
                        g.tensor_scalar(cur32, cur32, 256.0, None, ALU.add).then_inc(c_bld, 1)
                        g.tensor_scalar(curc, curc, 256.0, None, ALU.add).then_inc(c_bld, 1)
                        pool.wait_ge(c_bld, gi * 5 + 2)
                        pool.sem_inc(pool_step, 1)
                        build_block(cur32, curc, sel[1 - s], wT[1 - s], c_bld, gi * 5 + 2, sel_ok, wT_ok)
                        e = it * 2 + s
                        more = pool.value_load(tab[0:1, 0, bass.ds(e, 1)], min_val=0, max_val=7)
                        before = pool.value_load(tab[0:1, 1, bass.ds(e, 1)], min_val=0, max_val=64)
                        with pool.If(more > 0):
                            g.tensor_scalar(xcur32, cur32, -256.0, None, ALU.add)
                            g.tensor_scalar(xcurc, curc, -256.0, None, ALU.add)
                            pool.drain()
                            with pool.Fori(0, more) as r:
                                c = before + r
                                pool.wait_ge(X["x_done"], c + 1)
                                pool.sem_inc(pool_step, 1)
                                g.tensor_scalar(xcur32, xcur32, float(SLOTS), None, ALU.add).then_inc(x_bld, 1)
                                g.tensor_scalar(xcurc, xcurc, float(SLOTS), None, ALU.add).then_inc(x_bld, 1)
                                pool.wait_ge(x_bld, c * 5 + 2)
                                pool.sem_inc(pool_step, 1)
                                build_block(xcur32, xcurc, xsel, xwT, x_bld, c * 5 + 2, X["x_sel"], X["x_wT"])

            rsqrt(1, rstd[:, 1, :])
            for c in range(KD):
                pool.wait_ge(glu_ok, c + 1)
                if c >= 2:
                    pool.wait_ge(conv_ok, c - 1)
                for i_ in range(POOL_TAPS):
                    w = TAPS - PE_TAPS - POOL_TAPS + i_
                    u = cv0[:, c, w:w + T]
                    if i_ == 0:
                        g.tensor_scalar(pac[c % 2], u, wdw[:, c, w:w + 1], None, ALU.mult).then_inc(c_pool, 1)
                        own[0] += 1
                    else:
                        link(g.tensor_scalar(ptm, u, wdw[:, c, w:w + 1], None, ALU.mult))
                        i = g.tensor_tensor(pac[c % 2], pac[c % 2], ptm, ALU.add)
                        if i_ < POOL_TAPS - 1:
                            link(i)
                i.then_inc(ptap_ok, 1)
                pool.wait_ge(ptap_ok, c + 1)
            rsqrt(2, rstd[:, 1, :])
            moe(0)
            rsqrt(3, rstd[:, 1, :])
            rsqrt(4, rstd[:, 1, :])
            pool.wait_ge(h_dve, H_DVE[3])
            link(g.memset(mka, 0.0))
            link(g.memset(mk1, 1.0))
            for t in range(NT):
                for m, f in ((mka, NEG), (mk1, 0.0)):
                    link(g.affine_select(out=m[:, t, :], in_=m[:, t, :], compare_op=ALU.is_ge, fill=f,
                                         base=t * P - (CMP_BLOCK - 1), pattern=[[-CMP_STRIDE, NC_]], channel_multiplier=1))
            g.memset(mcol[:, 2:3], 0.0).then_inc(mask_ok, 1)
            rsqrt(5, mcol[0:60, 1:2])
            for hp in range(8):
                pool.wait_ge(s_fac, hp + 1)
                for s in range(2):
                    v = Pb[:, hp % 2, 1, 256 + 256 * s:512 + 256 * s]
                    g.tensor_scalar(v, v, fac[:, hp % 2, 6 + s:7 + s], None, ALU.mult).then_inc(s_scl, 1)
            rsqrt(6, rstd[:, 1, :])
            moe(1)
            rsqrt(7, rstd[:, 1, :])

        @block.scalar
        def _(act):
            own = [0]

            def link(i):
                own[0] += 1
                i.then_inc(c_act, 1)
                act.wait_ge(c_act, own[0])

            def norm(a, row):
                junk = xnT[:, :, :].rearrange("p k q -> p (k q)")
                if a == 0:
                    act.wait_ge(x_in, 16 * NT)
                else:
                    act.wait_ge(h_dve, H_DVE[a])
                    if H_ACT[a]:
                        act.wait_ge(h_act, H_ACT[a])
                nc.scalar.activation(junk[:, D:2 * D], h[:, 1, :], ACT.Square, accum_out=rstd[:, 0, 1:2]).then_inc(ssq_ok, 1)
                act.wait_ge(rs_ok, (1, 2, 3, 4, 6, 7)[a])
                nc.scalar.activation(hn[:, 1, :], h[:, 1, :], ACT.Copy, scale=rstd[:, 1, 1:2]).then_inc(hn_act, 1)
                if a == 0:
                    act.wait_ge(vec_ok, 3)
                for kp in (1, 3):
                    act.wait_ge(tr_ok, 4 * a + kp + 1)
                    for k in (2 * kp, 2 * kp + 1):
                        nc.scalar.activation(xnT[:, k, :], PS[:, 4 + kp, 256 * (k % 2):256 * (k % 2 + 1)], ACT.Copy,
                                             scale=vecT[:, row + k:row + k + 1]).then_inc(xt_act, 1)

            def fill2(dst, src):
                act.dma_start(dst, src, allow_slow_non_contiguous=True).then_inc(misc_in, 16)

            for L in range(DEPTH):
                fill2(wr[:, L, :, 0:NG], moe_w_rg[L].rearrange("(k p) n -> p k n", p=P))
                fill2(wr[:, L, :, NG:], moe_w_re[L].rearrange("(k p) n -> p k n", p=P))
                fill2(rowb[0:1, 36 * L:36 * L + NG], moe_b_rg[L:L + 1, :])
                fill2(rowb[0:1, 36 * L + NG:36 * (L + 1)], moe_b_re[L:L + 1, :])
            for t in range(NT):
                fill2(posi[:, t:t + 1], positions[0:1, t * P:(t + 1) * P].rearrange("o q -> q o"))
            for g in range(NKV):
                fill2(posi[NC_ * g:NC_ * (g + 1), 2:3],
                      positions[0:1, CMP_BLOCK - 1:T:CMP_STRIDE].rearrange("o q -> q o"))

            norm(0, ROW_MIX)
            for c in range(KD):
                act.wait_ge(pw1_mm, c + 1)
                if c >= 2:
                    act.wait_ge(glu_ok, c - 1)
                nc.scalar.activation(sgm[c % 2], PS[:, c % 4, T:2 * T], ACT.Sigmoid,
                                     bias=vecT[:, ROW_BPW1 + 8 + c:ROW_BPW1 + 9 + c]).then_inc(sig_ok, 1)
                if c >= 2:
                    act.wait_ge(tap_mm, c - 1)
                for i_ in range(PE_TAPS):
                    w = TAPS - PE_TAPS + i_
                    i = nc.scalar.activation(dgb[:, c % 2, i_, :], ident[:, :], ACT.Copy, scale=wdw[:, c, w:w + 1])
                i.then_inc(dg_ok, 1)
            for c in range(KD):
                act.wait_ge(ln_c, c + 1)
                nc.scalar.activation(xnT[:, c, :], cT[:, c, :], ACT.Square).then_inc(ln_sq, 1)
            act.wait_ge(root_in, 1)
            nc.scalar.activation(var, var, ACT.Sqrt).then_inc(root_ok, 1)
            for c in range(KD):
                act.wait_ge(ln_r, c + 1)
                nc.scalar.activation(cT[:, c, :], cT[:, c, :], ACT.Silu, scale=vecT[:, ROW_LNG + c:ROW_LNG + c + 1],
                                     bias=vecT[:, ROW_LNB + c:ROW_LNB + c + 1]).then_inc(silu_ok, 1)

            def moe(L):
                a = 3 * L + 1
                norm(a, ROW_FFN + 8 * L)
                act.wait_ge(ptr, L + 1)
                nc.scalar.copy(pT2, PS[:, 5, :].rearrange("p (c q) -> p c q", c=2)).then_inc(pT_ok, 1)
                act.wait_ge(rt_d, 2 * L + 1)
                nc.scalar.activation(eg, dg, ACT.Exp).then_inc(rt_e, 1)
                for n in range(2):
                    for t in range(NT):
                        act.wait_ge(pp_mm, 4 * L + 2 * n + t + 1)
                        nc.scalar.copy(pp[:, t, 512 * n:512 * (n + 1)], PS[:, 2 * n + t, :]).then_inc(pp_ok, 1)
                act.wait_ge(rt_d, 2 * L + 2)
                nc.scalar.activation(sm[:, 4, :], sm[:, 3, :], ACT.Exp).then_inc(rt_e, 1)
                act.wait_ge(rt_row, L + 1)
                nc.scalar.copy(wrow, PS[:, 7, :].rearrange("p (a q) -> p a q", a=2)).then_inc(row_act, 1)
                g0 = (NE + 1) * L
                act.wait_ge(ga_mm, g0 + 1)
                nc.scalar.copy(xg, PS[:, BGX, 0:Q4]).then_inc(xg_ok, 1)
                act.wait_ge(tab_ok, L + 1)
                with act.Fori(0, NE // 2) as it:
                    for s in range(2):
                        n = it * 2 + (s + NE * L + 1)
                        gi = it * 2 + (s + g0 + 2)
                        act.wait_ge(gu_mm, n)
                        nc.scalar.activation(gs[64:128, :], PS[0:64, BGU, 0:256], ACT.Silu).then_inc(sil_ok, 1)
                        act.wait_ge(ga_mm, gi)
                        nc.scalar.copy(xg, PS[:, BGX, 0:Q4]).then_inc(xg_ok, 1)
                        act.wait_ge(y_mm, n)
                        nc.scalar.copy(ysb, PS[:, BY, 0:Q4]).then_inc(y_ok, 1)
                        e = it * 2 + s
                        more = act.value_load(tab[0:1, 0, bass.ds(e, 1)], min_val=0, max_val=7)
                        before = act.value_load(tab[0:1, 1, bass.ds(e, 1)], min_val=0, max_val=64)
                        with act.If(more > 0):
                            with act.Fori(0, more) as r:
                                c = before + r + 1
                                act.wait_ge(X["x_ga"], c)
                                nc.scalar.copy(xg, PS[:, BGX, 0:Q4]).then_inc(X["x_xg"], 1)
                                act.wait_ge(X["x_gu"], c)
                                nc.scalar.activation(gs[64:128, :], PS[0:64, BGU, 0:256], ACT.Silu).then_inc(X["x_sil"], 1)
                                act.wait_ge(X["x_y"], c)
                                nc.scalar.copy(ysb, PS[:, BY, 0:Q4]).then_inc(X["x_ysb"], 1)
                act.wait_ge(slot_free, NE * (L + 1))
                for j in (1, 3):
                    nc.scalar.copy(h[:, :, Q4 * j:Q4 * (j + 1)],
                                   PS[:, ACC + j, :].rearrange("p (t q) -> p t q", t=2)).then_inc(h_act, 1)
                norm(a + 1, ROW_PLE + 8 * L)
                if L == 0:
                    act.wait_ge(trig_ok, 1)
                    nc.scalar.activation(trig, trig, ACT.Sin).then_inc(sin_ok, 1)
                    act.wait_ge(trig_ok, 2)
                    nc.scalar.activation(tcc[0:60, 0:64], tcc[0:60, 0:64], ACT.Sin).then_inc(sin_ok, 1)
                for n in range(2):
                    for t in range(NT):
                        b = 2 * n + t
                        act.wait_ge(pl_mm, 4 * L + b + 1)
                        nc.scalar.activation(hn[:, t, 512 * n:512 * (n + 1)], PS[:, b, :], ACT.Sigmoid).then_inc(pl_sig, 1)

            moe(0)
            norm(3, ROW_MIX + 8)
            for u in range(2):
                act.wait_ge(xp_mm, u + 1)
                nc.scalar.copy(xp[:, :, :, u, :], PS[:, u, :].rearrange("p (s g e) -> p s g e", s=2, g=4)).then_inc(xp_ok, 1)
            for s in range(2):
                for t in range(NT):
                    act.wait_ge(kv_dve, 2 * s + t + 1)
                    nc.scalar.copy(vv[:, t, s, :], PS[:, 2 + 2 * s + t, 256:512]).then_inc(kv_act, 1)
            act.wait_ge(gate_mm, 1)
            nc.scalar.activation(gt, PS[:, 6, 0:128].rearrange("p (t c) -> p t c", t=2)[:, :, 0:48], ACT.Sigmoid).then_inc(gate_ok, 1)
            def squares_and_root(i, t, lo, n):
                if i:
                    act.wait_ge(sq_used, i)
                nc.scalar.activation(sq[:, 0:64 * n].rearrange("p (m e) -> p m e", m=n), raw[:, t, lo:lo + n, :], ACT.Square).then_inc(sq_ok, 1)
                act.wait_ge(root_in, i + 2)
                nc.scalar.activation(ssn[:, 24:24 + n], ssn[:, 24:24 + n], ACT.Sqrt).then_inc(root_ok, 1)

            for t in range(NT):
                squares_and_root(t, t, 16, 8)
            for t in range(NT):
                for n in range(2):
                    act.wait_ge(q_mm, 2 * t + n + 1)
                    nc.scalar.copy(raw[:, t, 8 * n:8 * n + 8, :],
                                   PS[:, 2 + 2 * n + t, :].rearrange("p (m e) -> p m e", m=8)).then_inc(c_act, 1)
                    own[0] += 1
                act.wait_ge(c_act, own[0])
                squares_and_root(2 + t, t, 0, 16)
            for s in range(2):
                act.wait_ge(c1_x, s + 1)
                nc.scalar.activation(sq[0:60, 512:768], sq[0:60, 256:512], ACT.Sigmoid, scale=2.0 * float(np.sqrt(2.0 / np.pi))).then_inc(c1_s, 1)
                act.wait_ge(c1_t, s + 1)
                nc.scalar.copy(h1T[:, :, 0:60], PS[:, 0, 256:384].rearrange("p (c n) -> p c n", c=2)[:, :, 0:60]).then_inc(c1_T, 1)
            act.wait_ge(kc_mm, 2)
            act.wait_ge(const_ok, 1)
            for q in range(4):
                i = nc.scalar.copy(vcr[32 * q:32 * q + NC_, :, :], PS[32 * q:32 * q + NC_, 1, 256:512].rearrange("p (g e) -> p g e", g=4))
            i.then_inc(vcr_ok, 1)
            for b in (1, 3):
                act.wait_ge(qt_mm, b + 1)
                nc.scalar.copy(kT[:, b // 2, 2 * (b % 2):2 * (b % 2) + 2, :],
                               PS[:, 7, :].rearrange("p (k q) -> p k q", k=2)).then_inc(qt_act, 1)
            for b in (1, 3):
                act.wait_ge(qt_mm, 4 + b + 1)
                nc.scalar.copy(qT[:, 2 * b:2 * b + 2, :], PS[:, 2 + b, :].rearrange("p (k q) -> p k q", k=2)).then_inc(qt_act, 1)
            act.wait_ge(sc_d, 2)
            nc.scalar.activation(Pc[:, :, :, 0:NC_], Pc[:, :, :, 0:NC_], ACT.Exp, scale=SCALE).then_inc(sc_e, 1)

            def exps(hp):
                act.wait_ge(s_max, 8 * (hp + 1) + (hp + 1))
                if hp >= 2:
                    act.wait_ge(s_fac, hp - 1)
                for i_ in range(2):
                    for t in range(NT):
                        for s in range(2):
                            n = 4 * i_ + 2 * t + s
                            v = Pb[:, hp % 2, i_, 256 * t + 128 * (t + 1) * s:256 * t + 128 * (t + 1) * (s + 1)]
                            nc.scalar.activation(v, v, ACT.Exp, scale=SCALE, bias=nmx[:, hp % 2, n:n + 1],
                                                 accum_out=sme[:, hp % 2, n:n + 1]).then_inc(s_exp, 1)

            exps(0)
            for c in range(1):
                act.wait_ge(sct_mm, 1)
                nc.scalar.copy(PcT[:, 0:2, :], PS[:, 4, :].rearrange("p (k q) -> p k q", k=2)).then_inc(pct_ok, 1)
            for hp in range(8):
                if hp < 7:
                    exps(hp + 1)
                if hp >= 2:
                    act.wait_ge(o_mm, hp - 1)
                for b in (1, 2):
                    act.wait_ge(t_mm, 3 * hp + b + 1)
                    nc.scalar.copy(pT[:, hp % 2, 512 * b:512 * (b + 1)], PS[:, 4 + b, :]).then_inc(pt_act, 1)
                act.wait_ge(o_mm, hp + 1)
                nc.scalar.copy(OT[:, hp, :], PS[:, 7, 0:256]).then_inc(o_ok, 1)
            moe(1)

        @block.vector
        def _(dve):
            v = nc.vector
            own = [0]

            def link(i):
                own[0] += 1
                i.then_inc(c_dve, 1)
                dve.wait_ge(c_dve, own[0])

            def bc(ap, dims):
                return ap.broadcast_to(dims)

            def norm(a, row):
                if a > 0 and H_ACT[a]:
                    dve.wait_ge(h_act, H_ACT[a])
                if a > 0:
                    dve.wait_ge(h_dve, H_DVE[a])
                link(v.tensor_tensor_reduce(xnT[:, :, :].rearrange("p k q -> p (k q)")[:, 0:D], h[:, 0, :], h[:, 0, :], 1.0, 0.0,
                                            ALU.mult, ALU.add, rstd[:, 0, 0:1]))
                dve.wait_ge(ssq_ok, a + 1)
                v.tensor_scalar(rstd[:, 1, :], rstd[:, 0, :], 1.0 / D, EPS, ALU.mult, ALU.add).then_inc(var_ok, 1)
                dve.wait_ge(rs_ok, (1, 2, 3, 4, 6, 7)[a])
                v.tensor_scalar(hn[:, 0, :], h[:, 0, :], rstd[:, 1, 0:1], None, ALU.mult).then_inc(hn_dve, 1)
                if a == 0:
                    first_columns()
                for kp in (0, 2):
                    dve.wait_ge(tr_ok, 4 * a + kp + 1)
                    for k in (2 * kp, 2 * kp + 1):
                        v.tensor_scalar(xnT[:, k, :], PS[:, 4 + kp, 256 * (k % 2):256 * (k % 2 + 1)],
                                        vecT[:, row + k:row + k + 1], None, ALU.mult).then_inc(xt_dve, 1)

            def first_columns():
                dve.wait_ge(vtr, 1)
                v.tensor_copy(vecT[:, :], PS[:, 0, 0:NROWS]).then_inc(vec_ok, 1)
                dve.wait_ge(vtr, 2)
                v.tensor_copy(g8[:, :, :], PS[:, 1, 0:16].rearrange("p (c n) -> p c n", c=2)).then_inc(vec_ok, 1)
                dve.wait_ge(vtr, 3)
                v.tensor_copy(wdw, PS[:, 2, 0:8 * TAPS].rearrange("p (c w) -> p c w", c=8)).then_inc(vec_ok, 1)
                dve.wait_ge(vec_ok, 3)
                link(v.memset(cv0[:, :, 0:TAPS - 1], 0.0))

            dve.wait_ge(x_in, 16 * NT)
            norm(0, ROW_MIX)
            for c in range(KD):
                dve.wait_ge(sig_ok, c + 1)
                v.scalar_tensor_tensor(out=cv0[:, c, TAPS - 1:], in0=PS[:, c % 4, 0:T],
                                       scalar=vecT[:, ROW_BPW1 + c:ROW_BPW1 + c + 1], in1=sgm[c % 2],
                                       op0=ALU.add, op1=ALU.mult).then_inc(glu_ok, 1)
                dve.wait_ge(glu_ok, c + 1)
                if c == 0:
                    dve.wait_ge(tr_ok, 4)
                nv = TAPS - PE_TAPS - POOL_TAPS
                for w in range(nv):
                    o = cT[:, c, :] if w % 2 == 0 else accb[0]
                    u = cv0[:, c, w:w + T]
                    if w == 0:
                        i = v.tensor_scalar(o, u, wdw[:, c, w:w + 1], vecT[:, ROW_BDW + c:ROW_BDW + c + 1], ALU.mult, ALU.add)
                    elif w == 1:
                        i = v.tensor_scalar(o, u, wdw[:, c, w:w + 1], None, ALU.mult)
                    else:
                        i = v.scalar_tensor_tensor(out=o, in0=u, scalar=wdw[:, c, w:w + 1], in1=o, op0=ALU.mult, op1=ALU.add)
                    i.then_inc(c_dve, 1)
                    own[0] += 1
                    if w >= 1:
                        dve.wait_ge(c_dve, own[0] - 1)
                dve.wait_ge(tap_mm, c + 1)
                dve.wait_ge(ptap_ok, c + 1)
                link(v.tensor_tensor(accb[1], PS[:, 4 + c % 2, 0:T], pac[c % 2], ALU.add))
                link(v.tensor_tensor(cT[:, c, :], cT[:, c, :], accb[0], ALU.add))
                v.tensor_tensor(cT[:, c, :], cT[:, c, :], accb[1], ALU.add).then_inc(conv_ok, 1)
                dve.wait_ge(conv_ok, c + 1)
            dve.wait_ge(lnmm, 1)
            link(v.tensor_scalar(mu, PS[:, 6, 0:T], 1.0 / D, None, ALU.mult))
            for c in range(KD):
                v.tensor_tensor(cT[:, c, :], cT[:, c, :], mu, ALU.subtract).then_inc(ln_c, 1)
            dve.wait_ge(lnmm, 2)
            v.tensor_scalar(var, PS[:, 7, 0:T], 1.0 / D, EPS, ALU.mult, ALU.add).then_inc(root_in, 1)
            dve.wait_ge(root_ok, 1)
            link(v.reciprocal(var, var))
            dve.wait_ge(ln_c, KD)
            for c in range(KD):
                v.tensor_tensor(cT[:, c, :], cT[:, c, :], var, ALU.mult).then_inc(ln_r, 1)
            for n in range(2):
                for t in range(NT):
                    dve.wait_ge(out_mm, 2 * n + t + 1)
                    hs = h[:, t, 512 * n:512 * (n + 1)]
                    v.tensor_tensor(hs, PS[:, 2 * n + t, :], hs, ALU.add).then_inc(h_dve, 1)

            def first_of(vals, mx_, onehot, idx, n, d):
                link(v.tensor_reduce(mx_, vals, AX.X, ALU.max))
                link(v.tensor_tensor(d, vals, bc(mx_.unsqueeze(2), [P, 2, n]), ALU.subtract))
                link(v.tensor_scalar(onehot, d, 0.0, -BIGI, ALU.is_equal, ALU.mult))
                link(v.tensor_tensor(onehot, onehot, bc(iot[:, 0:n].unsqueeze(1), [P, 2, n]), ALU.add))
                link(v.tensor_reduce(idx, onehot, AX.X, ALU.min))
                link(v.tensor_tensor(onehot, onehot, bc(idx.unsqueeze(2), [P, 2, n]), ALU.is_equal))

            def xgT_copy(dst, L):
                gain = g8[:, :, 4 * L:4 * L + 4].rearrange("p c j -> p j c").unsqueeze(3)
                return v.tensor_tensor(dst.rearrange("p (j c) s -> p j c s", c=2),
                                       PS[:, BGX, Q4:Q4 + 256].rearrange("p (c j s) -> p j c s", c=2, j=4),
                                       bc(gain, [P, 4, 2, SLOTS]), ALU.mult)

            def hmul():
                return v.tensor_tensor(hh[64:128, :], PS[64:128, BGU, 0:256], gs[64:128, :], ALU.mult)

            def hT_copy():
                return v.tensor_copy(hT, PS[:, BHT, 0:128].rearrange("p (c s) -> p c s", c=2))

            def moe(L):
                a = 3 * L + 1
                norm(a, ROW_FFN + 8 * L)
                dve.wait_ge(rt_mm, L + 1)
                link(v.tensor_copy(R, PS[:, BGU, 0:128].rearrange("p (t e) -> p t e", t=2)[:, :, 0:36]))
                lg, le = R[:, :, 0:NG], R[:, :, NG:]
                link(v.tensor_reduce(sm[:, 0, :], lg, AX.X, ALU.max))
                v.tensor_tensor(dg, lg, bc(sm[:, 0, :].unsqueeze(2), [P, 2, NG]), ALU.subtract).then_inc(rt_d, 1)
                dve.wait_ge(rt_d, 2 * L + 1)
                link(v.tensor_scalar(og, dg, 0.0, -BIGI, ALU.is_equal, ALU.mult))
                link(v.tensor_tensor(og, og, bc(iot[:, 0:NG].unsqueeze(1), [P, 2, NG]), ALU.add))
                link(v.tensor_reduce(sm[:, 1, :], og, AX.X, ALU.min))
                link(v.tensor_tensor(og, og, bc(sm[:, 1, :].unsqueeze(2), [P, 2, NG]), ALU.is_equal))
                link(v.tensor_scalar(cg, og, -1.0, -NEG, ALU.add, ALU.mult))
                for t in range(NT):
                    grp = [P, NG, NEG_E]
                    link(v.tensor_tensor(lm[:, t, :].rearrange("p (g e) -> p g e", g=NG), le[:, t, :].rearrange("p (g e) -> p g e", g=NG),
                                         bc(og[:, t, :].unsqueeze(2), grp), ALU.mult))
                    link(v.tensor_tensor(lm[:, t, :].rearrange("p (g e) -> p g e", g=NG), lm[:, t, :].rearrange("p (g e) -> p g e", g=NG),
                                         bc(cg[:, t, :].unsqueeze(2), grp), ALU.add))
                first_of(lm, sm[:, 2, :], O1, sm[:, 5, :], NE, dd)
                link(v.scalar_tensor_tensor(out=lm, in0=O1, scalar=NEG, in1=lm, op0=ALU.mult, op1=ALU.add))
                first_of(lm, sm[:, 6, :], O2, sm[:, 7, :], NE, dd)
                v.tensor_tensor(Cc, O1, O2, ALU.add).then_inc(rt_c, 1)
                v.tensor_tensor(sm[:, 3, :], sm[:, 6, :], sm[:, 2, :], ALU.subtract).then_inc(rt_d, 1)
                dve.wait_ge(rt_e, 2 * L + 2)
                link(v.tensor_reduce(sm[:, 8, :], eg, AX.X, ALU.add))
                link(v.tensor_scalar(sm[:, 9, :], sm[:, 4, :], 1.0, None, ALU.add))
                link(v.tensor_tensor(sm[:, 8, :], sm[:, 8, :], sm[:, 9, :], ALU.mult))
                link(v.reciprocal(W4[:, :, 0], sm[:, 8, :]))
                link(v.tensor_tensor(W4[:, :, 1], W4[:, :, 0], sm[:, 4, :], ALU.mult))
                dve.wait_ge(rt_pf, L + 1)
                dve.wait_ge(rt_c, L + 1)
                pf = PS[:, 6, 0:64].rearrange("p (t e) -> p t e", t=2)
                for s, (O, ix) in enumerate(((O1, 5), (O2, 7))):
                    link(v.tensor_tensor(dd, pf, O, ALU.mult))
                    link(v.tensor_reduce(sm[:, 10, :], dd, AX.X, ALU.add))
                    link(v.tensor_scalar(sm[:, 11, :], sm[:, ix, :], BIGI, 256.0, ALU.add, ALU.mult))
                    link(v.tensor_tensor(S4[:, :, s], sm[:, 11, :], sm[:, 10, :], ALU.add))
                v.tensor_copy(cnt, PS[:, 6, 64:96]).then_inc(rt_s, 1)
                dve.wait_ge(rt_s, L + 1)
                link(v.tensor_scalar(ext, cnt, float(SLOTS), None, ALU.is_gt))
                for m in range(2, T // SLOTS):
                    link(v.scalar_tensor_tensor(out=ext, in0=cnt, scalar=float(SLOTS * m), in1=ext, op0=ALU.is_gt, op1=ALU.add))
                dve.wait_ge(rt_row, L + 1)
                v.tensor_copy(srow, PS[:, 5, :].rearrange("p (a q) -> p a q", a=2)).then_inc(row_dve, 1)
                link(v.tensor_copy(scn[:, 0, :], ext))
                b = 0
                for sh in (1, 2, 4, 8, 16):
                    link(v.tensor_copy(scn[:, 1 - b, 0:sh], scn[:, b, 0:sh]))
                    link(v.tensor_tensor(scn[:, 1 - b, sh:], scn[:, b, sh:], scn[:, b, 0:NE - sh], ALU.add))
                    b = 1 - b
                if L == 0:
                    link(v.tensor_copy(xtot[:, :], scn[:, b, NE - 1:NE]))
                else:
                    link(v.tensor_scalar(scn[:, b, :], scn[:, b, :], xtot[:, 0:1], None, ALU.add))
                link(v.tensor_tensor(scn[:, b, :], scn[:, b, :], ext, ALU.subtract))
                link(v.tensor_copy(tab[:, 0, :], ext))
                v.tensor_copy(tab[:, 1, :], scn[:, b, :]).then_inc(tab_ok, 1)
                dve.wait_ge(tab_ok, L + 1)
                g0 = (NE + 1) * L
                dve.wait_ge(xt_mm, g0 + 1)
                xgT_copy(xgT, L).then_inc(xgT_ok, 1)
                with dve.Fori(0, NE // 2) as it:
                    for s in range(2):
                        n = it * 2 + (s + NE * L + 1)
                        gi = it * 2 + (s + g0 + 2)
                        dve.wait_ge(sil_ok, n)
                        hmul().then_inc(h_ok, 1)
                        dve.wait_ge(ht_mm, n)
                        hT_copy().then_inc(hT_ok, 1)
                        dve.wait_ge(xt_mm, gi)
                        xgT_copy(xgT, L).then_inc(xgT_ok, 1)
                        e = it * 2 + s
                        more = dve.value_load(tab[0:1, 0, bass.ds(e, 1)], min_val=0, max_val=7)
                        before = dve.value_load(tab[0:1, 1, bass.ds(e, 1)], min_val=0, max_val=64)
                        with dve.If(more > 0):
                            with dve.Fori(0, more) as r:
                                c = before + r + 1
                                dve.wait_ge(X["x_xt"], c)
                                xgT_copy(xxgT, L).then_inc(X["x_xgT"], 1)
                                dve.wait_ge(X["x_sil"], c)
                                hmul().then_inc(X["x_h"], 1)
                                dve.wait_ge(X["x_ht"], c)
                                hT_copy().then_inc(X["x_hT"], 1)
                dve.wait_ge(slot_free, NE * (L + 1))
                for j in (0, 2):
                    v.tensor_copy(h[:, :, Q4 * j:Q4 * (j + 1)],
                                  PS[:, ACC + j, :].rearrange("p (t q) -> p t q", t=2)).then_inc(h_dve, 1)
                norm(a + 1, ROW_PLE + 8 * L)
                if L == 0:
                    trig_args()
                    all_tables()
                for n in range(2):
                    for t in range(NT):
                        b = 2 * n + t
                        dve.wait_ge(pl_sig, 4 * L + b + 1)
                        if b == 0:
                            dve.wait_ge(pp_ok, 4 * (L + 1))
                        gsl = hn[:, t, 512 * n:512 * (n + 1)]
                        hs = h[:, t, 512 * n:512 * (n + 1)]
                        v.tensor_tensor(gsl, gsl, pp[:, t, 512 * n:512 * (n + 1)], ALU.mult).then_inc(pl_mul, 1)
                        dve.wait_ge(pl_mul, 4 * L + b + 1)
                        v.tensor_tensor(hs, hs, gsl, ALU.add).then_inc(h_dve, 1)

            def reduce_angles(ang, k):
                link(v.tensor_scalar(k, k, MAGIC, None, ALU.add))
                link(v.tensor_scalar(k, k, MAGIC, None, ALU.subtract))
                for part in TWO_PI:
                    link(v.scalar_tensor_tensor(out=ang, in0=k, scalar=-part, in1=ang, op0=ALU.mult, op1=ALU.add))

            def trig_args():
                dve.wait_ge(misc_in, 16 * N_MISC)
                dve.wait_ge(att_in, 16 * N_ATT)
                link(v.tensor_copy(posf[:, 0:2], posi[:, 0:2]))
                link(v.tensor_copy(posf[0:60, 2:3], posi[0:60, 2:3]))
                tc2, kc2 = tcc[0:60, 0:64].rearrange("p (f e) -> p f e", f=2), tcc[0:60, 64:128].rearrange("p (f e) -> p f e", f=2)
                for rows, dst, k, pos in ((P, trig[:, 0], trk[:, 0], posf[:, 0:1]), (P, trig[:, 1], trk[:, 1], posf[:, 1:2]),
                                          (60, tc2, kc2, posf[0:60, 2:3])):
                    v.tensor_scalar(dst, bc(invb[0:rows, :].unsqueeze(1), [rows, 2, DH // 2]), pos, None, ALU.mult).then_inc(c_dve, 1)
                    own[0] += 1
                dve.wait_ge(c_dve, own[0])
                for dst, k in ((trig, trk), (tcc[0:60, 0:64], tcc[0:60, 64:128])):
                    four = len(dst.shape) == 4
                    cos_d, cos_k = (dst[:, :, 0, :], k[:, :, 0, :]) if four else (dst[:, 0:32], k[:, 0:32])
                    link(v.tensor_scalar(k, dst, float(1 / (2 * np.pi)), None, ALU.mult))
                    link(v.tensor_scalar(cos_k, cos_k, 0.25, None, ALU.add))
                    reduce_angles(dst, k)
                    link(v.tensor_scalar(cos_d, cos_d, float(np.pi / 2), None, ALU.add))
                    v.tensor_scalar(dst, dst, PI_LO, -PI_LO, ALU.min, ALU.max).then_inc(trig_ok, 1)

            def gain_tables(dst, tr, gains, n):
                def g(lo):
                    x = gains[:, lo:lo + 32]
                    return bc(x.unsqueeze(1), [P, n, 32]) if n else x
                for f, lo, gl in ((0, 0, 0), (0, 32, 32), (1, 32, 0)):
                    v.tensor_tensor(dst(f, lo), tr(f), g(gl), ALU.mult).then_inc(c_dve, 1)
                    own[0] += 1
                v.scalar_tensor_tensor(out=dst(1, 0), in0=tr(1), scalar=-1.0, in1=g(32), op0=ALU.mult, op1=ALU.mult).then_inc(c_dve, 1)
                own[0] += 1

            def all_tables():
                dve.wait_ge(sin_ok, 2)
                for m in range(3):
                    gain_tables(lambda f, lo: tcos[:, :, f, m, lo:lo + 32], lambda f: trig[:, :, f, :], gn[:, m, :], 2)
                gain_tables(lambda f, lo: tcc[0:60, 64 + 64 * f + lo:64 + 64 * f + lo + 32],
                            lambda f: tcc[0:60, 32 * f:32 * f + 32], gn[0:60, 3, :], 0)
                dve.wait_ge(c_dve, own[0])

            moe(0)

            norm(3, ROW_MIX + 8)
            ktab = tcc[0:60, 64:192].rearrange("p (f e) -> p f e", f=2)
            for s in range(2):
                for t in range(NT):
                    dve.wait_ge(kv_mm, 2 * s + t + 1)
                    v.tensor_copy(raw[:, t, 16 + 4 * s:20 + 4 * s, :],
                                  PS[:, 2 + 2 * s + t, 0:256].rearrange("p (m e) -> p m e", m=4)).then_inc(kv_dve, 1)
            dve.wait_ge(xpt_mm, 3)
            link(v.tensor_copy(peT, PS[:, 7, 0:32].rearrange("p (s j) -> p s j", s=2)))
            for s in range(2):
                v.tensor_copy(xpT[:, s, :, :], PS[:, s, :].rearrange("p (g m) -> p g m", g=4)).then_inc(xpt_ok, 1)
                dve.wait_ge(xpt_ok, s + 1)
                for b in range(2):
                    x3 = xpT[:, s, :, 8 * b:8 * b + 8 * NC_].rearrange("p g (n j) -> p j g n", j=8)
                    i = v.tensor_tensor(Bc[:, s, 8 * b:8 * b + 8, :, :], x3,
                                        bc(peT[:, s, 8 * b:8 * b + 8].unsqueeze(2).unsqueeze(3), [P, 8, NKV, NC_]), ALU.add)
                i.then_inc(B_ok, 1)

            for i_, (t, lo, n) in enumerate(((0, 16, 8), (1, 16, 8), (0, 0, 16), (1, 0, 16))):
                dve.wait_ge(sq_ok, i_ + 1)
                v.tensor_reduce(ssn[:, 0:n], sq[:, 0:64 * n].rearrange("p (m e) -> p m e", m=n), AX.X, ALU.add).then_inc(sq_used, 1)
                dve.wait_ge(sq_used, i_ + 1)
                v.tensor_scalar(ssn[:, 24:24 + n], ssn[:, 0:n], 1.0 / DH, EPS, ALU.mult, ALU.add).then_inc(root_in, 1)
                dve.wait_ge(root_ok, i_ + 2)
                link(v.reciprocal(ssn[:, 24:24 + n], ssn[:, 24:24 + n]))
                x_ = raw[:, t, lo:lo + n, :]
                link(v.tensor_tensor(x_, x_, bc(ssn[:, 24:24 + n].unsqueeze(2), [P, n, 64]), ALU.mult))
                for m, lo2, nn in (((0, 0, 16),) if lo == 0 else ((1, 16, 4), (2, 20, 4))):
                    x_ = raw[:, t, lo2:lo2 + nn, :]
                    tA = bc(tcos[:, t, 0, m, :].unsqueeze(1), [P, nn, 64])
                    dst = rotq[:, t, :, :] if m == 0 else rotk[:, t, 4 * (m - 1):4 * m, 0, :]
                    tmp = rot_tmp[:, 0:64 * nn].rearrange("p (m e) -> p m e", m=nn)
                    v.tensor_tensor(dst, x_, tA, ALU.mult).then_inc(c_dve, 1)
                    for f in range(2):
                        i = v.tensor_tensor(tmp[:, :, 32 * f:32 * f + 32], x_[:, :, 32 * (1 - f):32 * (1 - f) + 32],
                                            bc(tcos[:, t, 1, m, 32 * f:32 * f + 32].unsqueeze(1), [P, nn, 32]), ALU.mult)
                        i.then_inc(c_dve, 1)
                    own[0] += 3
                    dve.wait_ge(c_dve, own[0])
                    if m > 0:
                        link(v.tensor_tensor(rotk[:, t, 4 * (m - 1):4 * m, 1, :], dst, tmp, ALU.add))
                    link(v.tensor_tensor(dst, dst, tmp, ALU.add))
                if lo == 0:
                    v.memset(mcol[:, 3 + t:4 + t], 0.0).then_inc(rot_ok, 1)
                elif t == 1:
                    v.memset(mcol[:, 5:6], 0.0).then_inc(rot_ok, 1)

            for s in range(2):
                dve.wait_ge(c1_mm, s + 1)
                xx, t1, sg = sq[0:60, 0:256], sq[0:60, 256:512], sq[0:60, 512:768]
                link(v.tensor_copy(xx, PS[0:60, s, 0:256]))
                link(v.tensor_tensor(t1, xx, xx, ALU.mult))
                link(v.tensor_scalar(t1, t1, 0.044715, 1.0, ALU.mult, ALU.add))
                v.tensor_tensor(t1, t1, xx, ALU.mult).then_inc(c1_x, 1)
                dve.wait_ge(c1_s, s + 1)
                v.tensor_tensor(h1v[s][0:60, :], xx, sg, ALU.mult).then_inc(c1_g, 1)
                if s == 0:
                    dve.wait_ge(kc_mm, 1)
                    link(v.tensor_copy(kcx[0:60, 0, :], PS[0:60, 0, 0:64]))
                    v.tensor_copy(kcx[0:60, 1, :], kcx[0:60, 0, :]).then_inc(kc_x, 1)
                    dve.wait_ge(kc_x, 1)
                    link(v.tensor_tensor(kcx[0:60, 1, :], kcx[0:60, 0, :], kcx[0:60, 0, :], ALU.mult))
                    link(v.tensor_reduce(mcol[0:60, 0:1], kcx[0:60, 1, :], AX.X, ALU.add))
                    v.tensor_scalar(mcol[0:60, 1:2], mcol[0:60, 0:1], 1.0 / DH, EPS, ALU.mult, ALU.add).then_inc(var_ok, 1)
                    dve.wait_ge(rs_ok, 5)
                    link(v.tensor_scalar(kcx[0:60, 0, :], kcx[0:60, 0, :], mcol[0:60, 1:2], None, ALU.mult))
                    link(v.tensor_tensor(kcx[0:60, 2, :], kcx[0:60, 0, :], ktab[:, 0, :], ALU.mult))
                    for f in range(2):
                        link(v.tensor_tensor(kcx[0:60, 1, 32 * f:32 * f + 32], kcx[0:60, 0, 32 * (1 - f):32 * (1 - f) + 32],
                                             ktab[:, 1, 32 * f:32 * f + 32], ALU.mult))
                    link(v.tensor_tensor(kcx[0:60, 3, :], kcx[0:60, 2, :], kcx[0:60, 1, :], ALU.add))
                    v.tensor_tensor(kcx[0:60, 2, :], kcx[0:60, 2, :], kcx[0:60, 1, :], ALU.add).then_inc(kc_x, 1)
                    dve.wait_ge(kc_x, 2)
            for b in (0, 2):
                dve.wait_ge(qt_mm, b + 1)
                v.tensor_copy(kT[:, b // 2, 2 * (b % 2):2 * (b % 2) + 2, :],
                              PS[:, 6, :].rearrange("p (k q) -> p k q", k=2)).then_inc(qt_dve, 1)
            for b in (0, 2):
                dve.wait_ge(qt_mm, 4 + b + 1)
                v.tensor_copy(qT[:, 2 * b:2 * b + 2, :], PS[:, 2 + b, :].rearrange("p (k q) -> p k q", k=2)).then_inc(qt_dve, 1)
            dve.wait_ge(kct_mm, 1)
            v.tensor_copy(kcT, PS[:, 0, 384:444]).then_inc(kcT_ok, 1)
            dve.wait_ge(sc_mm, 1)
            dve.wait_ge(mask_ok, 1)
            link(v.memset(Pc[:, :, :, NC_:], 0.0))
            for i_ in range(2):
                for t in range(NT):
                    i = v.tensor_tensor(Pc[:, t, i_::2, 0:NC_], PS[:, i_, 128 * t:128 * (t + 1)].rearrange("p (m n) -> p m n", m=8)[:, :, 0:NC_],
                                        bc(mka[:, t, :].unsqueeze(1), [P, 8, NC_]), ALU.add)
            i.then_inc(sc_d, 1)
            dve.wait_ge(sc_d, 1)
            pc3 = Pc.rearrange("p t n e -> p (t n) e")[:, :, 0:NC_]
            link(v.tensor_reduce(cst[:, 0, :], pc3, AX.X, ALU.max))
            v.tensor_tensor(pc3, pc3, bc(cst[:, 0, :].unsqueeze(2), [P, 32, NC_]), ALU.subtract).then_inc(sc_d, 1)

            def maxes(hp):
                dve.wait_ge(s_mm, hp + 1)
                if hp >= 2:
                    dve.wait_ge(t_mm, 3 * (hp - 1))
                for i_ in range(2):
                    for t in range(NT):
                        for s in range(2):
                            n = 4 * i_ + 2 * t + s
                            w = 128 * (t + 1)
                            mk = cmask[:, 1, :] if t == 0 else cmask[:, :, :].rearrange("p a b -> p (a b)")
                            v.tensor_tensor_reduce(Pb[:, hp % 2, i_, 256 * t + w * s:256 * t + w * (s + 1)],
                                                   PS[:, 2 * t + i_, w * s:w * (s + 1)], mk, 1.0, NEG, ALU.add, ALU.max,
                                                   mx[:, hp % 2, n:n + 1]).then_inc(s_max, 1)
                dve.wait_ge(s_max, 9 * hp + 8)
                v.tensor_scalar(nmx[:, hp % 2, :], mx[:, hp % 2, :], -SCALE, None, ALU.mult).then_inc(s_max, 1)

            def factors(hp):
                dve.wait_ge(s_exp, 8 * (hp + 1))
                if hp == 0:
                    dve.wait_ge(gate_ok, 1)
                link(v.reciprocal(sme[:, hp % 2, :], sme[:, hp % 2, :]))
                for i_ in range(2):
                    hd = 2 * hp + i_
                    i = v.tensor_tensor(fac[:, hp % 2, 4 * i_:4 * i_ + 4].rearrange("p (t s) -> p t s", t=2),
                                        sme[:, hp % 2, 4 * i_:4 * i_ + 4].rearrange("p (t s) -> p t s", t=2),
                                        gt[:, :, 3 * hd + 1:3 * hd + 3], ALU.mult)
                i.then_inc(s_fac, 1)
                dve.wait_ge(s_fac, hp + 1)
                for i_ in range(2):
                    for t in range(2 - i_):
                        for s in range(2):
                            n = 4 * i_ + 2 * t + s
                            x_ = Pb[:, hp % 2, i_, 256 * t + 128 * (t + 1) * s:256 * t + 128 * (t + 1) * (s + 1)]
                            i = v.tensor_scalar(x_, x_, fac[:, hp % 2, n:n + 1], None, ALU.mult)
                i.then_inc(s_sclv, 1)

            maxes(0)
            dve.wait_ge(sc_e, 1)
            link(v.tensor_reduce(cst[:, 1, :], pc3, AX.X, ALU.add))
            link(v.reciprocal(cst[:, 2, :], cst[:, 1, :]))
            dve.wait_ge(gate_ok, 1)
            link(v.tensor_tensor(cst[:, 2, :].rearrange("p (t n) -> p t n", t=2), cst[:, 2, :].rearrange("p (t n) -> p t n", t=2),
                                 gt.rearrange("p t (n b) -> p t n b", b=3)[:, :, :, 0], ALU.mult))
            link(v.tensor_tensor(pc3, pc3, bc(cst[:, 2, :].unsqueeze(2), [P, 32, NC_]), ALU.mult))
            v.tensor_tensor(Pc[:, :, :, 0:NC_], Pc[:, :, :, 0:NC_], bc(mk1.unsqueeze(2), [P, 2, 16, NC_]), ALU.mult).then_inc(sc_p, 1)
            factors(0)
            dve.wait_ge(sct_mm, 1)
            v.tensor_copy(PcT[:, 2:4, :], PS[:, 5, :].rearrange("p (k q) -> p k q", k=2)).then_inc(pct_ok, 1)
            for hp in range(8):
                if hp < 7:
                    maxes(hp + 1)
                dve.wait_ge(t_mm, 3 * hp + 1)
                if hp >= 2:
                    dve.wait_ge(o_mm, hp - 1)
                v.tensor_copy(pT[:, hp % 2, 0:512], PS[:, 4, :]).then_inc(pt_dve, 1)
                if hp < 7:
                    factors(hp + 1)
            for n in range(2):
                for t in range(NT):
                    dve.wait_ge(out_mm, 4 + 2 * n + t + 1)
                    hs = h[:, t, 512 * n:512 * (n + 1)]
                    v.tensor_tensor(hs, PS[:, 2 * n + t, :], hs, ALU.add).then_inc(h_dve, 1)
            moe(1)


_INS = ['x', 'p', 'positions', 'g_mix', 'g_ffn', 'g_ple', 'conv_w_pw1', 'conv_b_pw1', 'conv_w_dw', 'conv_b_dw',
        'conv_ln_g', 'conv_ln_b', 'conv_w_pw2', 'conv_b_pw2', 'nsa_w_in', 'nsa_q_norm', 'nsa_k_norm',
        'nsa_cmp_pe', 'nsa_cmp_w1', 'nsa_cmp_w2', 'nsa_w_out', 'moe_w_rg', 'moe_b_rg', 'moe_w_re', 'moe_b_re',
        'moe_w_gate', 'moe_w_up', 'moe_w_down', 'ple_w_proj', 'ple_w_gate']


def kernel(**inputs):
    import numpy as _np
    import concourse.bacc as _bacc
    from concourse import mybir as _mybir
    from concourse.bass_utils import run_bass_kernel_spmd as _run

    nc = _bacc.Bacc("TRN2", target_bir_lowering=False, num_devices=1)
    arrays, args = {}, []
    given = {name: _np.ascontiguousarray(inputs[name]) for name in _INS}
    half = DH // 2
    given["inv_freq"] = (1.0 / (ROPE_THETA ** (_np.arange(half, dtype=_np.float32) / half))).astype(_np.float32)[None, :]
    for name, a in given.items():
        arrays[f"in_{name}"] = a
        args.append(nc.dram_tensor(f"in_{name}", a.shape, _mybir.dt.from_np(a.dtype), kind="ExternalInput").ap())
    args.append(nc.dram_tensor("out_h", (1, T, D), F32, kind="ExternalOutput").ap())
    build(nc, *args)
    return _run(nc, [arrays], core_ids=[0]).results[0]["out_h"]
```

```python
from contextlib import ExitStack

import numpy as np

import concourse.bass as bass
from concourse import mybir

ALU = mybir.AluOpType
ACT = mybir.ActivationFunctionType
F32 = mybir.dt.float32
I32 = mybir.dt.int32
AX = mybir.AxisListType

P = 128
DEPTH = 2
D = 1024
T = 256
NT = T // P
KD = D // P
TAPS = 31
HEADS, DH, NKV = 16, 64, 4
CMP_STRIDE, CMP_BLOCK, CMP_HID = 16, 32, 256
NC_ = T // CMP_STRIDE - 1
NG, NE, NEG_E = 4, 32, 8
F = 512
SLOTS = 32
Q4 = D // 4
EPS = 1e-6
NEG = -1e30
BIGI = 1000.0
MAGIC = 12582912.0
TWO_PI = (6.28125, 1.9350051879882812e-3, 3.0199159819567e-7)
PI_LO = 3.1415925
PW1_PARTS = ((0, 1), (1, 2), (2, 4), (4, 8))
PE_TAPS, POOL_TAPS = 6, 5
N_VEC, N_MISC, N_ATT = 10, 8 + 6, 8
SCALE = DH ** -0.5
ROPE_THETA = 10000.0

ACC = 0
BGU, BGX, BHT, BY = 4, 5, 6, 7

H_DVE = [0, 4, 6, 10, 14, 16, 20]
H_ACT = [0, 0, 2, 2, 2, 4, 4]
RS_BEFORE = [0, 2, 4, 6, 9, 11]
ROW_MIX, ROW_FFN, ROW_PLE, ROW_BPW1, ROW_BDW, ROW_LNG, ROW_LNB, NROWS = 0, 16, 32, 48, 64, 72, 80, 88


def build(nc, x, p, positions, g_mix, g_ffn, g_ple, conv_w_pw1, conv_b_pw1, conv_w_dw, conv_b_dw,
          conv_ln_g, conv_ln_b, conv_w_pw2, conv_b_pw2, nsa_w_in, nsa_q_norm, nsa_k_norm,
          nsa_cmp_pe, nsa_cmp_w1, nsa_cmp_w2, nsa_w_out, moe_w_rg, moe_b_rg, moe_w_re, moe_b_re,
          moe_w_gate, moe_w_up, moe_w_down, ple_w_proj, ple_w_gate, inv_freq, out):
    with ExitStack() as ctx:
        def sb(name, shape, dt=F32):
            return ctx.enter_context(nc.sbuf_tensor(name, shape, dt))

        def sem(name):
            return ctx.enter_context(nc.semaphore(name))

        PS = ctx.enter_context(nc.psum_tensor("PS", [P, 8, 512], F32))

        ring = sb("ring", [P, 2, 12288])
        wb = sb("wb", [P, 3, 4096])
        h = sb("h", [P, NT, D])
        hn = sb("hn", [P, NT, D])
        xnT = sb("xnT", [P, KD, T])
        ppw = sb("ppw", [P, 4096])
        ident = sb("ident", [P, P])
        ones = sb("ones", [P, P])
        upper = sb("upper", [P, P])
        cmask = sb("cmask", [P, 2, P])
        vecT = sb("vecT", [P, NROWS])
        g8 = sb("g8", [P, 2, 8])
        wr = sb("wr", [P, DEPTH, KD, NG + NE])
        rowb = sb("rowb", [1, DEPTH * (NG + NE)])
        rstd = sb("rstd", [P, 2, NT])
        iot = sb("iot", [P, 32])
        ioti = sb("ioti", [P, 32], I32)
        nhalf = sb("nhalf", [P, 1])
        colp = sb("colp", [P, 1])
        xtot = sb("xtot", [P, 1])
        tab = sb("tab", [P, 2, NE], I32)
        A = sb("arena", [P, 4480])

        off = [0]

        def carve(n):
            a = off[0]
            off[0] += n
            assert off[0] <= 4480, off[0]
            return A[:, a:a + n]

        srow = carve(512).rearrange("p (a t) -> p a t", a=2)
        wrow = carve(512).rearrange("p (a t) -> p a t", a=2)
        eqr = carve(512).rearrange("p (a t) -> p a t", a=2)
        wT = [carve(256) for _ in range(2)]
        eq4 = carve(128).rearrange("p (t a s) -> p t a s", t=2, a=2)
        sel = [carve(64).rearrange("p (t s) -> p t s", t=2) for _ in range(2)]
        cur32 = carve(32)
        curc = carve(1)
        xcur32 = carve(32)
        xcurc = carve(1)
        xg = carve(256)
        xgT = carve(256).rearrange("p (k s) -> p k s", k=8)
        xfree = [off[0], 0]
        xsel = carve(64).rearrange("p (t s) -> p t s", t=2)
        xwT = carve(256)
        xxgT = carve(256).rearrange("p (k s) -> p k s", k=8)
        xfree[1] = off[0]
        gs = carve(256)
        hh = carve(256)
        hT = carve(128).rearrange("p (c s) -> p c s", c=2)
        ysb = carve(256)
        S4 = carve(4).rearrange("p (t a) -> p t a", t=2)
        W4 = carve(4).rearrange("p (t a) -> p t a", t=2)
        scn = carve(64).rearrange("p (n e) -> p n e", n=2)
        rt_mem, rt_off = A[:, xfree[0]:xfree[1]], [0]

        def rt(n):
            rt_off[0] += n
            assert rt_off[0] <= xfree[1] - xfree[0]
            return rt_mem[:, rt_off[0] - n:rt_off[0]]

        R = rt(72).rearrange("p (t e) -> p t e", t=2)
        dg = rt(8).rearrange("p (t e) -> p t e", t=2)
        eg = rt(8).rearrange("p (t e) -> p t e", t=2)
        cg = rt(8).rearrange("p (t e) -> p t e", t=2)
        og = rt(8).rearrange("p (t e) -> p t e", t=2)
        lm = rt(64).rearrange("p (t e) -> p t e", t=2)
        dd = rt(64).rearrange("p (t e) -> p t e", t=2)
        O1 = rt(64).rearrange("p (t e) -> p t e", t=2)
        O2 = rt(64).rearrange("p (t e) -> p t e", t=2)
        Cc = rt(64).rearrange("p (t e) -> p t e", t=2)
        cnt = rt(32)
        ext = rt(32)
        sm = rt(32).rearrange("p (n t) -> p n t", t=2)

        off[0] = 0
        sq = ppw[:, 0:1536]
        wgate3 = ppw[:, 1536:1920].rearrange("p (k c) -> p k c", k=KD)
        rot_tmp = ppw[:, 2048:3072]
        tcos = ppw[:, 3072:3840].rearrange("p (t f m e) -> p t f m e", t=2, f=2, m=3)
        gn = ppw[:, 3840:4096].rearrange("p (m e) -> p m e", m=4)
        invb = carve(DH // 2)
        trig = carve(128).rearrange("p (t f e) -> p t f e", t=2, f=2)
        trk = carve(128).rearrange("p (t f e) -> p t f e", t=2, f=2)
        kcB = carve(128).rearrange("p (g u n) -> p g u n", g=NKV, u=2)
        posf = carve(4)
        gt = carve(96).rearrange("p (t c) -> p t c", t=2)
        ssn = carve(48)
        mx = carve(2 * 8).rearrange("p (b n) -> p b n", b=2)
        nmx = carve(2 * 8).rearrange("p (b n) -> p b n", b=2)
        sme = carve(2 * 8).rearrange("p (b n) -> p b n", b=2)
        fac = carve(2 * 8).rearrange("p (b n) -> p b n", b=2)
        cst = carve(32 * 3).rearrange("p (n m) -> p n m", n=3)
        mka = carve(2 * NC_).rearrange("p (t n) -> p t n", t=2)
        mk1 = carve(2 * NC_).rearrange("p (t n) -> p t n", t=2)
        pei = carve(256).rearrange("p (s c) -> p s c", s=2)
        peT = carve(32).rearrange("p (s j) -> p s j", s=2)
        h1v = [sq[:, 768:1024], sq[:, 1024:1280]]
        vcr = carve(256).rearrange("p (g e) -> p g e", g=4)
        w2c = carve(256).rearrange("p (s c e) -> p s c e", s=2, c=2)
        h1T = carve(2 * 128).rearrange("p (c n) -> p c n", c=2)
        kcx = carve(64 * 4).rearrange("p (n e) -> p n e", n=4)
        tcc = carve(128 + 64 * 3)
        mcol = carve(8)
        off[0] = 0
        sgm = [carve(256) for _ in range(2)]
        prow = carve(512)
        mu, var = prow[:, 0:256], prow[:, 256:512]
        wdw = carve(8 * TAPS).rearrange("p (c w) -> p c w", c=8)
        accb = [carve(256) for _ in range(2)]
        dgb = carve(2 * PE_TAPS * P).rearrange("p (b i q) -> p b i q", b=2, i=PE_TAPS)
        pac = [ppw[:, 2304:2560], ppw[:, 2560:2816]]
        ptm = ppw[:, 2816:3072]
        bpw2 = carve(1024)[0:1, :]
        wdw_rows = ppw[0:TAPS, 3072:4096]

        posi = sb("posi", [P, 4], I32)
        pp = ppw[:, 0:2048].rearrange("p (t d) -> p t d", t=NT)
        wproj = ppw[:, 2048:4096].rearrange("p (c d) -> p c d", c=2)
        pin = ppw[:, 0:512].rearrange("p (t d) -> p t d", t=NT)
        pT2 = eqr

        def w_gu(s):
            return ring[:, s, 0:8192].rearrange("p (g k f) -> p g k f", g=2, k=8)

        def w_dn(s):
            return ring[:, s, 8192:12288].rearrange("p (f c d) -> p f c d", f=2, c=2)

        def dense(buf):
            return buf.rearrange("p (k n) -> p k n", k=KD)

        WB = [wb[:, i, :] for i in range(3)]
        R0 = [ring[:, 0, 4096 * i:4096 * (i + 1)] for i in range(3)]
        R1 = [ring[:, 1, 4096 * i:4096 * (i + 1)] for i in range(3)]
        PW1 = [WB[0], WB[1], WB[2], R1[0]]
        PW2 = [R1[1], R1[2]]
        w_last = WB[1].rearrange("p (k f) -> p k f", k=8)
        cv0 = ppw[:, 0:KD * (T + TAPS - 1)].rearrange("p (k q) -> p k q", k=KD)
        cT = hn[:, :, :].rearrange("p t (k q) -> p (t k) q", q=T)

        S = ring[:, 1, :]
        raw = S[:, 0:3072].rearrange("p (t n e) -> p t n e", t=2, n=24)
        rotq = S[:, 3072:5120].rearrange("p (t n e) -> p t n e", t=2, n=16)
        rotk = S[:, 5120:7168].rearrange("p (t m u e) -> p t m u e", t=2, m=8, u=2)
        vv = S[:, 7168:8192].rearrange("p (t s e) -> p t s e", t=2, s=2)
        xp = S[:, 8192:9216].rearrange("p (s g u e) -> p s g u e", s=2, g=4, u=2)
        xpT = S[:, 9216:10240].rearrange("p (s g m) -> p s g m", s=2, g=4)
        Bc = S[:, 10240:12160].rearrange("p (s j g n) -> p s j g n", s=2, j=16, g=4)
        OT = S[:, 0:2048].rearrange("p (k q) -> p k q", k=8)
        Pc = ppw[:, 3072:4096].rearrange("p (t n e) -> p t n e", t=2, n=16)
        pT = S[:, 3072:6144].rearrange("p (b n) -> p b n", b=2)
        Pb = ppw[:, 0:3072].rearrange("p (b i n) -> p b i n", b=2, i=2)
        PcT = S[:, 6144:7168].rearrange("p (c q) -> p c q", c=4)
        qT = hn[:, :, :].rearrange("p t (k q) -> p (t k) q", q=T)
        kT = xnT[:, :, :].rearrange("p (s g) q -> p s g q", s=2)

        x_in, vec_in, misc_in, p_in = sem("x_in"), sem("vec_in"), sem("misc_in"), sem("p_in")
        pw1_in = [sem(f"pw1_in{i}") for i in range(4)]
        w2_in = [sem(f"w2_in{i}") for i in range(2)]
        ple_in = [sem(f"ple_in{i}") for i in range(2)]
        proj_in = sem("proj_in")
        att_in, gate_in, mask_ok, c_bld = sem("att_in"), sem("gate_in"), sem("mask_ok"), sem("c_bld")
        tap_mm, dg_ok, ptap_ok, root_in, root_ok = sem("tap_mm"), sem("dg_ok"), sem("ptap_ok"), sem("root_in"), sem("root_ok")
        x_bld = sem("x_bld")
        pe_step, pool_step = sem("pe_step"), sem("pool_step")
        in_in = [sem(f"in_in{i}") for i in range(5)]
        gu_in = [sem(f"gu_in{i}") for i in range(2)]
        last_in = sem("last_in")
        dn_in = [sem(f"dn_in{i}") for i in range(2)]
        out_st = sem("out_st")
        c_pool, c_dve, c_act = sem("c_pool"), sem("c_dve"), sem("c_act")
        const_ok = sem("const_ok")
        vtr, vec_ok = sem("vtr"), sem("vec_ok")
        h_dve, h_act = sem("h_dve"), sem("h_act")
        ssq_ok, var_ok, rs_ok, hn_dve, hn_act, tr_ok = sem("ssq_ok"), sem("var_ok"), sem("rs_ok"), sem("hn_dve"), sem("hn_act"), sem("tr_ok")
        xt_dve, xt_act = sem("xt_dve"), sem("xt_act")
        pw1_mm, sig_ok, glu_ok, conv_ok, lnmm, ln_c, ln_sq, ln_r, silu_ok, out_mm = [
            sem(s) for s in ("pw1_mm", "sig_ok", "glu_ok", "conv_ok", "lnmm", "ln_c", "ln_sq",
                             "ln_r", "silu_ok", "out_mm")]
        ptr, pT_ok, pp_mm, pp_ok = sem("ptr"), sem("pT_ok"), sem("pp_mm"), sem("pp_ok")
        rt_mm, rt_d, rt_e, rt_c, rt_pf, rt_s, rt_row, row_dve, row_act, tab_ok = [
            sem(s) for s in ("rt_mm", "rt_d", "rt_e", "rt_c", "rt_pf", "rt_s", "rt_row", "row_dve",
                             "row_act", "tab_ok")]
        sel_ok, wT_ok, wT_free = sem("sel_ok"), sem("wT_ok"), sem("wT_free")
        ga_mm, xg_ok, xt_mm, xgT_ok = sem("ga_mm"), sem("xg_ok"), sem("xt_mm"), sem("xgT_ok")
        gu_mm, sil_ok, h_ok, ht_mm, hT_ok, y_mm, y_ok = [
            sem(s) for s in ("gu_mm", "sil_ok", "h_ok", "ht_mm", "hT_ok", "y_mm", "y_ok")]
        slot_free = sem("slot_free")
        XN = ("x_sel", "x_ga", "x_xg", "x_xt", "x_xgT", "x_gu", "x_sil", "x_h", "x_ht", "x_hT", "x_y", "x_ysb", "x_done", "x_wT")
        X = {n: sem(n) for n in XN}
        pl_mm, pl_sig, pl_mul = sem("pl_mm"), sem("pl_sig"), sem("pl_mul")
        xp_mm, xp_ok, xpt_mm, xpt_ok, B_ok = sem("xp_mm"), sem("xp_ok"), sem("xpt_mm"), sem("xpt_ok"), sem("B_ok")
        kv_mm, kv_dve, kv_act, gate_mm, gate_ok, q_mm = (sem("kv_mm"), sem("kv_dve"), sem("kv_act"), sem("gate_mm"),
                                                         sem("gate_ok"), sem("q_mm"))
        trig_ok, sin_ok = sem("trig_ok"), sem("sin_ok")
        sq_ok, sq_used, rot_ok = sem("sq_ok"), sem("sq_used"), sem("rot_ok")
        s_sclv = sem("s_sclv")
        c1_mm, c1_x, c1_s, c1_g, c1_t, c1_T, kc_mm, kc_x, kct_mm, kcT_ok, vcr_ok = [
            sem(s) for s in ("c1_mm", "c1_x", "c1_s", "c1_g", "c1_t", "c1_T", "kc_mm", "kc_x", "kct_mm",
                             "kcT_ok", "vcr_ok")]
        qt_mm, qt_act = sem("qt_mm"), sem("qt_act")
        sc_mm, sc_d, sc_e, sc_p, sct_mm, pct_ok = (sem("sc_mm"), sem("sc_d"), sem("sc_e"), sem("sc_p"),
                                                   sem("sct_mm"), sem("pct_ok"))
        s_mm, s_max, s_exp, s_fac, s_scl, t_mm, pt_dve, pt_act, o_mm, o_ok = [
            sem(s) for s in ("s_mm", "s_max", "s_exp", "s_fac", "s_scl", "t_mm", "pt_dve", "pt_act", "o_mm",
                             "o_ok")]

        block = ctx.enter_context(nc.Block())

        @block.sync
        def _(sp):
            def cols(w, n):
                return w.rearrange("(k p) n -> p k n", p=P)[:, :, 512 * n:512 * (n + 1)]

            def gate_up_load(L, e, to, g, done):
                sp.dma_start(to.rearrange("p (j r) -> p j r", j=4),
                             (moe_w_gate, moe_w_up)[g][L, e].rearrange("(j p c) f -> p j (c f)", j=4, c=2)).then_inc(done, 16)

            def down_load(L, e, to, done):
                sp.dma_start(to.rearrange("p (f r) -> p f r", f=2),
                             moe_w_down[L, e].rearrange("(f p c) d -> p f (c d)", f=2, c=2)).then_inc(done, 16)

            def expert(L, e, s):
                for g in range(2):
                    gate_up_load(L, e, ring[:, s, 4096 * g:4096 * (g + 1)], g, gu_in[s])
                down_load(L, e, ring[:, s, 8192:12288], dn_in[s])

            def experts(L):
                with sp.Fori(1, NE // 2 - L) as it:
                    for s in range(2):
                        sp.wait_ge(slot_free, it * 2 + (s - 1 + NE * L))
                        expert(L, it * 2 + s, s)
                if L == 1:
                    sp.wait_ge(slot_free, NE + NE - 3)
                    expert(1, NE - 2, 0)
                    sp.wait_ge(slot_free, NE + NE - 2)
                    gate_up_load(1, NE - 1, R1[1], 1, gu_in[1])
                    down_load(1, NE - 1, R1[2], dn_in[1])

            def embeddings(L):
                sp.dma_start(pin, p[L, 0].rearrange("(t q) d -> q t d", q=P)).then_inc(p_in, 16)
                sp.dma_start(wproj, ple_w_proj[L].rearrange("(c p) d -> p c d", p=P)).then_inc(proj_in, 16)

            for t in range(NT):
                sp.dma_start(h[:, t, :], x[0, t * P:(t + 1) * P, :]).then_inc(x_in, 16)
            for r, v in ((ROW_MIX, g_mix), (ROW_FFN, g_ffn), (ROW_PLE, g_ple), (ROW_BPW1, conv_b_pw1),
                         (ROW_BDW, conv_b_dw), (ROW_LNG, conv_ln_g), (ROW_LNB, conv_ln_b)):
                rows = v.shape[0] * v.shape[1] // P
                sp.dma_start(prow[r:r + rows, 0:P], v.rearrange("l (r c) -> (l r) c", c=P)).then_inc(vec_in, 16)
            sp.dma_start(prow[0:8, P:P + 256], g_ffn.rearrange("l (r c) -> (l r) c", c=256)).then_inc(vec_in, 16)
            sp.dma_start(wdw_rows, conv_w_dw[0]).then_inc(vec_in, 16)
            sp.dma_start(bpw2, conv_b_pw2).then_inc(vec_in, 16)
            for i, (c0, c1) in enumerate(PW1_PARTS):
                for g in range(2):
                    w = conv_w_pw1[0].rearrange("(k p) n -> p k n", p=P)[:, :, D * g + P * c0:D * g + P * c1]
                    o = P * (c0 % 4)
                    sp.dma_start(dense(PW1[2 * (c0 // 4) + g])[:, :, o:o + P * (c1 - c0)], w).then_inc(pw1_in[i], 16)
            for n in range(2):
                sp.dma_start(dense(PW2[n]), cols(conv_w_pw2[0], n)).then_inc(w2_in[n], 16)
            expert(0, 0, 0)
            sp.wait_ge(pw1_mm, 4)
            for n in range(2):
                sp.dma_start(dense(WB[n]), cols(ple_w_gate[0], n)).then_inc(ple_in[n], 16)
            sp.wait_ge(pw1_mm, 8)
            sp.dma_start(dense(WB[2]), cols(nsa_w_in[0], 2)).then_inc(in_in[2], 16)
            gate_up_load(0, 1, R1[0], 0, gu_in[1])
            sp.wait_ge(conv_ok, KD)
            embeddings(0)
            sp.wait_ge(out_mm, 4)
            gate_up_load(0, 1, R1[1], 1, gu_in[1])
            down_load(0, 1, R1[2], dn_in[1])
            experts(0)
            sp.wait_ge(slot_free, NE - 1)
            for n, b in ((3, 0), (4, 1), (0, 2)):
                sp.dma_start(dense(R0[b]), cols(nsa_w_in[0], n)).then_inc(in_in[n], 16)
            sp.wait_ge(slot_free, NE)
            sp.wait_ge(wT_ok, NE + 1)
            sp.dma_start(pei[0:16, :, :], nsa_cmp_pe[0].rearrange("s (j u) e -> j s (u e)", u=2)).then_inc(att_in, 16)
            for m, v in enumerate((nsa_q_norm[0:1, :], nsa_k_norm[0, 1:2, :], nsa_k_norm[0, 2:3, :], nsa_k_norm[0, 0:1, :])):
                sp.dma_start(gn[:, m, :], v.broadcast_to([P, DH])).then_inc(att_in, 16)
            sp.dma_start(invb, inv_freq.broadcast_to([P, DH // 2])).then_inc(att_in, 16)
            for s in range(2):
                sp.dma_start(w2c[:, s, :, :], nsa_cmp_w2[0, s].rearrange("(c p) n -> p c n", p=P)).then_inc(att_in, 16)
            sp.wait_ge(pl_mm, 3)
            sp.dma_start(dense(WB[0]), cols(nsa_w_in[0], 1)).then_inc(in_in[1], 16)
            sp.wait_ge(pl_mm, 4)
            sp.dma_start(WB[1].rearrange("p (j n) -> p j n", j=16),
                         nsa_cmp_w1[0, 0].rearrange("(j p) n -> p j n", p=P)).then_inc(w2_in[0], 16)
            sp.wait_ge(h_dve, H_DVE[3])
            sp.dma_start(wgate3, nsa_w_in[0].rearrange("(k p) n -> p k n", p=P)[:, :, 2560:2608]).then_inc(gate_in, 16)
            sp.wait_ge(xp_mm, 2)
            sp.dma_start(WB[2].rearrange("p (j n) -> p j n", j=16),
                         nsa_cmp_w1[0, 1].rearrange("(j p) n -> p j n", p=P)).then_inc(w2_in[1], 16)
            sp.wait_ge(q_mm, 4)
            sp.dma_start(dense(WB[0]), cols(nsa_w_out[0], 0)).then_inc(in_in[0], 16)
            sp.wait_ge(c1_mm, 1)
            sp.dma_start(dense(WB[1]), cols(nsa_w_out[0], 1)).then_inc(in_in[1], 16)
            expert(1, 0, 0)
            sp.wait_ge(c1_mm, 2)
            sp.dma_start(dense(WB[2]), cols(ple_w_gate[1], 0)).then_inc(ple_in[0], 16)
            down_load(1, 1, R1[2], dn_in[1])
            sp.wait_ge(o_mm, 8)
            embeddings(1)
            sp.wait_ge(out_mm, 8)
            gate_up_load(1, 1, R1[0], 0, gu_in[1])
            gate_up_load(1, 1, R1[1], 1, gu_in[1])
            sp.dma_start(dense(WB[0]), cols(ple_w_gate[1], 1)).then_inc(ple_in[1], 16)
            gate_up_load(1, NE - 1, WB[1], 0, last_in)
            experts(1)
            for t in range(NT):
                sp.wait_ge(h_dve, H_DVE[6] - 2 + 2 * t)
                sp.dma_start(out[0, t * P:(t + 1) * P, :], h[:, t, :]).then_inc(out_st, 16)
            sp.wait_ge(out_st, 16 * NT)

        PLE_W = [[WB[0], WB[1]], [WB[2], WB[0]]]

        @block.tensor
        def _(pe):
            def norm_T(a, t):
                pe.wait_ge(hn_act if t else hn_dve, a + 1)
                for k in range(KD):
                    i = pe.transpose(PS[:, 4 + 2 * t + k // 4, (k % 4) * P:(k % 4 + 1) * P],
                                     hn[:, t, k * P:(k + 1) * P], ident[:, :])
                    if k % 4 == 3:
                        i.then_inc(tr_ok, 1)

            def xnT_ready(a, k, t):
                pe.wait_ge(xt_dve if k < 4 else xt_act, 2 * a + t + 1)

            def tokens_out(w, bank, t, done, a=None, lhs=xnT, start=True):
                for k in range(KD):
                    if a is not None:
                        xnT_ready(a, k, t)
                    i = pe.matmul(PS[:, bank, :], lhs[:, k, t * P:(t + 1) * P], w[:, k, :],
                                  start=start and k == 0, stop=(k == KD - 1))
                i.then_inc(done, 1)

            def embeddings_T(L):
                pe.wait_ge(p_in, 16 * (L + 1))
                for c in range(2):
                    for t in range(NT):
                        i = pe.transpose(PS[:, 4, (2 * c + t) * P:(2 * c + t + 1) * P], pin[:, t, c * P:(c + 1) * P], ident[:, :])
                i.then_inc(ptr, 1)

            def embedding_product(L, n, t):
                if (n, t) == (0, 0):
                    pe.wait_ge(pT_ok, L + 1)
                    pe.wait_ge(proj_in, 16 * (L + 1))
                    pe.wait_ge(h_dve, H_DVE[3 * L + 1] - 2)
                for c in range(2):
                    i = pe.matmul(PS[:, 2 * n + t, :], pT2[:, c, t * P:(t + 1) * P],
                                  wproj[:, c, 512 * n:512 * (n + 1)], start=(c == 0), stop=(c == 1))
                i.then_inc(pp_mm, 1)

            pe.wait_ge(const_ok, 1)
            pe.wait_ge(vec_in, 16 * N_VEC)
            pe.transpose(PS[:, 0, 0:NROWS], prow[0:NROWS, 0:P], ident[0:NROWS, 0:NROWS]).then_inc(vtr, 1)
            for c in range(2):
                i = pe.transpose(PS[:, 1, c * 8:c * 8 + 8], prow[0:8, P + c:P + 256:2], ident[0:8, 0:8])
            i.then_inc(vtr, 1)
            for c in range(KD):
                i = pe.transpose(PS[:, 2, c * TAPS:(c + 1) * TAPS], wdw_rows[:, c * P:(c + 1) * P],
                                 ident[0:TAPS, 0:TAPS])
            i.then_inc(vtr, 1)

            norm_T(0, 0)
            norm_T(0, 1)
            def taps(c):
                pe.wait_ge(glu_ok, c + 1)
                pe.wait_ge(dg_ok, c + 1)
                if c >= 2:
                    pe.wait_ge(conv_ok, c - 1)
                for i_ in range(PE_TAPS):
                    w = TAPS - PE_TAPS + i_
                    i = pe.matmul(PS[:, 4 + c % 2, 0:T], dgb[:, c % 2, i_, :], cv0[:, c, w:w + T],
                                  start=(i_ == 0), stop=(i_ == PE_TAPS - 1))
                i.then_inc(tap_mm, 1)

            def channel_sum(c):
                pe.wait_ge(conv_ok, c + 1)
                i = pe.matmul(PS[:, 6, 0:T], ones[:, :], cT[:, c, :], start=(c == 0), stop=(c == KD - 1))
                if c == KD - 1:
                    i.then_inc(lnmm, 1)

            for c in range(KD):
                part = (0, 1, 2, 2, 3, 3, 3, 3)[c]
                pe.wait_ge(pw1_in[part], 32)
                if c >= 4:
                    pe.wait_ge(glu_ok, c - 3)
                else:
                    pe.wait_ge(vec_ok, 3)
                for g in range(2):
                    w = dense(PW1[2 * (c // 4) + g])
                    for k in range(KD):
                        xnT_ready(0, k, 1)
                        i = pe.matmul(PS[:, c % 4, g * T:(g + 1) * T], w[:, k, (c % 4) * P:(c % 4 + 1) * P],
                                      xnT[:, k, :], start=(k == 0), stop=(k == KD - 1))
                i.then_inc(pw1_mm, 1)
                if c >= 1:
                    taps(c - 1)
                if c >= 3:
                    channel_sum(c - 3)
            taps(KD - 1)
            for n in range(2):
                for t in range(NT):
                    pe.matmul(PS[:, 2 * n + t, :], ones[0:1, :], bpw2[:, 512 * n:512 * (n + 1)], start=True, stop=False)
            for c in range(KD - 3, KD):
                channel_sum(c)
            for c in range(KD):
                pe.wait_ge(ln_sq, c + 1)
                i = pe.matmul(PS[:, 7, 0:T], ones[:, :], xnT[:, c, :], start=(c == 0), stop=(c == KD - 1))
            i.then_inc(lnmm, 1)
            for n in range(2):
                pe.wait_ge(w2_in[n], 16)
                for t in range(NT):
                    if (n, t) == (1, 1):
                        embeddings_T(0)
                    for k in range(KD):
                        pe.wait_ge(silu_ok, k + 1)
                        i = pe.matmul(PS[:, 2 * n + t, :], cT[:, k, t * P:(t + 1) * P], dense(PW2[n])[:, k, :],
                                      start=False, stop=(k == KD - 1))
                    i.then_inc(out_mm, 1)

            embedding_product(0, 0, 0)
            embedding_product(0, 0, 1)

            def gather(lhs):
                for t in range(NT):
                    for j in range(4):
                        i = pe.matmul(PS[32 * j:32 * j + 32, BGX, 0:Q4], lhs[:, t, :], hn[:, t, Q4 * j:Q4 * (j + 1)],
                                      start=(t == 0), stop=(t == NT - 1))
                return i

            def xg_T():
                for c in range(2):
                    i = pe.transpose(PS[:, BGX, Q4 + P * c:Q4 + P * (c + 1)], xg[:, c::2], ident[:, :])
                return i

            def gate_up(s, xT, early_gate):
                for k in range(8):
                    for j in range(4):
                        w = w_last if early_gate and j < 2 else w_gu(s)[:, j // 2, :, :]
                        i = pe.matmul(PS[32 * j:32 * j + 32, BGU, 0:256], xT[:, k, :],
                                      w[:, k, 256 * (j % 2):256 * (j % 2 + 1)],
                                      start=(k == 0), stop=(k == 7))
                return i

            def h_T():
                pe.sem_inc(pe_step, 1)
                for c in range(2):
                    i = pe.transpose(PS[:, BHT, 64 * c:64 * (c + 1)], hh[64:128, c::2], ident[64:128, 64:128])
                return i

            def down(s):
                for q in range(4):
                    f, c = q // 2, q % 2
                    for j in range(4):
                        i = pe.matmul(PS[32 * j:32 * j + 32, BY, 0:Q4], hT[:, c, 32 * f:32 * f + 32],
                                      w_dn(s)[:, f, c, Q4 * j:Q4 * (j + 1)], start=(q == 0), stop=(q == 3))
                return i

            def scatter(w):
                for t in range(NT):
                    for j in range(4):
                        i = pe.matmul(PS[:, ACC + j, 256 * t:256 * (t + 1)], w[32 * j:32 * j + 32, t * P:(t + 1) * P],
                                      ysb[32 * j:32 * j + 32, :], start=False, stop=False, skip_group_check=True)
                return i

            def moe(L):
                a = 3 * L + 1
                norm_T(a, 0)
                norm_T(a, 1)
                pe.wait_ge(misc_in, 16 * N_MISC)
                xnT_ready(a, 4, 0)
                xnT_ready(a, 0, 0)
                for t in range(NT):
                    o = PS[:, BGU, 64 * t:64 * t + 36]
                    pe.matmul(o, ones[0:1, :], rowb[0:1, 36 * L:36 * (L + 1)], start=True, stop=False)
                    for k in range(KD):
                        xnT_ready(a, k, t)
                        i = pe.matmul(o, xnT[:, k, t * P:(t + 1) * P], wr[:, L, k, :], start=False, stop=(k == KD - 1))
                i.then_inc(rt_mm, 1)
                embedding_product(L, 1, 0)
                embedding_product(L, 1, 1)
                pe.wait_ge(xt_dve, 2 * a + 2)
                pe.wait_ge(xt_act, 2 * a + 2)
                pe.wait_ge(rt_c, L + 1)
                pe.matmul(PS[:, 6, 0:32], upper[:, :], Cc[:, 0, :], start=True, stop=True)
                pe.matmul(PS[:, 6, 32:64], upper[:, :], Cc[:, 1, :], start=True, stop=False)
                pe.matmul(PS[:, 6, 32:64], ones[:, :], Cc[:, 0, :], start=False, stop=True)
                pe.matmul(PS[:, 6, 64:96], ones[:, :], Cc[:, 0, :], start=True, stop=False)
                pe.matmul(PS[:, 6, 64:96], ones[:, :], Cc[:, 1, :], start=False, stop=True).then_inc(rt_pf, 1)
                pe.wait_ge(pp_ok, 4 * (L + 1))
                for t in range(NT):
                    for j in range(4):
                        i = pe.matmul(PS[:, ACC + j, 256 * t:256 * (t + 1)], ident[:, :], h[:, t, Q4 * j:Q4 * (j + 1)],
                                      start=(t == 0), stop=False, skip_group_check=True)
                pe.wait_ge(rt_s, L + 1)
                for v, bk in ((S4, 4), (W4, 7)):
                    for t in range(NT):
                        for s in range(2):
                            i = pe.matmul(PS[:, bk, (2 * s + t) * P:(2 * s + t + 1) * P],
                                          v[:, t, s:s + 1].broadcast_to([P, P]), ident[:, :], start=True, stop=True)
                i.then_inc(rt_row, 1)
                g0 = (NE + 1) * L
                pe.wait_ge(sel_ok, g0 + 1)
                gather(sel[0]).then_inc(ga_mm, 1)
                pe.wait_ge(xg_ok, g0 + 1)
                xg_T().then_inc(xt_mm, 1)
                pe.wait_ge(row_dve, L + 1)
                pe.wait_ge(row_act, L + 1)
                def one_expert(it, s, early_gate=False):
                    n = it * 2 + (s + NE * L + 1)
                    gi = it * 2 + (s + g0 + 2)
                    ld = it * 16 + 16 * (NE // 2 * L + 1)
                    if early_gate:
                        pe.wait_ge(last_in, 16)
                        pe.wait_ge(gu_in[s], ld * 2 - 16)
                    else:
                        pe.wait_ge(gu_in[s], ld * 2)
                    pe.wait_ge(xgT_ok, gi - 1)
                    gate_up(s, xgT, early_gate).then_inc(gu_mm, 1)
                    pe.wait_ge(sel_ok, gi)
                    gather(sel[1 - s]).then_inc(ga_mm, 1)
                    pe.wait_ge(h_ok, n)
                    h_T().then_inc(ht_mm, 1)
                    pe.wait_ge(dn_in[s], ld)
                    pe.wait_ge(hT_ok, n)
                    down(s).then_inc(y_mm, 1)
                    pe.wait_ge(xg_ok, gi)
                    xg_T().then_inc(xt_mm, 1)
                    pe.wait_ge(wT_ok, gi - 1)
                    pe.wait_ge(y_ok, n)
                    scatter(wT[s]).then_inc(wT_free, 1)
                    e = it * 2 + s
                    pe.wait_ge(tab_ok, L + 1)
                    more = pe.value_load(tab[0:1, 0, bass.ds(e, 1)], min_val=0, max_val=7)
                    before = pe.value_load(tab[0:1, 1, bass.ds(e, 1)], min_val=0, max_val=64)
                    with pe.If(more > 0):
                        with pe.Fori(0, more) as r:
                            c = before + r + 1
                            pe.wait_ge(X["x_sel"], c)
                            pe.wait_ge(xgT_ok, gi)
                            gather(xsel).then_inc(X["x_ga"], 1)
                            pe.wait_ge(X["x_xg"], c)
                            xg_T().then_inc(X["x_xt"], 1)
                            pe.wait_ge(X["x_xgT"], c)
                            gate_up(s, xxgT, early_gate).then_inc(X["x_gu"], 1)
                            pe.wait_ge(X["x_h"], c)
                            h_T().then_inc(X["x_ht"], 1)
                            pe.wait_ge(X["x_hT"], c)
                            down(s).then_inc(X["x_y"], 1)
                            pe.wait_ge(X["x_wT"], c)
                            pe.wait_ge(X["x_ysb"], c)
                            scatter(xwT).then_inc(X["x_done"], 1)
                    pe.drain().then_inc(slot_free, 1)
                with pe.Fori(0, NE // 2 - L) as it:
                    one_expert(it, 0)
                    one_expert(it, 1)
                if L == 1:
                    one_expert(NE // 2 - 1, 0)
                    one_expert(NE // 2 - 1, 1, True)
                norm_T(a + 1, 0)
                for t in range(NT):
                    for n in range(2):
                        pe.wait_ge(ple_in[n], 16 * (L + 1))
                        if (t, n) == (1, 1) and L == 0:
                            norm_T(3, 0)
                        tokens_out(dense(PLE_W[L][n]), 2 * n + t, t, pl_mm, a + 1)
                        if (t, n) == (0, 0):
                            norm_T(a + 1, 1)

            pe.sem_inc(wT_free, 1)
            pe.sem_inc(X["x_done"], 1)
            moe(0)

            for t in range(NT):
                for s in range(2):
                    pe.wait_ge(in_in[3 + s], 16)
                    bk = 2 + t if s == 0 else 4 + t
                    tokens_out(dense(R0[s]), bk, t, kv_mm, 3)
                    if (t, s) == (0, 0):
                        norm_T(3, 1)
            pe.wait_ge(gate_in, 16)
            for t in range(NT):
                for k in range(KD):
                    i = pe.matmul(PS[:, 6, 64 * t:64 * t + 48], xnT[:, k, t * P:(t + 1) * P], wgate3[:, k, :],
                                  start=(k == 0), stop=(k == KD - 1))
            i.then_inc(gate_mm, 1)
            pe.wait_ge(in_in[2], 16)
            pe.wait_ge(pl_mul, 4)
            for u in range(2):
                for k in range(KD):
                    i = pe.matmul(PS[:, u, :], xnT[:, k, u::2], dense(WB[2])[:, k, :], start=(k == 0), stop=(k == KD - 1))
                i.then_inc(xp_mm, 1)

            def q_products(t):
                for n in range(2):
                    pe.wait_ge(in_in[n], 16)
                    tokens_out(dense(R0[2] if n == 0 else WB[0]), 2 + 2 * n + t, t, q_mm)

            pe.wait_ge(kv_dve, 4)
            pe.wait_ge(kv_act, 4)
            q_products(0)
            pe.wait_ge(xp_ok, 2)
            for s in range(2):
                for g in range(NKV):
                    i = pe.transpose(PS[:, s, g * P:(g + 1) * P], xp[:, s, g, :, :].rearrange("p u e -> p (u e)"), ident[:, :])
                i.then_inc(xpt_mm, 1)
            for s in range(2):
                i = pe.transpose(PS[:, 7, 16 * s:16 * s + 16], pei[0:16, s, :], ident[0:16, 0:16])
            i.then_inc(xpt_mm, 1)
            q_products(1)
            for s in range(2):
                pe.wait_ge(w2_in[s], 32)
                pe.wait_ge(B_ok, s + 1)
                w1 = (WB[1] if s == 0 else WB[2]).rearrange("p (j n) -> p j n", j=16)
                for j in range(16):
                    i = pe.matmul(PS[0:60, s, 0:256], Bc[:, s, j, :, :].rearrange("p g n -> p (g n)"), w1[:, j, :], start=(j == 0), stop=(j == 15))
                i.then_inc(c1_mm, 1)

            def mlp_out(s):
                pe.wait_ge(c1_g, s + 1)
                if s == 1:
                    pe.wait_ge(kc_x, 1)
                for c in range(2):
                    i = pe.transpose(PS[:, 0, 256 + 64 * c:256 + 64 * c + 60], h1v[s][0:60, c * P:(c + 1) * P], ident[0:60, 0:60])
                i.then_inc(c1_t, 1)
                pe.wait_ge(c1_T, s + 1)
                if s == 0:
                    for c in range(2):
                        i = pe.matmul(PS[0:60, 0, 0:64], h1T[:, c, 0:60], w2c[:, 0, c, :], start=(c == 0), stop=(c == 1))
                else:
                    for c in range(2):
                        for g in range(4):
                            for q in range(4):
                                i = pe.matmul(PS[32 * q:32 * q + NC_, 1, 256 + 64 * g:256 + 64 * g + 64], h1T[:, c, NC_ * g:NC_ * (g + 1)],
                                              w2c[:, 1, c, :], start=(c == 0 and g == 0), stop=(c == 1), skip_group_check=True)
                i.then_inc(kc_mm, 1)

            def k_T(b):
                for kk in range(2):
                    for t in range(NT):
                        m = 4 * (b // 2) + 2 * (b % 2) + kk
                        i = pe.transpose(PS[:, 6 + b % 2, (2 * kk + t) * P:(2 * kk + t + 1) * P], rotk[:, t, m, :, :], ident[:, :])
                i.then_inc(qt_mm, 1)

            mlp_out(0)
            pe.wait_ge(rot_ok, 3)
            pe.wait_ge(gate_ok, 1)
            k_T(0)
            k_T(1)
            for b in range(4):
                for kk in range(2):
                    for t in range(NT):
                        hp = 2 * b + kk
                        i = pe.transpose(PS[:, 2 + b, (2 * kk + t) * P:(2 * kk + t + 1) * P],
                                         rotq[:, t, 2 * hp:2 * hp + 2, :], ident[:, :])
                i.then_inc(qt_mm, 1)
            pe.wait_ge(qt_act, 2)
            k_T(2)
            k_T(3)
            mlp_out(1)
            pe.wait_ge(kc_x, 2)
            pe.transpose(PS[:, 0, 384:444], kcx[0:60, 2:4, :], ident[0:60, 0:60]).then_inc(kct_mm, 1)
            def scores(hp):
                g = hp // 2
                if hp > 0:
                    pe.wait_ge(s_max, 9 * hp - 1)
                for t in range(NT):
                    for i_ in range(2):
                        r = slice(64 * i_, 64 * i_ + 64)
                        i = pe.matmul(PS[:, 2 * t + i_, 0:256 * (t + 1)], qT[r, hp, t * P:(t + 1) * P],
                                      kT[r, :, g, 0:P * (t + 1)], start=True, stop=True)
                i.then_inc(s_mm, 1)

            def probs_T(hp):
                pe.wait_ge(s_scl, 2 * (hp + 1))
                pe.wait_ge(s_sclv, hp + 1)
                if hp > 0:
                    pe.wait_ge(pt_dve, hp)
                    pe.wait_ge(pt_act, 2 * hp)
                for n in range(12):
                    i_, s, q = n // 6, (n // 3) % 2, n % 3
                    src = Pb[:, hp % 2, i_, 128 * s:128 * s + 128] if q == 0 else \
                        Pb[:, hp % 2, i_, 256 + 256 * s + 128 * (q - 1):256 + 256 * s + 128 * q]
                    i = pe.transpose(PS[:, 4 + n // 4, (n % 4) * P:(n % 4 + 1) * P], src, ident[:, :])
                    if n % 4 == 3:
                        i.then_inc(t_mm, 1)

            def pv(hp):
                g = hp // 2
                pe.wait_ge(pt_dve, hp + 1)
                pe.wait_ge(pt_act, 2 * hp + 2)
                if hp > 0:
                    pe.wait_ge(o_ok, hp)
                for s in range(2):
                    for kb in range(2):
                        for i_ in range(2):
                            o = i_ * 768 + s * 384
                            rhs = pT[:, hp % 2, o:o + 256] if kb == 0 else pT[:, hp % 2, o + 256:o + 384]
                            pe.matmul(PS[64 * i_:64 * i_ + 64, 7, 128 * kb:256], vv[:, kb, s, 64 * g:64 * g + 64], rhs,
                                      start=(s == 0 and kb == 0), stop=False, skip_group_check=True)
                for i_ in range(2):
                    hd = 2 * hp + i_
                    r = slice(32 * (hd % 4), 32 * (hd % 4) + NC_)
                    i = pe.matmul(PS[64 * i_:64 * i_ + 64, 7, 0:256], vcr[r, g, :], PcT[r, hd // 4, :],
                                  start=False, stop=True, skip_group_check=True)
                i.then_inc(o_mm, 1)

            pe.wait_ge(kcT_ok, 2)
            pe.wait_ge(vcr_ok, 1)
            pe.wait_ge(qt_act, 8)
            scores(0)
            for hp in range(8):
                for t in range(NT):
                    i = pe.matmul(PS[:, 7, 256 * t + 32 * hp:256 * t + 32 * hp + 32], qT[:, hp, t * P:(t + 1) * P],
                                  kcB[:, hp // 2, :, :].rearrange("p u n -> p (u n)"), start=True, stop=True)
            i.then_inc(sc_mm, 1)
            scores(1)
            pe.wait_ge(sc_p, 1)
            for t in range(NT):
                for c in range(4):
                    i = pe.transpose(PS[:, 4 + c // 2, (2 * (c % 2) + t) * P:(2 * (c % 2) + t + 1) * P], Pc[:, t, 4 * c:4 * c + 4, :], ident[:, :])
            i.then_inc(sct_mm, 1)
            pe.wait_ge(pct_ok, 2)
            for hp in range(8):
                if 0 < hp < 7:
                    scores(hp + 1)
                probs_T(hp)
                pv(hp)
            pe.wait_ge(o_ok, 8)
            for n in range(2):
                pe.wait_ge(in_in[n], 32)
                for t in range(NT):
                    if (n, t) == (1, 1):
                        embeddings_T(1)
                    tokens_out(dense(WB[n]), 2 * n + t, t, out_mm, lhs=OT)
            embedding_product(1, 0, 0)
            embedding_product(1, 0, 1)
            moe(1)

        @block.gpsimd
        def _(pool):
            g = nc.gpsimd
            own = [0]

            def link(i):
                own[0] += 1
                i.then_inc(c_pool, 1)
                pool.wait_ge(c_pool, own[0])

            link(g.memset(ident[:, :], 0.0))
            link(g.affine_select(out=ident[:, :], in_=ident[:, :], compare_op=ALU.not_equal, fill=1.0, base=0,
                                 pattern=[[-1, P]], channel_multiplier=1))
            link(g.memset(ones[:, :], 1.0))
            link(g.memset(nhalf[:, :], -0.5))
            link(g.affine_select(out=upper[:, :], in_=ones[:, :], compare_op=ALU.is_gt, fill=0.0, base=0,
                                 pattern=[[1, P]], channel_multiplier=-1))
            link(g.memset(cmask[:, :, :], 0.0))
            link(g.affine_select(out=cmask[:, 1, :], in_=cmask[:, 1, :], compare_op=ALU.is_ge, fill=NEG, base=0,
                                 pattern=[[-1, P]], channel_multiplier=1))
            link(g.iota(ioti[:, :], pattern=[[1, 32]], base=0, channel_multiplier=0))
            link(g.tensor_copy(iot[:, :], ioti[:, :]))
            for q in range(4):
                link(g.iota(ioti[32 * q:32 * q + 32, 0:1], pattern=[[0, 1]], base=0, channel_multiplier=1))
            g.tensor_copy(colp[:, :], ioti[:, 0:1]).then_inc(const_ok, 1)

            def rsqrt(n, x):
                pool.wait_ge(var_ok, n)
                g.tensor_tensor(x, x, nhalf[0:x.shape[0], 0:1].broadcast_to(list(x.shape)), ALU.pow).then_inc(rs_ok, 1)

            def build_block(c32, cc, to_sel, to_wT, count, base, s_ok, w_ok, rows=None):
                for t in range(NT):
                    for k in range(2):
                        i = g.tensor_scalar(eq4[:, t, k, :], c32, S4[:, t, k:k + 1], None, ALU.is_equal)
                i.then_inc(count, 1)
                pool.wait_ge(count, base + 1)
                g.tensor_tensor(to_sel, eq4[:, :, 0, :], eq4[:, :, 1, :], ALU.add).then_inc(s_ok, 1)
                if rows is not None:
                    pool.wait_ge(row_dve, rows)
                    pool.wait_ge(row_act, rows)
                g.tensor_scalar(eqr, srow, cc, None, ALU.is_equal).then_inc(count, 1)
                pool.wait_ge(count, base + 2)
                g.tensor_tensor(eqr, eqr, wrow, ALU.mult).then_inc(count, 1)
                pool.wait_ge(count, base + 3)
                g.tensor_tensor(to_wT, eqr[:, 0, :], eqr[:, 1, :], ALU.add).then_inc(w_ok, 1)

            def moe(L):
                g0 = (NE + 1) * L
                pool.wait_ge(rt_s, L + 1)
                g.tensor_copy(cur32, iot[:, :]).then_inc(c_bld, 1)
                g.tensor_copy(curc, colp[:, :]).then_inc(c_bld, 1)
                pool.wait_ge(c_bld, 5 * g0 + 2)
                build_block(cur32, curc, sel[0], wT[0], c_bld, 5 * g0 + 2, sel_ok, wT_ok, L + 1)
                with pool.Fori(0, NE // 2) as it:
                    for s in range(2):
                        gi = it * 2 + (s + g0 + 1)
                        pool.wait_ge(wT_free, it * 2 + (s + NE * L + 1))
                        pool.sem_inc(pool_step, 1)
                        g.tensor_scalar(cur32, cur32, 256.0, None, ALU.add).then_inc(c_bld, 1)
                        g.tensor_scalar(curc, curc, 256.0, None, ALU.add).then_inc(c_bld, 1)
                        pool.wait_ge(c_bld, gi * 5 + 2)
                        pool.sem_inc(pool_step, 1)
                        build_block(cur32, curc, sel[1 - s], wT[1 - s], c_bld, gi * 5 + 2, sel_ok, wT_ok)
                        e = it * 2 + s
                        pool.wait_ge(tab_ok, L + 1)
                        more = pool.value_load(tab[0:1, 0, bass.ds(e, 1)], min_val=0, max_val=7)
                        before = pool.value_load(tab[0:1, 1, bass.ds(e, 1)], min_val=0, max_val=64)
                        with pool.If(more > 0):
                            g.tensor_scalar(xcur32, cur32, -256.0, None, ALU.add)
                            g.tensor_scalar(xcurc, curc, -256.0, None, ALU.add)
                            pool.drain()
                            with pool.Fori(0, more) as r:
                                c = before + r
                                pool.wait_ge(X["x_done"], c + 1)
                                pool.sem_inc(pool_step, 1)
                                g.tensor_scalar(xcur32, xcur32, float(SLOTS), None, ALU.add).then_inc(x_bld, 1)
                                g.tensor_scalar(xcurc, xcurc, float(SLOTS), None, ALU.add).then_inc(x_bld, 1)
                                pool.wait_ge(x_bld, c * 5 + 2)
                                pool.sem_inc(pool_step, 1)
                                build_block(xcur32, xcurc, xsel, xwT, x_bld, c * 5 + 2, X["x_sel"], X["x_wT"])

            rsqrt(1, rstd[:, 1, 0:1])
            rsqrt(2, rstd[:, 1, 1:2])
            for c in range(KD):
                pool.wait_ge(glu_ok, c + 1)
                if c >= 2:
                    pool.wait_ge(conv_ok, c - 1)
                for i_ in range(POOL_TAPS):
                    w = TAPS - PE_TAPS - POOL_TAPS + i_
                    u = cv0[:, c, w:w + T]
                    if i_ == 0:
                        g.tensor_scalar(pac[c % 2], u, wdw[:, c, w:w + 1], None, ALU.mult).then_inc(c_pool, 1)
                        own[0] += 1
                    else:
                        link(g.tensor_scalar(ptm, u, wdw[:, c, w:w + 1], None, ALU.mult))
                        i = g.tensor_tensor(pac[c % 2], pac[c % 2], ptm, ALU.add)
                        if i_ < POOL_TAPS - 1:
                            link(i)
                i.then_inc(ptap_ok, 1)
                pool.wait_ge(ptap_ok, c + 1)
            rsqrt(3, rstd[:, 1, 0:1])
            rsqrt(4, rstd[:, 1, 1:2])
            moe(0)
            rsqrt(5, rstd[:, 1, 0:1])
            rsqrt(6, rstd[:, 1, 1:2])
            rsqrt(7, rstd[:, 1, 0:1])
            rsqrt(8, rstd[:, 1, 1:2])
            pool.wait_ge(h_dve, H_DVE[3])
            link(g.memset(mka, 0.0))
            link(g.memset(mk1, 1.0))
            for t in range(NT):
                for m, f in ((mka, NEG), (mk1, 0.0)):
                    link(g.affine_select(out=m[:, t, :], in_=m[:, t, :], compare_op=ALU.is_ge, fill=f,
                                         base=t * P - (CMP_BLOCK - 1), pattern=[[-CMP_STRIDE, NC_]], channel_multiplier=1))
            g.memset(mcol[:, 2:3], 0.0).then_inc(mask_ok, 1)
            rsqrt(9, mcol[0:60, 1:2])
            for hp in range(8):
                pool.wait_ge(s_fac, hp + 1)
                for s in range(2):
                    v = Pb[:, hp % 2, 1, 256 + 256 * s:512 + 256 * s]
                    g.tensor_scalar(v, v, fac[:, hp % 2, 6 + s:7 + s], None, ALU.mult).then_inc(s_scl, 1)
            rsqrt(10, rstd[:, 1, 0:1])
            rsqrt(11, rstd[:, 1, 1:2])
            moe(1)
            rsqrt(12, rstd[:, 1, 0:1])
            rsqrt(13, rstd[:, 1, 1:2])

        @block.scalar
        def _(act):
            own = [0]

            def link(i):
                own[0] += 1
                i.then_inc(c_act, 1)
                act.wait_ge(c_act, own[0])

            def norm_half(a):
                if a == 0:
                    act.wait_ge(x_in, 16 * NT)
                else:
                    act.wait_ge(h_dve, H_DVE[a])
                    if H_ACT[a]:
                        act.wait_ge(h_act, H_ACT[a])
                nc.scalar.activation(hn[:, 1, :], h[:, 1, :], ACT.Square, accum_out=rstd[:, 0, 1:2]).then_inc(ssq_ok, 1)
                act.wait_ge(rs_ok, RS_BEFORE[a] + 2)
                nc.scalar.activation(hn[:, 1, :], h[:, 1, :], ACT.Copy, scale=rstd[:, 1, 1:2]).then_inc(hn_act, 1)

            def xnT_copy(a, row, t):
                act.wait_ge(tr_ok, 4 * a + 2 * t + 2)
                for k in range(4, KD):
                    i = nc.scalar.activation(xnT[:, k, t * P:(t + 1) * P], PS[:, 5 + 2 * t, (k - 4) * P:(k - 3) * P], ACT.Copy,
                                             scale=vecT[:, row + k:row + k + 1])
                i.then_inc(xt_act, 1)

            def norm(a, row, then=None):
                norm_half(a)
                if then is not None:
                    then()
                if a == 0:
                    act.wait_ge(vec_ok, 3)
                for t in range(NT):
                    xnT_copy(a, row, t)

            def fill2(dst, src):
                act.dma_start(dst, src, allow_slow_non_contiguous=True).then_inc(misc_in, 16)

            for L in range(DEPTH):
                fill2(wr[:, L, :, 0:NG], moe_w_rg[L].rearrange("(k p) n -> p k n", p=P))
                fill2(wr[:, L, :, NG:], moe_w_re[L].rearrange("(k p) n -> p k n", p=P))
                fill2(rowb[0:1, 36 * L:36 * L + NG], moe_b_rg[L:L + 1, :])
                fill2(rowb[0:1, 36 * L + NG:36 * (L + 1)], moe_b_re[L:L + 1, :])
            for t in range(NT):
                fill2(posi[:, t:t + 1], positions[0:1, t * P:(t + 1) * P].rearrange("o q -> q o"))
            for g in range(NKV):
                fill2(posi[NC_ * g:NC_ * (g + 1), 2:3],
                      positions[0:1, CMP_BLOCK - 1:T:CMP_STRIDE].rearrange("o q -> q o"))

            norm(0, ROW_MIX)
            for c in range(KD):
                act.wait_ge(pw1_mm, c + 1)
                if c >= 2:
                    act.wait_ge(glu_ok, c - 1)
                nc.scalar.activation(sgm[c % 2], PS[:, c % 4, T:2 * T], ACT.Sigmoid,
                                     bias=vecT[:, ROW_BPW1 + 8 + c:ROW_BPW1 + 9 + c]).then_inc(sig_ok, 1)
                if c >= 2:
                    act.wait_ge(tap_mm, c - 1)
                for i_ in range(PE_TAPS):
                    w = TAPS - PE_TAPS + i_
                    i = nc.scalar.activation(dgb[:, c % 2, i_, :], ident[:, :], ACT.Copy, scale=wdw[:, c, w:w + 1])
                i.then_inc(dg_ok, 1)
            for c in range(KD):
                act.wait_ge(ln_c, c + 1)
                nc.scalar.activation(xnT[:, c, :], cT[:, c, :], ACT.Square).then_inc(ln_sq, 1)
            act.wait_ge(root_in, 1)
            nc.scalar.activation(var, var, ACT.Sqrt).then_inc(root_ok, 1)
            for c in range(KD):
                act.wait_ge(ln_r, c + 1)
                nc.scalar.activation(cT[:, c, :], cT[:, c, :], ACT.Silu, scale=vecT[:, ROW_LNG + c:ROW_LNG + c + 1],
                                     bias=vecT[:, ROW_LNB + c:ROW_LNB + c + 1]).then_inc(silu_ok, 1)

            def moe(L):
                a = 3 * L + 1
                act.wait_ge(ptr, L + 1)
                nc.scalar.copy(pT2, PS[:, 4, :].rearrange("p (c q) -> p c q", c=2)).then_inc(pT_ok, 1)

                def products(n):
                    for t in range(NT):
                        act.wait_ge(pp_mm, 4 * L + 2 * n + t + 1)
                        nc.scalar.copy(pp[:, t, 512 * n:512 * (n + 1)], PS[:, 2 * n + t, :]).then_inc(pp_ok, 1)

                norm(a, ROW_FFN + 8 * L, lambda: products(0))
                act.wait_ge(rt_d, 2 * L + 1)
                nc.scalar.activation(eg, dg, ACT.Exp).then_inc(rt_e, 1)
                products(1)
                act.wait_ge(rt_d, 2 * L + 2)
                nc.scalar.activation(sm[:, 4, :], sm[:, 3, :], ACT.Exp).then_inc(rt_e, 1)
                act.wait_ge(rt_row, L + 1)
                nc.scalar.copy(wrow, PS[:, 7, :].rearrange("p (a q) -> p a q", a=2)).then_inc(row_act, 1)
                g0 = (NE + 1) * L
                act.wait_ge(ga_mm, g0 + 1)
                nc.scalar.copy(xg, PS[:, BGX, 0:Q4]).then_inc(xg_ok, 1)
                with act.Fori(0, NE // 2) as it:
                    for s in range(2):
                        n = it * 2 + (s + NE * L + 1)
                        gi = it * 2 + (s + g0 + 2)
                        act.wait_ge(gu_mm, n)
                        nc.scalar.activation(gs[64:128, :], PS[0:64, BGU, 0:256], ACT.Silu).then_inc(sil_ok, 1)
                        act.wait_ge(ga_mm, gi)
                        nc.scalar.copy(xg, PS[:, BGX, 0:Q4]).then_inc(xg_ok, 1)
                        act.wait_ge(y_mm, n)
                        nc.scalar.copy(ysb, PS[:, BY, 0:Q4]).then_inc(y_ok, 1)
                        e = it * 2 + s
                        act.wait_ge(tab_ok, L + 1)
                        more = act.value_load(tab[0:1, 0, bass.ds(e, 1)], min_val=0, max_val=7)
                        before = act.value_load(tab[0:1, 1, bass.ds(e, 1)], min_val=0, max_val=64)
                        with act.If(more > 0):
                            with act.Fori(0, more) as r:
                                c = before + r + 1
                                act.wait_ge(X["x_ga"], c)
                                nc.scalar.copy(xg, PS[:, BGX, 0:Q4]).then_inc(X["x_xg"], 1)
                                act.wait_ge(X["x_gu"], c)
                                nc.scalar.activation(gs[64:128, :], PS[0:64, BGU, 0:256], ACT.Silu).then_inc(X["x_sil"], 1)
                                act.wait_ge(X["x_y"], c)
                                nc.scalar.copy(ysb, PS[:, BY, 0:Q4]).then_inc(X["x_ysb"], 1)
                act.wait_ge(slot_free, NE * (L + 1))
                for j in (1, 3):
                    nc.scalar.copy(h[:, :, Q4 * j:Q4 * (j + 1)],
                                   PS[:, ACC + j, :].rearrange("p (t q) -> p t q", t=2)).then_inc(h_act, 1)
                norm(a + 1, ROW_PLE + 8 * L)
                if L == 0:
                    act.wait_ge(trig_ok, 1)
                    nc.scalar.activation(trig, trig, ACT.Sin).then_inc(sin_ok, 1)
                    act.wait_ge(trig_ok, 2)
                    nc.scalar.activation(tcc[0:60, 0:64], tcc[0:60, 0:64], ACT.Sin).then_inc(sin_ok, 1)
                for t in range(NT):
                    for n in range(2):
                        act.wait_ge(pl_mm, 4 * L + 2 * t + n + 1)
                        nc.scalar.activation(hn[:, t, 512 * n:512 * (n + 1)], PS[:, 2 * n + t, :], ACT.Sigmoid).then_inc(pl_sig, 1)
                        if (t, n) == (1, 0) and L == 0:
                            xnT_copy(3, ROW_MIX + 8, 0)

            moe(0)
            norm_half(3)
            for t in range(NT):
                for s in range(2):
                    act.wait_ge(kv_dve, 2 * t + s + 1)
                    nc.scalar.copy(vv[:, t, s, :], PS[:, 2 + 2 * s + t, 256:512]).then_inc(kv_act, 1)
                    if (t, s) == (0, 0):
                        xnT_copy(3, ROW_MIX + 8, 1)
            act.wait_ge(gate_mm, 1)
            nc.scalar.activation(gt, PS[:, 6, 0:128].rearrange("p (t c) -> p t c", t=2)[:, :, 0:48], ACT.Sigmoid).then_inc(gate_ok, 1)
            for u in range(2):
                act.wait_ge(xp_mm, u + 1)
                nc.scalar.copy(xp[:, :, :, u, :], PS[:, u, :].rearrange("p (s g e) -> p s g e", s=2, g=4)).then_inc(xp_ok, 1)

            def squares_and_root(i, t, lo, n):
                if i:
                    act.wait_ge(sq_used, i)
                nc.scalar.activation(sq[:, 0:64 * n].rearrange("p (m e) -> p m e", m=n), raw[:, t, lo:lo + n, :], ACT.Square).then_inc(sq_ok, 1)
                act.wait_ge(root_in, i + 2)
                nc.scalar.activation(ssn[:, 24:24 + n], ssn[:, 24:24 + n], ACT.Sqrt).then_inc(root_ok, 1)

            for t in range(NT):
                squares_and_root(t, t, 16, 8)
            for t in range(NT):
                for n in range(2):
                    act.wait_ge(q_mm, 2 * t + n + 1)
                    nc.scalar.copy(raw[:, t, 8 * n:8 * n + 8, :],
                                   PS[:, 2 + 2 * n + t, :].rearrange("p (m e) -> p m e", m=8)).then_inc(c_act, 1)
                    own[0] += 1
                act.wait_ge(c_act, own[0])
                squares_and_root(2 + t, t, 0, 16)

            def gelu_sigmoid(s):
                act.wait_ge(c1_x, s + 1)
                nc.scalar.activation(sq[0:60, 512:768], sq[0:60, 256:512], ACT.Sigmoid, scale=2.0 * float(np.sqrt(2.0 / np.pi))).then_inc(c1_s, 1)

            def h1T_copy(s):
                act.wait_ge(c1_t, s + 1)
                nc.scalar.copy(h1T[:, :, 0:60], PS[:, 0, 256:384].rearrange("p (c n) -> p c n", c=2)[:, :, 0:60]).then_inc(c1_T, 1)

            def kT_copy(b, n):
                act.wait_ge(qt_mm, n)
                nc.scalar.copy(kT[:, b // 2, 2 * (b % 2):2 * (b % 2) + 2, :],
                               PS[:, 6 + b % 2, :].rearrange("p (k q) -> p k q", k=2)).then_inc(qt_act, 1)

            gelu_sigmoid(0)
            h1T_copy(0)
            gelu_sigmoid(1)
            kT_copy(0, 1)
            kT_copy(1, 2)
            for b in range(4):
                act.wait_ge(qt_mm, 3 + b)
                nc.scalar.copy(qT[:, 2 * b:2 * b + 2, :], PS[:, 2 + b, :].rearrange("p (k q) -> p k q", k=2)).then_inc(qt_act, 1)
            kT_copy(2, 7)
            kT_copy(3, 8)
            h1T_copy(1)
            act.wait_ge(kc_mm, 2)
            act.wait_ge(const_ok, 1)
            for q in range(4):
                i = nc.scalar.copy(vcr[32 * q:32 * q + NC_, :, :], PS[32 * q:32 * q + NC_, 1, 256:512].rearrange("p (g e) -> p g e", g=4))
            i.then_inc(vcr_ok, 1)

            def exps(hp):
                act.wait_ge(s_max, 8 * (hp + 1) + (hp + 1))
                if hp >= 2:
                    act.wait_ge(s_fac, hp - 1)
                for i_ in range(2):
                    for t in range(NT):
                        for s in range(2):
                            n = 4 * i_ + 2 * t + s
                            v = Pb[:, hp % 2, i_, 256 * t + 128 * (t + 1) * s:256 * t + 128 * (t + 1) * (s + 1)]
                            nc.scalar.activation(v, v, ACT.Exp, scale=SCALE, bias=nmx[:, hp % 2, n:n + 1],
                                                 accum_out=sme[:, hp % 2, n:n + 1]).then_inc(s_exp, 1)

            exps(0)
            act.wait_ge(sc_d, 2)
            nc.scalar.activation(Pc[:, :, :, 0:NC_], Pc[:, :, :, 0:NC_], ACT.Exp, scale=SCALE).then_inc(sc_e, 1)
            act.wait_ge(sct_mm, 1)
            nc.scalar.copy(PcT[:, 0:2, :], PS[:, 4, :].rearrange("p (k q) -> p k q", k=2)).then_inc(pct_ok, 1)
            for hp in range(8):
                if hp >= 2:
                    act.wait_ge(o_mm, hp - 1)
                for b in (1, 2):
                    act.wait_ge(t_mm, 3 * hp + b + 1)
                    nc.scalar.copy(pT[:, hp % 2, 512 * b:512 * (b + 1)], PS[:, 4 + b, :]).then_inc(pt_act, 1)
                if hp < 7:
                    exps(hp + 1)
                act.wait_ge(o_mm, hp + 1)
                nc.scalar.copy(OT[:, hp, :], PS[:, 7, 0:256]).then_inc(o_ok, 1)
            moe(1)

        @block.vector
        def _(dve):
            v = nc.vector
            own = [0]

            def link(i):
                own[0] += 1
                i.then_inc(c_dve, 1)
                dve.wait_ge(c_dve, own[0])

            def bc(ap, dims):
                return ap.broadcast_to(dims)

            def square_sum(a):
                if a > 0 and H_ACT[a]:
                    dve.wait_ge(h_act, H_ACT[a])
                if a > 0:
                    dve.wait_ge(h_dve, H_DVE[a] - (2 if a == 3 else 0))
                link(v.tensor_tensor_reduce(hn[:, 0, :], h[:, 0, :], h[:, 0, :], 1.0, 0.0, ALU.mult, ALU.add, rstd[:, 0, 0:1]))
                mean_square(0)

            def mean_square(t):
                v.tensor_scalar(rstd[:, 1, t:t + 1], rstd[:, 0, t:t + 1], 1.0 / D, EPS, ALU.mult, ALU.add).then_inc(var_ok, 1)

            def scale_half(a):
                dve.wait_ge(rs_ok, RS_BEFORE[a] + 1)
                v.tensor_scalar(hn[:, 0, :], h[:, 0, :], rstd[:, 1, 0:1], None, ALU.mult).then_inc(hn_dve, 1)

            def xnT_copy(a, row, t):
                dve.wait_ge(tr_ok, 4 * a + 2 * t + 1)
                v.tensor_tensor(xnT[:, 0:4, t * P:(t + 1) * P], PS[:, 4 + 2 * t, :].rearrange("p (k q) -> p k q", k=4),
                                bc(vecT[:, row:row + 4].unsqueeze(2), [P, 4, P]), ALU.mult).then_inc(xt_dve, 1)

            def norm(a, row):
                square_sum(a)
                dve.wait_ge(ssq_ok, a + 1)
                mean_square(1)
                scale_half(a)
                if a == 0:
                    first_columns()
                for t in range(NT):
                    xnT_copy(a, row, t)

            def first_columns():
                dve.wait_ge(vtr, 1)
                v.tensor_copy(vecT[:, :], PS[:, 0, 0:NROWS]).then_inc(vec_ok, 1)
                dve.wait_ge(vtr, 2)
                v.tensor_copy(g8[:, :, :], PS[:, 1, 0:16].rearrange("p (c n) -> p c n", c=2)).then_inc(vec_ok, 1)
                dve.wait_ge(vtr, 3)
                v.tensor_copy(wdw, PS[:, 2, 0:8 * TAPS].rearrange("p (c w) -> p c w", c=8)).then_inc(vec_ok, 1)
                dve.wait_ge(vec_ok, 3)
                link(v.memset(cv0[:, :, 0:TAPS - 1], 0.0))

            dve.wait_ge(x_in, 16 * NT)
            norm(0, ROW_MIX)

            def glu(c):
                dve.wait_ge(sig_ok, c + 1)
                v.scalar_tensor_tensor(out=cv0[:, c, TAPS - 1:], in0=PS[:, c % 4, 0:T],
                                       scalar=vecT[:, ROW_BPW1 + c:ROW_BPW1 + c + 1], in1=sgm[c % 2],
                                       op0=ALU.add, op1=ALU.mult).then_inc(glu_ok, 1)

            glu(0)
            for c in range(KD):
                dve.wait_ge(glu_ok, c + 1)
                if c == 0:
                    dve.wait_ge(tr_ok, 4)
                nv = TAPS - PE_TAPS - POOL_TAPS
                for w in range(nv):
                    o = cT[:, c, :] if w % 2 == 0 else accb[0]
                    u = cv0[:, c, w:w + T]
                    if w == 0:
                        i = v.tensor_scalar(o, u, wdw[:, c, w:w + 1], vecT[:, ROW_BDW + c:ROW_BDW + c + 1], ALU.mult, ALU.add)
                    elif w == 1:
                        i = v.tensor_scalar(o, u, wdw[:, c, w:w + 1], None, ALU.mult)
                    else:
                        i = v.scalar_tensor_tensor(out=o, in0=u, scalar=wdw[:, c, w:w + 1], in1=o, op0=ALU.mult, op1=ALU.add)
                    i.then_inc(c_dve, 1)
                    own[0] += 1
                    if w >= 1:
                        dve.wait_ge(c_dve, own[0] - 1)
                if c + 1 < KD:
                    glu(c + 1)
                dve.wait_ge(c_dve, own[0])
                dve.wait_ge(tap_mm, c + 1)
                dve.wait_ge(ptap_ok, c + 1)
                link(v.tensor_tensor(accb[1], PS[:, 4 + c % 2, 0:T], pac[c % 2], ALU.add))
                link(v.tensor_tensor(cT[:, c, :], cT[:, c, :], accb[0], ALU.add))
                v.tensor_tensor(cT[:, c, :], cT[:, c, :], accb[1], ALU.add).then_inc(conv_ok, 1)
                dve.wait_ge(conv_ok, c + 1)
            dve.wait_ge(lnmm, 1)
            link(v.tensor_scalar(mu, PS[:, 6, 0:T], 1.0 / D, None, ALU.mult))
            for c in range(KD):
                v.tensor_tensor(cT[:, c, :], cT[:, c, :], mu, ALU.subtract).then_inc(ln_c, 1)
            dve.wait_ge(lnmm, 2)
            v.tensor_scalar(var, PS[:, 7, 0:T], 1.0 / D, EPS, ALU.mult, ALU.add).then_inc(root_in, 1)
            dve.wait_ge(root_ok, 1)
            link(v.reciprocal(var, var))
            dve.wait_ge(ln_c, KD)
            for c in range(KD):
                v.tensor_tensor(cT[:, c, :], cT[:, c, :], var, ALU.mult).then_inc(ln_r, 1)
            for n in range(2):
                for t in range(NT):
                    dve.wait_ge(out_mm, 2 * n + t + 1)
                    hs = h[:, t, 512 * n:512 * (n + 1)]
                    v.tensor_tensor(hs, PS[:, 2 * n + t, :], hs, ALU.add).then_inc(h_dve, 1)

            def first_of(vals, mx_, onehot, idx, n, d):
                link(v.tensor_reduce(mx_, vals, AX.X, ALU.max))
                link(v.tensor_tensor(d, vals, bc(mx_.unsqueeze(2), [P, 2, n]), ALU.subtract))
                link(v.tensor_scalar(onehot, d, 0.0, -BIGI, ALU.is_equal, ALU.mult))
                link(v.tensor_tensor(onehot, onehot, bc(iot[:, 0:n].unsqueeze(1), [P, 2, n]), ALU.add))
                link(v.tensor_reduce(idx, onehot, AX.X, ALU.min))
                link(v.tensor_tensor(onehot, onehot, bc(idx.unsqueeze(2), [P, 2, n]), ALU.is_equal))

            def xgT_copy(dst, L):
                gain = g8[:, :, 4 * L:4 * L + 4].rearrange("p c j -> p j c").unsqueeze(3)
                return v.tensor_tensor(dst.rearrange("p (j c) s -> p j c s", c=2),
                                       PS[:, BGX, Q4:Q4 + 256].rearrange("p (c j s) -> p j c s", c=2, j=4),
                                       bc(gain, [P, 4, 2, SLOTS]), ALU.mult)

            def hmul():
                return v.tensor_tensor(hh[64:128, :], PS[64:128, BGU, 0:256], gs[64:128, :], ALU.mult)

            def hT_copy():
                return v.tensor_copy(hT, PS[:, BHT, 0:128].rearrange("p (c s) -> p c s", c=2))

            def moe(L):
                a = 3 * L + 1
                norm(a, ROW_FFN + 8 * L)
                dve.wait_ge(rt_mm, L + 1)
                link(v.tensor_copy(R, PS[:, BGU, 0:128].rearrange("p (t e) -> p t e", t=2)[:, :, 0:36]))
                lg, le = R[:, :, 0:NG], R[:, :, NG:]
                link(v.tensor_reduce(sm[:, 0, :], lg, AX.X, ALU.max))
                v.tensor_tensor(dg, lg, bc(sm[:, 0, :].unsqueeze(2), [P, 2, NG]), ALU.subtract).then_inc(rt_d, 1)
                dve.wait_ge(rt_d, 2 * L + 1)
                link(v.tensor_scalar(og, dg, 0.0, -BIGI, ALU.is_equal, ALU.mult))
                link(v.tensor_tensor(og, og, bc(iot[:, 0:NG].unsqueeze(1), [P, 2, NG]), ALU.add))
                link(v.tensor_reduce(sm[:, 1, :], og, AX.X, ALU.min))
                link(v.tensor_tensor(og, og, bc(sm[:, 1, :].unsqueeze(2), [P, 2, NG]), ALU.is_equal))
                link(v.tensor_scalar(cg, og, -1.0, -NEG, ALU.add, ALU.mult))
                for t in range(NT):
                    grp = [P, NG, NEG_E]
                    link(v.tensor_tensor(lm[:, t, :].rearrange("p (g e) -> p g e", g=NG), le[:, t, :].rearrange("p (g e) -> p g e", g=NG),
                                         bc(og[:, t, :].unsqueeze(2), grp), ALU.mult))
                    link(v.tensor_tensor(lm[:, t, :].rearrange("p (g e) -> p g e", g=NG), lm[:, t, :].rearrange("p (g e) -> p g e", g=NG),
                                         bc(cg[:, t, :].unsqueeze(2), grp), ALU.add))
                first_of(lm, sm[:, 2, :], O1, sm[:, 5, :], NE, dd)
                link(v.scalar_tensor_tensor(out=lm, in0=O1, scalar=NEG, in1=lm, op0=ALU.mult, op1=ALU.add))
                first_of(lm, sm[:, 6, :], O2, sm[:, 7, :], NE, dd)
                v.tensor_tensor(Cc, O1, O2, ALU.add).then_inc(rt_c, 1)
                v.tensor_tensor(sm[:, 3, :], sm[:, 6, :], sm[:, 2, :], ALU.subtract).then_inc(rt_d, 1)
                dve.wait_ge(rt_e, 2 * L + 2)
                link(v.tensor_reduce(sm[:, 8, :], eg, AX.X, ALU.add))
                link(v.tensor_scalar(sm[:, 9, :], sm[:, 4, :], 1.0, None, ALU.add))
                link(v.tensor_tensor(sm[:, 8, :], sm[:, 8, :], sm[:, 9, :], ALU.mult))
                link(v.reciprocal(W4[:, :, 0], sm[:, 8, :]))
                link(v.tensor_tensor(W4[:, :, 1], W4[:, :, 0], sm[:, 4, :], ALU.mult))
                dve.wait_ge(rt_pf, L + 1)
                dve.wait_ge(rt_c, L + 1)
                pf = PS[:, 6, 0:64].rearrange("p (t e) -> p t e", t=2)
                for s, (O, ix) in enumerate(((O1, 5), (O2, 7))):
                    link(v.tensor_tensor(dd, pf, O, ALU.mult))
                    link(v.tensor_reduce(sm[:, 10, :], dd, AX.X, ALU.add))
                    link(v.tensor_scalar(sm[:, 11, :], sm[:, ix, :], BIGI, 256.0, ALU.add, ALU.mult))
                    link(v.tensor_tensor(S4[:, :, s], sm[:, 11, :], sm[:, 10, :], ALU.add))
                v.tensor_copy(cnt, PS[:, 6, 64:96]).then_inc(rt_s, 1)
                dve.wait_ge(rt_s, L + 1)
                link(v.tensor_scalar(ext, cnt, float(SLOTS), None, ALU.is_gt))
                for m in range(2, T // SLOTS):
                    link(v.scalar_tensor_tensor(out=ext, in0=cnt, scalar=float(SLOTS * m), in1=ext, op0=ALU.is_gt, op1=ALU.add))
                dve.wait_ge(rt_row, L + 1)
                v.tensor_copy(srow, PS[:, 4, :].rearrange("p (a q) -> p a q", a=2)).then_inc(row_dve, 1)
                g0 = (NE + 1) * L
                dve.wait_ge(xt_mm, g0 + 1)
                xgT_copy(xgT, L).then_inc(xgT_ok, 1)
                link(v.tensor_copy(scn[:, 0, :], ext))
                b = 0
                for sh in (1, 2, 4, 8, 16):
                    link(v.tensor_copy(scn[:, 1 - b, 0:sh], scn[:, b, 0:sh]))
                    link(v.tensor_tensor(scn[:, 1 - b, sh:], scn[:, b, sh:], scn[:, b, 0:NE - sh], ALU.add))
                    b = 1 - b
                if L == 0:
                    link(v.tensor_copy(xtot[:, :], scn[:, b, NE - 1:NE]))
                else:
                    link(v.tensor_scalar(scn[:, b, :], scn[:, b, :], xtot[:, 0:1], None, ALU.add))
                link(v.tensor_tensor(scn[:, b, :], scn[:, b, :], ext, ALU.subtract))
                link(v.tensor_copy(tab[:, 0, :], ext))
                v.tensor_copy(tab[:, 1, :], scn[:, b, :]).then_inc(tab_ok, 1)
                dve.wait_ge(tab_ok, L + 1)
                with dve.Fori(0, NE // 2) as it:
                    for s in range(2):
                        n = it * 2 + (s + NE * L + 1)
                        gi = it * 2 + (s + g0 + 2)
                        dve.wait_ge(sil_ok, n)
                        hmul().then_inc(h_ok, 1)
                        dve.wait_ge(ht_mm, n)
                        hT_copy().then_inc(hT_ok, 1)
                        dve.wait_ge(xt_mm, gi)
                        xgT_copy(xgT, L).then_inc(xgT_ok, 1)
                        e = it * 2 + s
                        more = dve.value_load(tab[0:1, 0, bass.ds(e, 1)], min_val=0, max_val=7)
                        before = dve.value_load(tab[0:1, 1, bass.ds(e, 1)], min_val=0, max_val=64)
                        with dve.If(more > 0):
                            with dve.Fori(0, more) as r:
                                c = before + r + 1
                                dve.wait_ge(X["x_xt"], c)
                                xgT_copy(xxgT, L).then_inc(X["x_xgT"], 1)
                                dve.wait_ge(X["x_sil"], c)
                                hmul().then_inc(X["x_h"], 1)
                                dve.wait_ge(X["x_ht"], c)
                                hT_copy().then_inc(X["x_hT"], 1)
                dve.wait_ge(slot_free, NE * (L + 1))
                for j in (0, 2):
                    v.tensor_copy(h[:, :, Q4 * j:Q4 * (j + 1)],
                                  PS[:, ACC + j, :].rearrange("p (t q) -> p t q", t=2)).then_inc(h_dve, 1)
                norm(a + 1, ROW_PLE + 8 * L)
                if L == 0:
                    trig_args()
                    all_tables()
                for t in range(NT):
                    for n in range(2):
                        b = 2 * t + n
                        dve.wait_ge(pl_sig, 4 * L + b + 1)
                        if b == 0:
                            dve.wait_ge(pp_ok, 4 * (L + 1))
                        gsl = hn[:, t, 512 * n:512 * (n + 1)]
                        hs = h[:, t, 512 * n:512 * (n + 1)]
                        v.tensor_tensor(gsl, gsl, pp[:, t, 512 * n:512 * (n + 1)], ALU.mult).then_inc(pl_mul, 1)
                        dve.wait_ge(pl_mul, 4 * L + b + 1)
                        v.tensor_tensor(hs, hs, gsl, ALU.add).then_inc(h_dve, 1)
                        if (t, n) == (0, 1) and L == 0:
                            square_sum(3)
                            scale_half(3)
                        if (t, n) == (1, 0) and L == 0:
                            xnT_copy(3, ROW_MIX + 8, 0)

            def reduce_angles(ang, k):
                link(v.tensor_scalar(k, k, MAGIC, None, ALU.add))
                link(v.tensor_scalar(k, k, MAGIC, None, ALU.subtract))
                for part in TWO_PI:
                    link(v.scalar_tensor_tensor(out=ang, in0=k, scalar=-part, in1=ang, op0=ALU.mult, op1=ALU.add))

            def trig_args():
                dve.wait_ge(misc_in, 16 * N_MISC)
                dve.wait_ge(att_in, 16 * N_ATT)
                link(v.tensor_copy(posf[:, 0:2], posi[:, 0:2]))
                link(v.tensor_copy(posf[0:60, 2:3], posi[0:60, 2:3]))
                tc2, kc2 = tcc[0:60, 0:64].rearrange("p (f e) -> p f e", f=2), tcc[0:60, 64:128].rearrange("p (f e) -> p f e", f=2)
                for rows, dst, k, pos in ((P, trig[:, 0], trk[:, 0], posf[:, 0:1]), (P, trig[:, 1], trk[:, 1], posf[:, 1:2]),
                                          (60, tc2, kc2, posf[0:60, 2:3])):
                    v.tensor_scalar(dst, bc(invb[0:rows, :].unsqueeze(1), [rows, 2, DH // 2]), pos, None, ALU.mult).then_inc(c_dve, 1)
                    own[0] += 1
                dve.wait_ge(c_dve, own[0])
                for dst, k in ((trig, trk), (tcc[0:60, 0:64], tcc[0:60, 64:128])):
                    four = len(dst.shape) == 4
                    cos_d, cos_k = (dst[:, :, 0, :], k[:, :, 0, :]) if four else (dst[:, 0:32], k[:, 0:32])
                    link(v.tensor_scalar(k, dst, float(1 / (2 * np.pi)), None, ALU.mult))
                    link(v.tensor_scalar(cos_k, cos_k, 0.25, None, ALU.add))
                    reduce_angles(dst, k)
                    link(v.tensor_scalar(cos_d, cos_d, float(np.pi / 2), None, ALU.add))
                    v.tensor_scalar(dst, dst, PI_LO, -PI_LO, ALU.min, ALU.max).then_inc(trig_ok, 1)

            def gain_tables(dst, tr, gains, n):
                def g(lo):
                    x = gains[:, lo:lo + 32]
                    return bc(x.unsqueeze(1), [P, n, 32]) if n else x
                for f, lo, gl in ((0, 0, 0), (0, 32, 32), (1, 32, 0)):
                    v.tensor_tensor(dst(f, lo), tr(f), g(gl), ALU.mult).then_inc(c_dve, 1)
                    own[0] += 1
                v.scalar_tensor_tensor(out=dst(1, 0), in0=tr(1), scalar=-1.0, in1=g(32), op0=ALU.mult, op1=ALU.mult).then_inc(c_dve, 1)
                own[0] += 1

            def all_tables():
                dve.wait_ge(sin_ok, 2)
                for m in range(3):
                    gain_tables(lambda f, lo: tcos[:, :, f, m, lo:lo + 32], lambda f: trig[:, :, f, :], gn[:, m, :], 2)
                gain_tables(lambda f, lo: tcc[0:60, 64 + 64 * f + lo:64 + 64 * f + lo + 32],
                            lambda f: tcc[0:60, 32 * f:32 * f + 32], gn[0:60, 3, :], 0)
                dve.wait_ge(c_dve, own[0])

            moe(0)

            dve.wait_ge(ssq_ok, 4)
            mean_square(1)
            ktab = tcc[0:60, 64:192].rearrange("p (f e) -> p f e", f=2)
            for t in range(NT):
                for s in range(2):
                    dve.wait_ge(kv_mm, 2 * t + s + 1)
                    v.tensor_copy(raw[:, t, 16 + 4 * s:20 + 4 * s, :],
                                  PS[:, 2 + 2 * s + t, 0:256].rearrange("p (m e) -> p m e", m=4)).then_inc(kv_dve, 1)
                    if (t, s) == (0, 0):
                        xnT_copy(3, ROW_MIX + 8, 1)

            def stream_blocks():
                dve.wait_ge(xpt_mm, 3)
                link(v.tensor_copy(peT, PS[:, 7, 0:32].rearrange("p (s j) -> p s j", s=2)))
                for s in range(2):
                    v.tensor_copy(xpT[:, s, :, :], PS[:, s, :].rearrange("p (g m) -> p g m", g=4)).then_inc(xpt_ok, 1)
                    dve.wait_ge(xpt_ok, s + 1)
                    for b in range(2):
                        x3 = xpT[:, s, :, 8 * b:8 * b + 8 * NC_].rearrange("p g (n j) -> p j g n", j=8)
                        i = v.tensor_tensor(Bc[:, s, 8 * b:8 * b + 8, :, :], x3,
                                            bc(peT[:, s, 8 * b:8 * b + 8].unsqueeze(2).unsqueeze(3), [P, 8, NKV, NC_]), ALU.add)
                    i.then_inc(B_ok, 1)

            for i_, (t, lo, n) in enumerate(((0, 16, 8), (1, 16, 8), (0, 0, 16), (1, 0, 16))):
                if i_ == 2:
                    stream_blocks()
                dve.wait_ge(sq_ok, i_ + 1)
                v.tensor_reduce(ssn[:, 0:n], sq[:, 0:64 * n].rearrange("p (m e) -> p m e", m=n), AX.X, ALU.add).then_inc(sq_used, 1)
                dve.wait_ge(sq_used, i_ + 1)
                v.tensor_scalar(ssn[:, 24:24 + n], ssn[:, 0:n], 1.0 / DH, EPS, ALU.mult, ALU.add).then_inc(root_in, 1)
                dve.wait_ge(root_ok, i_ + 2)
                link(v.reciprocal(ssn[:, 24:24 + n], ssn[:, 24:24 + n]))
                x_ = raw[:, t, lo:lo + n, :]
                link(v.tensor_tensor(x_, x_, bc(ssn[:, 24:24 + n].unsqueeze(2), [P, n, 64]), ALU.mult))
                for m, lo2, nn in (((0, 0, 16),) if lo == 0 else ((1, 16, 4), (2, 20, 4))):
                    x_ = raw[:, t, lo2:lo2 + nn, :]
                    tA = bc(tcos[:, t, 0, m, :].unsqueeze(1), [P, nn, 64])
                    dst = rotq[:, t, :, :] if m == 0 else rotk[:, t, 4 * (m - 1):4 * m, 0, :]
                    tmp = rot_tmp[:, 0:64 * nn].rearrange("p (m e) -> p m e", m=nn)
                    v.tensor_tensor(dst, x_, tA, ALU.mult).then_inc(c_dve, 1)
                    for f in range(2):
                        i = v.tensor_tensor(tmp[:, :, 32 * f:32 * f + 32], x_[:, :, 32 * (1 - f):32 * (1 - f) + 32],
                                            bc(tcos[:, t, 1, m, 32 * f:32 * f + 32].unsqueeze(1), [P, nn, 32]), ALU.mult)
                        i.then_inc(c_dve, 1)
                    own[0] += 3
                    dve.wait_ge(c_dve, own[0])
                    if m > 0:
                        link(v.tensor_tensor(rotk[:, t, 4 * (m - 1):4 * m, 1, :], dst, tmp, ALU.add))
                    link(v.tensor_tensor(dst, dst, tmp, ALU.add))
                if lo == 0:
                    v.memset(mcol[:, 3 + t:4 + t], 0.0).then_inc(rot_ok, 1)
                elif t == 1:
                    v.memset(mcol[:, 5:6], 0.0).then_inc(rot_ok, 1)

            for s in range(2):
                if s == 1:
                    dve.wait_ge(c1_g, 1)
                dve.wait_ge(c1_mm, s + 1)
                xx, t1, sg = sq[0:60, 0:256], sq[0:60, 256:512], sq[0:60, 512:768]
                link(v.tensor_copy(xx, PS[0:60, s, 0:256]))
                link(v.tensor_tensor(t1, xx, xx, ALU.mult))
                link(v.tensor_scalar(t1, t1, 0.044715, 1.0, ALU.mult, ALU.add))
                v.tensor_tensor(t1, t1, xx, ALU.mult).then_inc(c1_x, 1)
                dve.wait_ge(c1_s, s + 1)
                v.tensor_tensor(h1v[s][0:60, :], xx, sg, ALU.mult).then_inc(c1_g, 1)
            dve.wait_ge(kc_mm, 1)
            link(v.tensor_copy(kcx[0:60, 0, :], PS[0:60, 0, 0:64]))
            v.tensor_copy(kcx[0:60, 1, :], kcx[0:60, 0, :]).then_inc(kc_x, 1)
            dve.wait_ge(kc_x, 1)
            link(v.tensor_tensor(kcx[0:60, 1, :], kcx[0:60, 0, :], kcx[0:60, 0, :], ALU.mult))
            link(v.tensor_reduce(mcol[0:60, 0:1], kcx[0:60, 1, :], AX.X, ALU.add))
            v.tensor_scalar(mcol[0:60, 1:2], mcol[0:60, 0:1], 1.0 / DH, EPS, ALU.mult, ALU.add).then_inc(var_ok, 1)
            dve.wait_ge(rs_ok, 9)
            link(v.tensor_scalar(kcx[0:60, 0, :], kcx[0:60, 0, :], mcol[0:60, 1:2], None, ALU.mult))
            link(v.tensor_tensor(kcx[0:60, 2, :], kcx[0:60, 0, :], ktab[:, 0, :], ALU.mult))
            for f in range(2):
                link(v.tensor_tensor(kcx[0:60, 1, 32 * f:32 * f + 32], kcx[0:60, 0, 32 * (1 - f):32 * (1 - f) + 32],
                                     ktab[:, 1, 32 * f:32 * f + 32], ALU.mult))
            link(v.tensor_tensor(kcx[0:60, 3, :], kcx[0:60, 2, :], kcx[0:60, 1, :], ALU.add))
            v.tensor_tensor(kcx[0:60, 2, :], kcx[0:60, 2, :], kcx[0:60, 1, :], ALU.add).then_inc(kc_x, 1)
            dve.wait_ge(kc_x, 2)
            link(v.memset(kcB, 0.0))
            dve.wait_ge(kct_mm, 1)
            for u in range(2):
                r = slice(64 * u, 64 * u + 64)
                v.tensor_copy(kcB[r, :, u, 0:NC_], PS[r, 0, 384:444].rearrange("p (g n) -> p g n", g=NKV)).then_inc(kcT_ok, 1)
            def maxes(hp):
                dve.wait_ge(s_mm, hp + 1)
                if hp >= 2:
                    dve.wait_ge(t_mm, 3 * (hp - 1))
                for i_ in range(2):
                    for t in range(NT):
                        for s in range(2):
                            n = 4 * i_ + 2 * t + s
                            w = 128 * (t + 1)
                            mk = cmask[:, 1, :] if t == 0 else cmask[:, :, :].rearrange("p a b -> p (a b)")
                            v.tensor_tensor_reduce(Pb[:, hp % 2, i_, 256 * t + w * s:256 * t + w * (s + 1)],
                                                   PS[:, 2 * t + i_, w * s:w * (s + 1)], mk, 1.0, NEG, ALU.add, ALU.max,
                                                   mx[:, hp % 2, n:n + 1]).then_inc(s_max, 1)
                dve.wait_ge(s_max, 9 * hp + 8)
                v.tensor_scalar(nmx[:, hp % 2, :], mx[:, hp % 2, :], -SCALE, None, ALU.mult).then_inc(s_max, 1)

            def factors(hp):
                dve.wait_ge(s_exp, 8 * (hp + 1))
                if hp == 0:
                    dve.wait_ge(gate_ok, 1)
                link(v.reciprocal(sme[:, hp % 2, :], sme[:, hp % 2, :]))
                for i_ in range(2):
                    hd = 2 * hp + i_
                    i = v.tensor_tensor(fac[:, hp % 2, 4 * i_:4 * i_ + 4].rearrange("p (t s) -> p t s", t=2),
                                        sme[:, hp % 2, 4 * i_:4 * i_ + 4].rearrange("p (t s) -> p t s", t=2),
                                        gt[:, :, 3 * hd + 1:3 * hd + 3], ALU.mult)
                i.then_inc(s_fac, 1)
                dve.wait_ge(s_fac, hp + 1)
                for i_ in range(2):
                    for t in range(2 - i_):
                        for s in range(2):
                            n = 4 * i_ + 2 * t + s
                            x_ = Pb[:, hp % 2, i_, 256 * t + 128 * (t + 1) * s:256 * t + 128 * (t + 1) * (s + 1)]
                            i = v.tensor_scalar(x_, x_, fac[:, hp % 2, n:n + 1], None, ALU.mult)
                i.then_inc(s_sclv, 1)

            maxes(0)
            link(v.memset(Pc[:, :, :, NC_:], 0.0))
            dve.wait_ge(mask_ok, 1)
            dve.wait_ge(sc_mm, 1)
            i = v.tensor_tensor(Pc[:, :, :, 0:NC_], PS[:, 7, :].rearrange("p (t m n) -> p t m n", t=NT, m=HEADS)[:, :, :, 0:NC_],
                                bc(mka.unsqueeze(2), [P, NT, HEADS, NC_]), ALU.add)
            i.then_inc(sc_d, 1)
            dve.wait_ge(sc_d, 1)
            pc3 = Pc.rearrange("p t n e -> p (t n) e")[:, :, 0:NC_]
            link(v.tensor_reduce(cst[:, 0, :], pc3, AX.X, ALU.max))
            v.tensor_tensor(pc3, pc3, bc(cst[:, 0, :].unsqueeze(2), [P, 32, NC_]), ALU.subtract).then_inc(sc_d, 1)
            factors(0)
            dve.wait_ge(sc_e, 1)
            link(v.tensor_reduce(cst[:, 1, :], pc3, AX.X, ALU.add))
            link(v.reciprocal(cst[:, 2, :], cst[:, 1, :]))
            dve.wait_ge(gate_ok, 1)
            link(v.tensor_tensor(cst[:, 2, :].rearrange("p (t n) -> p t n", t=2), cst[:, 2, :].rearrange("p (t n) -> p t n", t=2),
                                 gt.rearrange("p t (n b) -> p t n b", b=3)[:, :, :, 0], ALU.mult))
            link(v.tensor_tensor(pc3, pc3, bc(cst[:, 2, :].unsqueeze(2), [P, 32, NC_]), ALU.mult))
            v.tensor_tensor(Pc[:, :, :, 0:NC_], Pc[:, :, :, 0:NC_], bc(mk1.unsqueeze(2), [P, 2, 16, NC_]), ALU.mult).then_inc(sc_p, 1)
            dve.wait_ge(sct_mm, 1)
            v.tensor_copy(PcT[:, 2:4, :], PS[:, 5, :].rearrange("p (k q) -> p k q", k=2)).then_inc(pct_ok, 1)
            for hp in range(8):
                if hp < 7:
                    maxes(hp + 1)
                dve.wait_ge(t_mm, 3 * hp + 1)
                if hp >= 2:
                    dve.wait_ge(o_mm, hp - 1)
                v.tensor_copy(pT[:, hp % 2, 0:512], PS[:, 4, :]).then_inc(pt_dve, 1)
                if hp < 7:
                    factors(hp + 1)
            for n in range(2):
                for t in range(NT):
                    dve.wait_ge(out_mm, 4 + 2 * n + t + 1)
                    hs = h[:, t, 512 * n:512 * (n + 1)]
                    v.tensor_tensor(hs, PS[:, 2 * n + t, :], hs, ALU.add).then_inc(h_dve, 1)
            moe(1)


_INS = ['x', 'p', 'positions', 'g_mix', 'g_ffn', 'g_ple', 'conv_w_pw1', 'conv_b_pw1', 'conv_w_dw', 'conv_b_dw',
        'conv_ln_g', 'conv_ln_b', 'conv_w_pw2', 'conv_b_pw2', 'nsa_w_in', 'nsa_q_norm', 'nsa_k_norm',
        'nsa_cmp_pe', 'nsa_cmp_w1', 'nsa_cmp_w2', 'nsa_w_out', 'moe_w_rg', 'moe_b_rg', 'moe_w_re', 'moe_b_re',
        'moe_w_gate', 'moe_w_up', 'moe_w_down', 'ple_w_proj', 'ple_w_gate']


def kernel(**inputs):
    import numpy as _np
    import concourse.bacc as _bacc
    from concourse import mybir as _mybir
    from concourse.bass_utils import run_bass_kernel_spmd as _run

    nc = _bacc.Bacc("TRN2", target_bir_lowering=False, num_devices=1)
    arrays, args = {}, []
    given = {name: _np.ascontiguousarray(inputs[name]) for name in _INS}
    half = DH // 2
    given["inv_freq"] = (1.0 / (ROPE_THETA ** (_np.arange(half, dtype=_np.float32) / half))).astype(_np.float32)[None, :]
    for name, a in given.items():
        arrays[f"in_{name}"] = a
        args.append(nc.dram_tensor(f"in_{name}", a.shape, _mybir.dt.from_np(a.dtype), kind="ExternalInput").ap())
    args.append(nc.dram_tensor("out_h", (1, T, D), F32, kind="ExternalOutput").ap())
    build(nc, *args)
    return _run(nc, [arrays], core_ids=[0]).results[0]["out_h"]
```
